# Optimizing a Trainium2 kernel written in Bass

```python
import jax, jax.numpy as jnp
from jax import lax
import numpy as np
import math

D_MODEL = 1024
BATCH = 1
SEQ = 256
DEPTH = 2

GRID_W = 64
CTX_LEN = 256
N_MIXERS = 2
N_ATT_LAYERS = (DEPTH + 1) // 2
N_MLSTM_LAYERS = DEPTH // 2
ATT_HEADS = 8
ATT_KV_HEADS = 2
ATT_GROUP = ATT_HEADS // ATT_KV_HEADS
ATT_HEAD_DIM = D_MODEL // ATT_HEADS
ROPE_PAIRS_PER_AXIS = ATT_HEAD_DIM // 4
ROPE_THETA = 10000.0
Q_BLOCK = 128
MLSTM_HEADS = 4
MLSTM_V_DIM = D_MODEL // MLSTM_HEADS
MLSTM_QK_DIM = MLSTM_V_DIM // 2
MLSTM_CONV_W = 3
MLSTM_CHUNK = 64
D_FF = 2816
N_MOD = 9
DEEPNORM_ALPHA = (2.0 * DEPTH) ** 0.25
DEEPNORM_BETA = (8.0 * DEPTH) ** -0.25
LN_EPS = 1e-5
RMS_EPS = 1e-6


def layer_norm(x, g, b):
    xf = x.astype(jnp.float32)
    mu = jnp.mean(xf, axis=-1, keepdims=True)
    var = jnp.mean(jnp.square(xf - mu), axis=-1, keepdims=True)
    return ((xf - mu) * lax.rsqrt(var + LN_EPS) * g + b).astype(x.dtype)

def rms_norm(x, g):
    xf = x.astype(jnp.float32)
    return (xf * lax.rsqrt(jnp.mean(jnp.square(xf), axis=-1, keepdims=True) + RMS_EPS) * g).astype(x.dtype)

def modulate(h, shift, scale):
    return h * (1.0 + scale) + shift

def post_norm(h, delta, g, b):
    return layer_norm(DEEPNORM_ALPHA * h + delta, g, b)

def half_ffn(h, shift, scale, gate, w_in, w_out, g, b):
    xm = modulate(h, shift, scale)
    a, u = jnp.split(xm @ w_in, 2, axis=-1)
    y = (jax.nn.silu(a) * u) @ w_out
    return post_norm(h, 0.5 * gate * y, g, b)

def axial_rope_tables(n_tokens):
    rows = n_tokens // GRID_W
    row = jnp.repeat(jnp.arange(rows, dtype=jnp.int32), GRID_W).astype(jnp.float32)
    col = jnp.tile(jnp.arange(GRID_W, dtype=jnp.int32), rows).astype(jnp.float32)
    inv = ROPE_THETA ** (-jnp.arange(ROPE_PAIRS_PER_AXIS, dtype=jnp.float32) / ROPE_PAIRS_PER_AXIS)
    ang = jnp.stack([row[:, None] * inv, col[:, None] * inv], axis=1)
    return jnp.cos(ang), jnp.sin(ang)

def apply_rope(x, cos, sin):
    B, L, H, Dh = x.shape
    xr = x.reshape(B, L, H, 2, 2, ROPE_PAIRS_PER_AXIS)
    x1, x2 = xr[..., 0, :], xr[..., 1, :]
    c = cos[None, :, None]
    s = sin[None, :, None]
    out = jnp.stack([x1 * c - x2 * s, x2 * c + x1 * s], axis=-2)
    return out.reshape(B, L, H, Dh).astype(x.dtype)

def gqa_softmax(q, k, v):
    s = jnp.einsum('bqhgd,bkhd->bhgqk', q, k).astype(jnp.float32) * (ATT_HEAD_DIM ** -0.5)
    p = jax.nn.softmax(s, axis=-1).astype(v.dtype)
    return jnp.einsum('bhgqk,bkhd->bqhgd', p, v)

def attention_mixer(xl, xc, cos, sin, w_in, q_gain, k_gain, w_out, need_ctx):
    def proj(xs):
        B, L, _ = xs.shape
        p = xs @ w_in
        q, k, v = jnp.split(p, [ATT_HEADS * ATT_HEAD_DIM, (ATT_HEADS + ATT_KV_HEADS) * ATT_HEAD_DIM], axis=-1)
        q = rms_norm(q.reshape(B, L, ATT_HEADS, ATT_HEAD_DIM), q_gain)
        k = rms_norm(k.reshape(B, L, ATT_KV_HEADS, ATT_HEAD_DIM), k_gain)
        v = v.reshape(B, L, ATT_KV_HEADS, ATT_HEAD_DIM)
        return q, k, v

    ql, kl, vl = proj(xl)
    qc, kc, vc = proj(xc)
    ql = apply_rope(ql, cos, sin)
    kl = apply_rope(kl, cos, sin)
    B, L = xl.shape[0], xl.shape[1]
    k_all = jnp.concatenate([kl, kc], axis=1)
    v_all = jnp.concatenate([vl, vc], axis=1)
    nb = L // Q_BLOCK
    qb = jnp.moveaxis(ql.reshape(B, nb, Q_BLOCK, ATT_KV_HEADS, ATT_GROUP, ATT_HEAD_DIM), 1, 0)
    ob = lax.map(lambda qblk: gqa_softmax(qblk, k_all, v_all), qb)
    o_lat = jnp.moveaxis(ob, 0, 1).reshape(B, L, D_MODEL) @ w_out
    o_ctx = None
    if need_ctx:
        Lc = xc.shape[1]
        oc = gqa_softmax(qc.reshape(B, Lc, ATT_KV_HEADS, ATT_GROUP, ATT_HEAD_DIM), kc, vc)
        o_ctx = oc.reshape(B, Lc, D_MODEL) @ w_out
    return o_lat, o_ctx

def centred_conv(a, w, b):
    L = a.shape[1]
    pad = MLSTM_CONV_W // 2
    ap = jnp.pad(a, ((0, 0), (pad, pad), (0, 0)))
    out = ap[:, 0:L] * w[0]
    for j in range(1, MLSTM_CONV_W):
        out = out + ap[:, j:j + L] * w[j]
    return out + b

def mlstm_scan(q, k, v, log_i, log_f, state):
    B, H, L, dk = q.shape
    dv = v.shape[-1]
    Lc = MLSTM_CHUNK
    nc = L // Lc

    def chunks(a):
        return jnp.moveaxis(a.reshape((B, H, nc, Lc) + a.shape[3:]), 2, 0)

    tri = jnp.tril(jnp.ones((Lc, Lc), dtype=bool))

    def step(carry, inp):
        C, n, m = carry
        qc, kc, vc, ic, fc = inp
        bcum = jnp.cumsum(fc, axis=-1)
        d = jnp.where(tri, bcum[..., :, None] - bcum[..., None, :] + ic[..., None, :], -jnp.inf)
        inter = m[..., None] + bcum
        m_t = jnp.maximum(inter, jnp.max(d, axis=-1))
        w_intra = jnp.exp(d - m_t[..., None])
        w_inter = jnp.exp(inter - m_t)
        s = jnp.einsum('bhtd,bhsd->bhts', qc, kc) * w_intra
        num = jnp.einsum('bhts,bhsv->bhtv', s, vc) + w_inter[..., None] * jnp.einsum('bhvd,bhtd->bhtv', C, qc)
        den = jnp.sum(s, axis=-1) + w_inter * jnp.einsum('bhd,bhtd->bht', n, qc)
        h = num / jnp.maximum(jnp.abs(den), jnp.exp(-m_t))[..., None]
        b_last = bcum[..., -1]
        d_last = b_last[..., None] - bcum + ic
        m_new = jnp.maximum(m + b_last, jnp.max(d_last, axis=-1))
        wk = jnp.exp(d_last - m_new[..., None])
        decay = jnp.exp(m + b_last - m_new)
        C_new = decay[..., None, None] * C + jnp.einsum('bhs,bhsv,bhsd->bhvd', wk, vc, kc)
        n_new = decay[..., None] * n + jnp.einsum('bhs,bhsd->bhd', wk, kc)
        return (C_new, n_new, m_new), h

    final, hs = lax.scan(step, state, (chunks(q), chunks(k), chunks(v), chunks(log_i), chunks(log_f)))
    h = jnp.moveaxis(hs, 0, 2).reshape(B, H, L, dv)
    return h, final

def mlstm_mixer(xl, xc, w_in, gate_b, conv_w, conv_b, norm_g, w_out, need_ctx):
    HQK = MLSTM_HEADS * MLSTM_QK_DIM
    HV = MLSTM_HEADS * MLSTM_V_DIM

    def proj(xs):
        B, L, _ = xs.shape
        p = xs @ w_in
        qk, v, o, g = jnp.split(p, [2 * HQK, 2 * HQK + HV, 2 * HQK + HV + D_MODEL], axis=-1)
        qk = jax.nn.silu(centred_conv(qk, conv_w, conv_b))
        q, k = jnp.split(qk, 2, axis=-1)

        def heads(a, dh):
            return jnp.transpose(a.reshape(B, L, MLSTM_HEADS, dh), (0, 2, 1, 3)).astype(jnp.float32)

        q = heads(q, MLSTM_QK_DIM)
        k = heads(k, MLSTM_QK_DIM) * (MLSTM_QK_DIM ** -0.5)
        v = heads(v, MLSTM_V_DIM)
        g = jnp.transpose((g.astype(jnp.float32) + gate_b).reshape(B, L, 4, MLSTM_HEADS), (2, 0, 3, 1))
        return q, k, v, g, o

    def zero_state(B):
        return (jnp.zeros((B, MLSTM_HEADS, MLSTM_V_DIM, MLSTM_QK_DIM), jnp.float32),
                jnp.zeros((B, MLSTM_HEADS, MLSTM_QK_DIM), jnp.float32),
                jnp.zeros((B, MLSTM_HEADS), jnp.float32))

    def flip(a):
        return jnp.flip(a, axis=2)

    def readout(h, o, dtype):
        B, H, L, dv = h.shape
        mu = jnp.mean(h, axis=-1, keepdims=True)
        var = jnp.mean(jnp.square(h - mu), axis=-1, keepdims=True)
        hn = (h - mu) * lax.rsqrt(var + LN_EPS)
        hn = jnp.transpose(hn, (0, 2, 1, 3)).reshape(B, L, D_MODEL) * norm_g
        return (hn * jax.nn.sigmoid(o.astype(jnp.float32))).astype(dtype) @ w_out

    ql, kl, vl, gl, ol = proj(xl)
    qc, kc, vc, gc, oc = proj(xc)
    B = xl.shape[0]
    hc_f, st_f = mlstm_scan(qc, kc, vc, gc[0], jax.nn.log_sigmoid(gc[1]), zero_state(B))
    hl_f, _ = mlstm_scan(ql, kl, vl, gl[0], jax.nn.log_sigmoid(gl[1]), st_f)
    hc_b, st_b = mlstm_scan(flip(qc), flip(kc), flip(vc), flip(gc[2]), jax.nn.log_sigmoid(flip(gc[3])), zero_state(B))
    hl_b, _ = mlstm_scan(flip(ql), flip(kl), flip(vl), flip(gl[2]), jax.nn.log_sigmoid(flip(gl[3])), st_b)
    o_lat = readout(hl_f + flip(hl_b), ol, xl.dtype)
    o_ctx = readout(hc_f + flip(hc_b), oc, xc.dtype) if need_ctx else None
    return o_lat, o_ctx

def first_inputs(seed: int = 0) -> dict:
    key = jax.random.key(seed)
    ks = jax.random.split(key, 24)
    D = D_MODEL
    HQK = MLSTM_HEADS * MLSTM_QK_DIM
    HV = MLSTM_HEADS * MLSTM_V_DIM
    att_cols = (ATT_HEADS + 2 * ATT_KV_HEADS) * ATT_HEAD_DIM
    ml_cols = 2 * HQK + HV + D + 4 * MLSTM_HEADS

    def nrm(k, shape, scale):
        return jax.random.normal(k, shape, jnp.float32) * scale

    forget_b = jnp.linspace(3.0, 6.0, MLSTM_HEADS, dtype=jnp.float32)
    gnoise = nrm(ks[15], (N_MLSTM_LAYERS, 4, MLSTM_HEADS), 0.1)
    gate_b = gnoise + jnp.stack([jnp.zeros_like(forget_b), forget_b, jnp.zeros_like(forget_b), forget_b], axis=0)[None]
    return {
        "x": nrm(ks[0], (BATCH, SEQ, D), 1.0),
        "c": nrm(ks[1], (BATCH, D), 1.0),
        "ctx": nrm(ks[2], (BATCH, CTX_LEN, D), 1.0),
        "c_ctx": nrm(ks[3], (D,), 1.0),
        "ada_w": nrm(ks[4], (DEPTH, D, N_MOD * D), 0.5 * D ** -0.5),
        "ada_b": nrm(ks[5], (DEPTH, N_MOD * D), 0.02),
        "ln_g": 1.0 + nrm(ks[6], (DEPTH, 3, D), 0.02),
        "ln_b": nrm(ks[7], (DEPTH, 3, D), 0.02),
        "ffn_w_in": nrm(ks[8], (DEPTH, 2, D, 2 * D_FF), D ** -0.5),
        "ffn_w_out": nrm(ks[9], (DEPTH, 2, D_FF, D), DEEPNORM_BETA * D_FF ** -0.5),
        "att_w_in": nrm(ks[10], (N_ATT_LAYERS, D, att_cols), D ** -0.5),
        "att_q_gain": 1.0 + nrm(ks[11], (N_ATT_LAYERS, ATT_HEAD_DIM), 0.02),
        "att_k_gain": 1.0 + nrm(ks[12], (N_ATT_LAYERS, ATT_HEAD_DIM), 0.02),
        "att_w_out": nrm(ks[13], (N_ATT_LAYERS, D, D), DEEPNORM_BETA * D ** -0.5),
        "ml_w_in": nrm(ks[14], (N_MLSTM_LAYERS, D, ml_cols), D ** -0.5),
        "ml_gate_b": gate_b.reshape(N_MLSTM_LAYERS, 4 * MLSTM_HEADS),
        "ml_conv_w": nrm(ks[16], (N_MLSTM_LAYERS, MLSTM_CONV_W, 2 * HQK), MLSTM_CONV_W ** -0.5),
        "ml_conv_b": nrm(ks[17], (N_MLSTM_LAYERS, 2 * HQK), 0.02),
        "ml_norm_g": 1.0 + nrm(ks[18], (N_MLSTM_LAYERS, D), 0.02),
        "ml_w_out": nrm(ks[19], (N_MLSTM_LAYERS, D, D), DEEPNORM_BETA * D ** -0.5),
    }

def first_block(x, c, ctx, c_ctx, ada_w, ada_b, ln_g, ln_b, ffn_w_in, ffn_w_out,
              att_w_in, att_q_gain, att_k_gain, att_w_out,
              ml_w_in, ml_gate_b, ml_conv_w, ml_conv_b, ml_norm_g, ml_w_out):
    n_lat = x.shape[1]
    cos, sin = axial_rope_tables(n_lat)
    h_lat, h_ctx = x, ctx
    for i in range(DEPTH):
        need_ctx = i < DEPTH - 1
        mod_lat = jnp.split((jax.nn.silu(c) @ ada_w[i] + ada_b[i])[:, None, :], N_MOD, axis=-1)
        mod_ctx = jnp.split((jax.nn.silu(c_ctx) @ ada_w[i] + ada_b[i])[None, None, :], N_MOD, axis=-1)
        h_lat = half_ffn(h_lat, mod_lat[0], mod_lat[1], mod_lat[2], ffn_w_in[i, 0], ffn_w_out[i, 0], ln_g[i, 0], ln_b[i, 0])
        h_ctx = half_ffn(h_ctx, mod_ctx[0], mod_ctx[1], mod_ctx[2], ffn_w_in[i, 0], ffn_w_out[i, 0], ln_g[i, 0], ln_b[i, 0])
        xm_lat = modulate(h_lat, mod_lat[3], mod_lat[4])
        xm_ctx = modulate(h_ctx, mod_ctx[3], mod_ctx[4])
        j = i // N_MIXERS
        if i % N_MIXERS == 0:
            o_lat, o_ctx = attention_mixer(xm_lat, xm_ctx, cos, sin, att_w_in[j], att_q_gain[j], att_k_gain[j],
                                           att_w_out[j], need_ctx)
        else:
            o_lat, o_ctx = mlstm_mixer(xm_lat, xm_ctx, ml_w_in[j], ml_gate_b[j], ml_conv_w[j], ml_conv_b[j],
                                       ml_norm_g[j], ml_w_out[j], need_ctx)
        h_lat = post_norm(h_lat, mod_lat[5] * o_lat, ln_g[i, 1], ln_b[i, 1])
        h_lat = half_ffn(h_lat, mod_lat[6], mod_lat[7], mod_lat[8], ffn_w_in[i, 1], ffn_w_out[i, 1], ln_g[i, 2], ln_b[i, 2])
        if need_ctx:
            h_ctx = post_norm(h_ctx, mod_ctx[5] * o_ctx, ln_g[i, 1], ln_b[i, 1])
            h_ctx = half_ffn(h_ctx, mod_ctx[6], mod_ctx[7], mod_ctx[8], ffn_w_in[i, 1], ffn_w_out[i, 1], ln_g[i, 2], ln_b[i, 2])
    return h_lat


DEPTH_2 = 1

N_HEADS = 8
HEAD_DIM = 64
V_DIM = 2 * HEAD_DIM
QK_WIDTH = N_HEADS * 2 * HEAD_DIM
ATTN_WIDTH = N_HEADS * V_DIM
SUBLN_EPS = 1e-5
LRU_WIDTH = D_MODEL
LRU_BLOCKS = 16
LRU_BLOCK_W = LRU_WIDTH // LRU_BLOCKS
CONV_WIDTH = 4
LRU_C = 8.0
N_GROUPS = 4
EXPERTS_PER_GROUP = 8
N_EXPERTS = N_GROUPS * EXPERTS_PER_GROUP
TOP_K_INNER = 2
EXPERT_FF = 512
ROUTER_BIAS_SCALE = 0.01
PLE_DIM = 256
NORM_EPS = 1e-6

IN_SIZES = (QK_WIDTH, QK_WIDTH, ATTN_WIDTH, LRU_WIDTH, LRU_WIDTH, D_MODEL, D_MODEL)
IN_COLS = sum(IN_SIZES)
IN_SPLITS = tuple(int(s) for s in np.cumsum(IN_SIZES)[:-1])


def rmsnorm(x, g, eps=NORM_EPS):
    xf = x.astype(jnp.float32)
    y = xf * lax.rsqrt(jnp.mean(xf * xf, axis=-1, keepdims=True) + eps)
    return (y * g.astype(jnp.float32)).astype(x.dtype)

def diff_attention(q, k, v, lam):
    B, S = q.shape[0], q.shape[1]
    n_blk = S // Q_BLOCK
    scale = HEAD_DIM ** -0.5
    qb = jnp.moveaxis(q.reshape(B, n_blk, Q_BLOCK, N_HEADS, 2, HEAD_DIM), 1, 0)
    kf = k.astype(jnp.float32)
    vf = v.astype(jnp.float32)
    kpos = jnp.arange(S)
    neg = jnp.finfo(jnp.float32).min

    def one_block(args):
        qi, blk = args
        s = jnp.einsum('bqhcd,bkhcd->bhcqk', qi.astype(jnp.float32), kf) * scale
        qpos = blk * Q_BLOCK + jnp.arange(Q_BLOCK)
        causal = kpos[None, :] <= qpos[:, None]
        s = jnp.where(causal, s, neg)
        pr = jax.nn.softmax(s, axis=-1)
        a = pr[:, :, 0] - lam * pr[:, :, 1]
        return jnp.einsum('bhqk,bkhe->bqhe', a, vf)

    o = lax.map(one_block, (qb, jnp.arange(n_blk)))
    return jnp.moveaxis(o, 0, 1).reshape(B, S, N_HEADS, V_DIM).astype(q.dtype)

def causal_depthwise_conv(x, w, b):
    S = x.shape[1]
    xp = jnp.pad(x, ((0, 0), (CONV_WIDTH - 1, 0), (0, 0)))
    y = b
    for j in range(CONV_WIDTH):
        y = y + xp[:, j:j + S] * w[j]
    return y

def rg_lru(x, w_rg, b_rg, w_ig, b_ig, lru_lambda):
    B, S, W = x.shape
    xb = x.reshape(B, S, LRU_BLOCKS, LRU_BLOCK_W)
    r = jax.nn.sigmoid(jnp.einsum('bsnw,nwv->bsnv', xb, w_rg) + b_rg).reshape(B, S, W)
    ig = jax.nn.sigmoid(jnp.einsum('bsnw,nwv->bsnv', xb, w_ig) + b_ig).reshape(B, S, W)
    log_a = -LRU_C * r.astype(jnp.float32) * jax.nn.softplus(-lru_lambda.astype(jnp.float32))
    a = jnp.exp(log_a)
    mult = jnp.sqrt(-jnp.expm1(2.0 * log_a))
    u = mult * (ig * x).astype(jnp.float32)

    def combine(left, right):
        a_l, b_l = left
        a_r, b_r = right
        return a_l * a_r, a_r * b_l + b_r

    _, h = lax.associative_scan(combine, (a, u), axis=1)
    return h.astype(x.dtype)

def hier_moe(h, w_rt_group, b_rt_group, w_rt_expert, b_rt_expert, w_e_gate, w_e_up, w_e_down):
    B, S, D = h.shape
    t = h.reshape(B * S, D)
    grp_logits = (t @ w_rt_group + b_rt_group).astype(jnp.float32)
    grp_prob = jax.nn.softmax(grp_logits, axis=-1)
    g_idx = jnp.argmax(grp_logits, axis=-1)
    g_w = jnp.take_along_axis(grp_prob, g_idx[:, None], axis=1)[:, 0]
    fine = (jnp.einsum('nd,gde->nge', t, w_rt_expert) + b_rt_expert).astype(jnp.float32)
    fine_sel = jnp.take_along_axis(fine, g_idx[:, None, None], axis=1)[:, 0]
    top_logit, top_idx = lax.top_k(fine_sel, TOP_K_INNER)
    top_w = jax.nn.softmax(top_logit, axis=-1)
    expert_id = g_idx[:, None] * EXPERTS_PER_GROUP + top_idx
    weights = g_w[:, None] * top_w
    combine = jnp.sum(jax.nn.one_hot(expert_id, N_EXPERTS, dtype=jnp.float32)
                      * weights[..., None], axis=1)

    def expert_step(acc, params):
        wg, wu, wd, c = params
        hid = jax.nn.silu(t @ wg) * (t @ wu)
        return acc + c[:, None] * (hid @ wd).astype(jnp.float32), None

    acc0 = jnp.zeros((B * S, D), jnp.float32)
    y, _ = lax.scan(expert_step, acc0, (w_e_gate, w_e_up, w_e_down, combine.T))
    return y.reshape(B, S, D).astype(h.dtype)

def second_inputs(seed: int = 0) -> dict:
    key = jax.random.key(seed)
    ks = jax.random.split(key, 32)
    f32 = jnp.float32
    L, D = DEPTH_2, D_MODEL

    def nrm(k, shape, fan_in):
        return jax.random.normal(k, shape, f32) * (fan_in ** -0.5)

    def gain(k, shape):
        return 1.0 + 0.05 * jax.random.normal(k, shape, f32)

    u = jax.random.uniform(ks[16], (L, LRU_WIDTH), f32, 0.9, 0.999)
    s = u ** (1.0 / LRU_C)
    lru_lambda = jnp.log(s) - jnp.log1p(-s)
    return {
        "x": jax.random.normal(ks[0], (BATCH, SEQ, D), f32),
        "p": jax.random.normal(ks[1], (L, BATCH, SEQ, PLE_DIM), f32),
        "g_mix": gain(ks[2], (L, D)),
        "w_in": nrm(ks[3], (L, D, IN_COLS), D),
        "lam_q1": 0.1 * jax.random.normal(ks[4], (L, HEAD_DIM), f32),
        "lam_k1": 0.1 * jax.random.normal(ks[5], (L, HEAD_DIM), f32),
        "lam_q2": 0.1 * jax.random.normal(ks[6], (L, HEAD_DIM), f32),
        "lam_k2": 0.1 * jax.random.normal(ks[7], (L, HEAD_DIM), f32),
        "g_subln": gain(ks[8], (L, V_DIM)),
        "w_conv": nrm(ks[9], (L, CONV_WIDTH, LRU_WIDTH), CONV_WIDTH),
        "b_conv": 0.02 * jax.random.normal(ks[10], (L, LRU_WIDTH), f32),
        "w_rg": nrm(ks[11], (L, LRU_BLOCKS, LRU_BLOCK_W, LRU_BLOCK_W), LRU_BLOCK_W),
        "b_rg": 0.02 * jax.random.normal(ks[12], (L, LRU_BLOCKS, LRU_BLOCK_W), f32),
        "w_ig": nrm(ks[13], (L, LRU_BLOCKS, LRU_BLOCK_W, LRU_BLOCK_W), LRU_BLOCK_W),
        "b_ig": 0.02 * jax.random.normal(ks[14], (L, LRU_BLOCKS, LRU_BLOCK_W), f32),
        "lru_lambda": lru_lambda,
        "w_attn_br": nrm(ks[17], (L, ATTN_WIDTH, D), ATTN_WIDTH),
        "w_lru_br": nrm(ks[18], (L, LRU_WIDTH, D), LRU_WIDTH),
        "w_out": nrm(ks[19], (L, D, D), D),
        "g_moe": gain(ks[20], (L, D)),
        "w_rt_group": nrm(ks[21], (L, D, N_GROUPS), D),
        "b_rt_group": ROUTER_BIAS_SCALE * jax.random.normal(ks[22], (L, N_GROUPS), f32),
        "w_rt_expert": nrm(ks[23], (L, N_GROUPS, D, EXPERTS_PER_GROUP), D),
        "b_rt_expert": ROUTER_BIAS_SCALE * jax.random.normal(ks[24], (L, N_GROUPS, EXPERTS_PER_GROUP), f32),
        "w_e_gate": nrm(ks[25], (L, N_EXPERTS, D, EXPERT_FF), D),
        "w_e_up": nrm(ks[26], (L, N_EXPERTS, D, EXPERT_FF), D),
        "w_e_down": nrm(ks[27], (L, N_EXPERTS, EXPERT_FF, D), EXPERT_FF),
        "g_ple": gain(ks[28], (L, D)),
        "w_ple_gate": nrm(ks[29], (L, D, D), D),
        "w_ple_proj": nrm(ks[30], (L, PLE_DIM, D), PLE_DIM),
        "g_final": gain(ks[31], (D,)),
    }

def second_block(x, p, g_mix, w_in, lam_q1, lam_k1, lam_q2, lam_k2, g_subln, w_conv, b_conv,
              w_rg, b_rg, w_ig, b_ig, lru_lambda, w_attn_br, w_lru_br, w_out, g_moe,
              w_rt_group, b_rt_group, w_rt_expert, b_rt_expert, w_e_gate, w_e_up, w_e_down,
              g_ple, w_ple_gate, w_ple_proj, g_final):
    B, S = x.shape[0], x.shape[1]
    for i in range(DEPTH_2):
        lam_init = 0.8 - 0.6 * math.exp(-0.3 * i)
        h = rmsnorm(x, g_mix[i])
        z = h @ w_in[i]
        q, k, v, xr, gr, ga, gb = jnp.split(z, IN_SPLITS, axis=-1)
        q = q.reshape(B, S, N_HEADS, 2, HEAD_DIM)
        k = k.reshape(B, S, N_HEADS, 2, HEAD_DIM)
        v = v.reshape(B, S, N_HEADS, V_DIM)
        lam = (jnp.exp(jnp.sum(lam_q1[i].astype(jnp.float32) * lam_k1[i].astype(jnp.float32)))
               - jnp.exp(jnp.sum(lam_q2[i].astype(jnp.float32) * lam_k2[i].astype(jnp.float32)))
               + lam_init)
        o = diff_attention(q, k, v, lam)
        o = rmsnorm(o, g_subln[i], SUBLN_EPS) * (1.0 - lam_init)
        attn_branch = o.reshape(B, S, ATTN_WIDTH) @ w_attn_br[i]
        xc = causal_depthwise_conv(xr, w_conv[i], b_conv[i])
        hr = rg_lru(xc, w_rg[i], b_rg[i], w_ig[i], b_ig[i], lru_lambda[i])
        lru_branch = (hr * jax.nn.gelu(gr)) @ w_lru_br[i]
        mixed = jax.nn.sigmoid(ga) * attn_branch + jax.nn.sigmoid(gb) * lru_branch
        x = x + mixed @ w_out[i]
        x = x + hier_moe(rmsnorm(x, g_moe[i]), w_rt_group[i], b_rt_group[i], w_rt_expert[i],
                         b_rt_expert[i], w_e_gate[i], w_e_up[i], w_e_down[i])
        gate = jax.nn.sigmoid(rmsnorm(x, g_ple[i]) @ w_ple_gate[i])
        x = x + gate * (p[i] @ w_ple_proj[i])
    return rmsnorm(x, g_final)


def setup_inputs(seed=0):
    out = dict(first_inputs(seed))
    for name, value in second_inputs(seed + 1).items():
        if name != "x":
            out[name + "_2"] = value
    return out


def reference(
    x, c, ctx, c_ctx, ada_w, ada_b, ln_g, ln_b, ffn_w_in, ffn_w_out, att_w_in, att_q_gain,
    att_k_gain, att_w_out, ml_w_in, ml_gate_b, ml_conv_w, ml_conv_b, ml_norm_g, ml_w_out, p_2,
    g_mix_2, w_in_2, lam_q1_2, lam_k1_2, lam_q2_2, lam_k2_2, g_subln_2, w_conv_2, b_conv_2,
    w_rg_2, b_rg_2, w_ig_2, b_ig_2, lru_lambda_2, w_attn_br_2, w_lru_br_2, w_out_2, g_moe_2,
    w_rt_group_2, b_rt_group_2, w_rt_expert_2, b_rt_expert_2, w_e_gate_2, w_e_up_2, w_e_down_2,
    g_ple_2, w_ple_gate_2, w_ple_proj_2, g_final_2,
):
    x = first_block(
        x, c, ctx, c_ctx, ada_w, ada_b, ln_g, ln_b, ffn_w_in, ffn_w_out, att_w_in, att_q_gain,
        att_k_gain, att_w_out, ml_w_in, ml_gate_b, ml_conv_w, ml_conv_b, ml_norm_g, ml_w_out,
    )
    return second_block(
        x, p_2, g_mix_2, w_in_2, lam_q1_2, lam_k1_2, lam_q2_2, lam_k2_2, g_subln_2, w_conv_2,
        b_conv_2, w_rg_2, b_rg_2, w_ig_2, b_ig_2, lru_lambda_2, w_attn_br_2, w_lru_br_2,
        w_out_2, g_moe_2, w_rt_group_2, b_rt_group_2, w_rt_expert_2, b_rt_expert_2, w_e_gate_2,
        w_e_up_2, w_e_down_2, g_ple_2, w_ple_gate_2, w_ple_proj_2, g_final_2,
    )


_drawn_inputs = setup_inputs


def setup_inputs(seed=0):
    import zlib

    import numpy as np

    out = dict(_drawn_inputs(seed))
    spreads = {}
    factors = {'att_q_gain': 8.0,
     'att_k_gain': 8.0,
     'ml_conv_b': 8.0,
     'ml_norm_g': 8.0,
     'lam_q1_2': 8.0,
     'b_rg_2': 26.897,
     'b_ig_2': 5.445,
     'b_rt_group_2': 15.097,
     'b_rt_expert_2': 9.683,
     'g_ple_2': 6.895}
    for name, (base, spread) in spreads.items():
        noise = np.random.default_rng([zlib.crc32(name.encode()), seed]).standard_normal(out[name].shape)
        drawn = base * np.exp(spread * noise) if base else spread * noise
        out[name] = __import__('jax').numpy.asarray(drawn.astype(out[name].dtype))
    for name, factor in factors.items():
        out[name] = (out[name] * factor).astype(out[name].dtype)
    return out
```

```python
from contextlib import ExitStack

import numpy as np

import concourse.bass as bass
from concourse import mybir

P = 128
D = 1024
KD = D // P
SEQ = 256
CTX = 256
TOK = SEQ + CTX
FF = 2816
FFB = FF // P
HALF_A, HALF_B = 12, 10
TILE = 2048
RING = 3
N_MOD = 9
ADA_TILES = 2 * N_MOD * D // 256
ADA_GROUP = 12
EXPERTS, GROUPS, PER_GROUP, EFF = 32, 4, 8, 512
FFN_TILES = FFB + FFB // 2
ALPHA = (2.0 * 2) ** 0.25
LN_EPS, RMS_EPS, SUBLN_EPS = 1e-5, 1e-6, 1e-5
ATT_SCALE = 128 ** -0.5
ML_SCALE = 128 ** -0.5
DIFF_SCALE = 64 ** -0.5
LAM_INIT = 0.8 - 0.6
LRU_C = 8.0
MASKED = -1e30
GELU_C = (2.0 / np.pi) ** 0.5

PLAN = [
    ("ffn00", FFN_TILES), ("att_in", 6), ("att_out", 4), ("ffn01", FFN_TILES),
    ("ffn10", FFN_TILES), ("ml_in", 13), ("ml_out", 4), ("ffn11", FFN_TILES),
    ("lru_in", 9), ("qkv", 12), ("gates_ab", 8), ("lru_br", 4), ("attn_br", 4), ("w_out", 4),
    ("router", 1), ("experts", EXPERTS * 6), ("ple", 5),
]
FIRST = {}
_n = 0
for _name, _count in PLAN:
    FIRST[_name] = (_n, _n + _count)
    _n += _count
TILES = _n

VECTORS = [
    ("c", 16), ("ada_b", 144), ("ln_g", 48), ("ln_b", 48), ("q_gain", 1), ("k_gain", 1),
    ("ml_conv_w", 24), ("ml_conv_b", 8), ("ml_norm_g", 8), ("gate_b", 2),
    ("g_mix", 8), ("g_moe", 8), ("g_ple", 8), ("g_final", 8), ("g_subln", 1),
    ("w_conv", 32), ("b_conv", 8), ("b_rg", 8), ("b_ig", 8), ("lru_lambda", 8), ("lam", 4), ("b_rt", 36),
]
VEC_AT = {}
_n = 0
for _name, _count in VECTORS:
    VEC_AT[_name] = _n
    _n += _count
N_VEC = _n

CONSTS = [("ident", 128), ("tri_f", 128), ("tri_b", 128), ("iota", 8),
          ("cos", SEQ), ("sin", SEQ), ("swap", 128), ("select", 8 * 128)]
CONST_AT = {}
_n = 0
for _name, _count in CONSTS:
    CONST_AT[_name] = _n
    _n += _count
N_CONST = _n
KEPT_CONST = CONST_AT["cos"]
START_VEC = VEC_AT["ln_g"]

GATE_ROWS = 64
F32 = mybir.dt.float32
F32R = mybir.dt.float32r
U32 = mybir.dt.uint32
ALU = mybir.AluOpType
ACT = mybir.ActivationFunctionType
AX_X = mybir.AxisListType.X


class Signal:

    def __init__(self, sem):
        self.sem, self.n = sem, 0

    def take(self, k):
        self.n += k
        return self.n - k


def program(nc, stream, vec_d, const_d, x_d, p_d, ada_d, out_d):
    ctx = ExitStack()
    with ctx:
        def sb(name, shape, dt=F32):
            return ctx.enter_context(nc.sbuf_tensor(name, shape, dt))

        def sig(name):
            return Signal(ctx.enter_context(nc.semaphore(name)))

        raw = sb("raw", [P, RING, TILE])
        whi = sb("whi", [P, RING, TILE], F32R)
        wlo = sb("wlo", [P, RING, TILE], F32R)
        h = sb("h", [P, KD, TOK])
        xm = sb("xm", [P, 2, KD, TOK], F32R)
        hid = sb("hid", [P, 2, HALF_A, TOK], F32R)
        work = sb("work", [P, 12, TOK])
        tmp = sb("tmp", [P, 4, TOK])
        vec = sb("vec", [P, N_VEC - START_VEC])
        const = sb("const", [P, KEPT_CONST])
        mods = sb("mods", [P, 2, 2, N_MOD, KD])
        ones_one = sb("ones_one", [P, SEQ])
        ratio = sb("ratio", [P, SEQ])
        sq_buf = sb("sq_buf", [P, SEQ])
        eps = sb("eps", [P, 3])
        silu_c = sb("silu_c", [P, KD, 2])
        small = sb("small", [P, 64])
        idx8 = sb("idx8", [P, 2, 2, 8], U32)
        bank = [ctx.enter_context(nc.psum_tensor(f"bank{i}", [P, 2, 512], F32)) for i in range(4)]

        def ps(i):
            return bank[i // 2][:, i % 2, :]

        def pair(i):
            return bank[i]

        def v(name, i=0, n=1):
            a = VEC_AT[name] + i - START_VEC
            return vec[:, a:a + n]

        def cst(name, w, i=0):
            a = CONST_AT[name] + i * w
            return const[:, a:a + w]

        ident = cst("ident", 128)

        def mod(layer, part, s, k):
            return mods[:, s, layer, part, k:k + 1]

        landed = [ctx.enter_context(nc.semaphore(f"landed{i}")) for i in range(RING)]
        hi_done = ctx.enter_context(nc.semaphore("hi_done"))
        lo_done = ctx.enter_context(nc.semaphore("lo_done"))
        tile_used = ctx.enter_context(nc.semaphore("tile_used"))

        def each_tile(eng, t0, t1, body):
            turns = (t1 - t0) // RING
            done = 0
            if turns >= 2:
                with eng.Fori(0, turns) as i:
                    for j in range(RING):
                        body(i * RING + (t0 + j), (t0 + j) % RING, i + (t0 + j + ADA_TILES) // RING, i * RING + j)
                done = turns * RING
            for n in range(t0 + done, t1):
                body(n, n % RING, (n + ADA_TILES) // RING, n - t0)

        def load_tiles(sp, t0, t1):
            def load(n, slot, turn, _):
                sp.wait_ge(lo_done, n - (RING - 1))
                sp.dma_start(raw[:, slot, :], stream[n + ADA_TILES]).then_inc(landed[slot], 16)
            each_tile(sp, t0, t1, load)

        def split_lo(pool, t0, t1):
            def lo(n, slot, turn, _):
                pool.wait_ge(hi_done, n + 1)
                nc.gpsimd.tensor_tensor(wlo[:, slot, :], raw[:, slot, :], whi[:, slot, :].bitcast(F32),
                                        ALU.subtract).then_inc(lo_done, 1)
            each_tile(pool, t0, t1, lo)

        def split_hi(act, n, slot, turn):
            act.wait_ge(tile_used, n - (RING - 1))
            act.wait_ge(landed[slot], turn * 16 + 16)
            nc.scalar.copy(whi[:, slot, :], raw[:, slot, :]).then_inc(hi_done, 1)

        def split_next(act, n, slot, turn):
            if isinstance(n, int) and n + RING >= TILES:
                act.wait_ge(tile_used, n + 1)
                return
            split_hi(act, n + RING, slot, turn + 1)

        def plain_splits(act, t0, t1):
            each_tile(act, t0, t1, lambda n, slot, turn, _: split_next(act, n, slot, turn))

        def mm3(pe, out, w_hi, w_lo, x_hi, x_lo, start):
            pe.matmul(out, w_hi, x_hi, start=start, stop=False, skip_group_check=True)
            pe.matmul(out, w_hi, x_lo, start=False, stop=False, skip_group_check=True)
            return pe.matmul(out, w_lo, x_hi, start=False, stop=True, skip_group_check=True)

        def c_unit(pe, n, slot, outs, cols=slice(0, TOK), ready=None, start=True):
            pe.wait_ge(lo_done, n + 1)
            for b in range(2):
                for k in range(KD):
                    if ready is not None and b == 0:
                        ready(k)
                    at = slice(k * 256 + b * P, k * 256 + b * P + P)
                    last = mm3(pe, outs[b], whi[:, slot, at], wlo[:, slot, at],
                               xm[:, 0, k, cols], xm[:, 1, k, cols], start and k == 0)
            last.then_inc(tile_used, 1)

        def t_unit(pe, n, slot, outs, blocks, fresh):
            pe.wait_ge(lo_done, n + 1)
            for t in range(blocks):
                at = slice(t * P, t * P + P)
                for k in range(KD):
                    w = slice(k * 256, k * 256 + 256)
                    start = k == 0 and t % 2 == 0 if fresh else k == 0
                    last = mm3(pe, outs[t], xm[:, 0, k, at], xm[:, 1, k, at],
                               whi[:, slot, w], wlo[:, slot, w], start)
            last.then_inc(tile_used, 1)

        def d_unit(pe, n, slot, outs, xs, first, signal=None):
            pe.wait_ge(lo_done, n + 1)

            def one(kk, ko):
                at = slice(kk * D + ko * P, kk * D + ko * P + P)
                x_hi, x_lo = xs(kk)
                width = x_hi.shape[-1]
                start = first and kk == 0 and (width == TOK or ko % 2 == 0)
                return mm3(pe, outs[ko], whi[:, slot, at], wlo[:, slot, at], x_hi, x_lo, start)

            if signal is None:
                for kk in range(2):
                    for ko in range(KD):
                        last = one(kk, ko)
            else:
                for ko in range(KD):
                    for kk in range(2):
                        last = one(kk, ko)
                    if ko < KD - 1:
                        last.then_inc(signal.sem, 1)
            last.then_inc(tile_used, 1)

        def d_outs(width):
            if width == TOK:
                return [ps(ko) for ko in range(KD)]
            return [ps(4 + ko // 2)[:, ko % 2 * SEQ:ko % 2 * SEQ + SEQ] for ko in range(KD)]

        xm_f, xm_h, xm_r, xm_a = sig("xm_f"), sig("xm_h"), sig("xm_r"), sig("xm_a")
        act_gate, hid_f, hid_h, hid_r = sig("act_gate"), sig("hid_f"), sig("hid_h"), sig("hid_r")
        d_block, res = sig("d_block"), sig("res")
        mean_done, cent, squared, var_step, std_done = (sig("mean_done"), sig("cent"), sig("squared"),
                                                        sig("var_step"), sig("std_done"))
        rstd_done, normed = sig("rstd_done"), sig("normed")
        vlink, slink, tlink = sig("vlink"), sig("slink"), sig("tlink")

        def linked(eng, link):
            def run(ins):
                ins.then_inc(link.sem, 1)
                link.n += 1
                eng.wait_ge(link.sem, link.n)
            return run

        class Modulated:

            def __init__(self, layer, part, width):
                self.layer, self.part, self.width, self.s = layer, part, width, width // SEQ
                self.f, self.h, self.r, self.a = (xm_f.take(KD * self.s), xm_h.take(KD), xm_r.take(KD),
                                                  xm_a.take(KD))

            def act(self, act):
                for k in range(KD):
                    if k >= 2:
                        act.wait_ge(xm_r.sem, self.r + k - 1)
                    for s in range(self.s):
                        at = slice(s * SEQ, s * SEQ + SEQ)
                        nc.scalar.activation(tmp[:, k % 2, at], h[:, k, at], ACT.Identity,
                                             bias=mod(self.layer, self.part, s, k),
                                             scale=mod(self.layer, self.part + 1, s, k)).then_inc(xm_f.sem, 1)

            def dve(self, dve):
                w = slice(0, self.width)
                for k in range(KD):
                    dve.wait_ge(xm_f.sem, self.f + self.s * (k + 1))
                    nc.vector.tensor_copy(xm[:, 0, k, w], tmp[:, k % 2, w]).then_inc(xm_h.sem, 1)
                    dve.wait_ge(xm_h.sem, self.h + k + 1)
                    nc.vector.tensor_tensor(xm[:, 1, k, w], tmp[:, k % 2, w], xm[:, 0, k, w].bitcast(F32),
                                            ALU.subtract).then_inc(xm_r.sem, 1)
                    nc.vector.tensor_scalar(h[:, k, w], h[:, k, w], ALPHA, None, ALU.mult).then_inc(xm_a.sem, 1)

            def ready(self, pe):
                return lambda k: pe.wait_ge(xm_r.sem, self.r + k + 1)

        class Residual:

            def __init__(self, t1, layer, part, width):
                self.t1, self.layer, self.part, self.width, self.s = t1, layer, part, width, width // SEQ
                self.d, self.r = d_block.take(KD - 1), res.take(KD * self.s)

            def dve(self, dve):
                outs = d_outs(self.width)
                for ko in range(KD):
                    whole = ko if self.width == TOK else ko | 1
                    if whole < KD - 1:
                        dve.wait_ge(d_block.sem, self.d + whole + 1)
                    else:
                        dve.wait_ge(tile_used, self.t1)
                    for s in range(self.s):
                        at = slice(s * SEQ, s * SEQ + SEQ)
                        gate = mod(self.layer, self.part, s, ko) if self.layer is not None else 1.0
                        nc.vector.scalar_tensor_tensor(out=h[:, ko, at], in0=outs[ko][:, at], scalar=gate,
                                                       in1=h[:, ko, at], op0=ALU.mult, op1=ALU.add)\
                            .then_inc(res.sem, 1)

        class LayerNorm:

            def __init__(self, index, width, after):
                self.index, self.width, self.after = index, width, after
                self.m, self.c, self.q = mean_done.take(1), cent.take(KD), squared.take(KD)
                self.v, self.s, self.r, self.n = var_step.take(KD), std_done.take(1), rstd_done.take(1), normed.take(KD)

            def pe(self, pe):
                w = slice(0, self.width)
                for k in range(KD):
                    pe.wait_ge(res.sem, self.after.r + self.after.s * (k + 1))
                    last = pe.matmul(ps(0)[:, w], ones_one[:, 0:P], h[:, k, w], start=(k == 0), stop=(k == KD - 1))
                last.then_inc(mean_done.sem, 1)
                for k in range(KD):
                    pe.wait_ge(squared.sem, self.q + k + 1)
                    pe.matmul(ps(1)[:, w], ones_one[:, 0:P], tmp[:, k % 2, w], start=(k == 0),
                              stop=(k == KD - 1)).then_inc(var_step.sem, 1)

            def dve(self, dve):
                w = slice(0, self.width)
                dve.wait_ge(mean_done.sem, self.m + 1)
                for k in range(KD):
                    nc.vector.scalar_tensor_tensor(out=h[:, k, w], in0=ps(0)[:, w], scalar=-1.0 / D, in1=h[:, k, w],
                                                   op0=ALU.mult, op1=ALU.add).then_inc(cent.sem, 1)
                dve.wait_ge(std_done.sem, self.s + 1)
                nc.vector.reciprocal(tmp[:, 3, w], tmp[:, 2, w]).then_inc(rstd_done.sem, 1)
                dve.wait_ge(rstd_done.sem, self.r + 1)
                for k in range(KD):
                    nc.vector.tensor_tensor(h[:, k, w], h[:, k, w], tmp[:, 3, w], ALU.mult).then_inc(normed.sem, 1)

            def act(self, act):
                w = slice(0, self.width)
                for k in range(KD):
                    act.wait_ge(cent.sem, self.c + k + 1)
                    if k >= 2:
                        act.wait_ge(var_step.sem, self.v + k - 1)
                    nc.scalar.activation(tmp[:, k % 2, w], h[:, k, w], ACT.Square).then_inc(squared.sem, 1)
                act.wait_ge(var_step.sem, self.v + KD)
                nc.scalar.activation(tmp[:, 2, w], ps(1)[:, w], ACT.Sqrt, bias=eps[:, 0:1], scale=1.0 / D)\
                    .then_inc(std_done.sem, 1)
                for k in range(KD):
                    act.wait_ge(normed.sem, self.n + k + 1)
                    nc.scalar.activation(h[:, k, w], h[:, k, w], ACT.Identity,
                                         bias=v("ln_b", self.index * KD + k), scale=v("ln_g", self.index * KD + k))

        class RmsNorm:

            def __init__(self, gain, after=None):
                self.gain = gain
                self.q, self.v, self.s, self.r, self.x = (squared.take(KD), var_step.take(KD), std_done.take(1),
                                                          rstd_done.take(1), xm_r.take(KD))
                self.after = after

            def act(self, act):
                w = slice(0, SEQ)
                for k in range(KD):
                    if self.after is not None:
                        act.wait_ge(res.sem, self.after.r + k + 1)
                    if k >= 2:
                        act.wait_ge(var_step.sem, self.v + k - 1)
                    nc.scalar.activation(tmp[:, k % 2, w], h[:, k, w], ACT.Square).then_inc(squared.sem, 1)
                act.wait_ge(var_step.sem, self.v + KD)
                nc.scalar.activation(tmp[:, 2, w], ps(1)[:, w], ACT.Sqrt, bias=eps[:, 1:2], scale=1.0 / D)\
                    .then_inc(std_done.sem, 1)

            def pe(self, pe):
                w = slice(0, SEQ)
                for k in range(KD):
                    pe.wait_ge(squared.sem, self.q + k + 1)
                    pe.matmul(ps(1)[:, w], ones_one[:, 0:P], tmp[:, k % 2, w], start=(k == 0),
                              stop=(k == KD - 1)).then_inc(var_step.sem, 1)

            def dve(self, dve, split=True):
                w = slice(0, SEQ)
                run = linked(dve, vlink)
                dve.wait_ge(std_done.sem, self.s + 1)
                nc.vector.reciprocal(tmp[:, 3, w], tmp[:, 2, w]).then_inc(rstd_done.sem, 1)
                dve.wait_ge(rstd_done.sem, self.r + 1)
                for k in range(KD):
                    out = tmp[:, k % 2, w] if split else work[:, k, w]
                    run(nc.vector.scalar_tensor_tensor(out=out, in0=h[:, k, w], scalar=v(self.gain, k),
                                                       in1=tmp[:, 3, w], op0=ALU.mult, op1=ALU.mult))
                    if split:
                        run(nc.vector.tensor_copy(xm[:, 0, k, w], out))
                        nc.vector.tensor_tensor(xm[:, 1, k, w], out, xm[:, 0, k, w].bitcast(F32),
                                                ALU.subtract).then_inc(xm_r.sem, 1)

            def ready(self, pe):
                return lambda k: pe.wait_ge(xm_r.sem, self.x + k + 1)

        def stage(t0, t1, tensor, vector, scalar):
            with nc.Block(no_gpsimd_drain=True) as block:
                @block.sync
                def _(sp):
                    load_tiles(sp, min(t0 + 2 * RING, TILES), min(t1 + 2 * RING, TILES))

                @block.gpsimd
                def _(pool):
                    split_lo(pool, min(t0 + RING, TILES), min(t1 + RING, TILES))

                @block.scalar
                def _(act):
                    scalar(act)

                @block.vector
                def _(dve):
                    vector(dve)

                @block.tensor
                def _(pe):
                    tensor(pe)

        params_in, silu_c_done, ada_used, row_done = sig("params_in"), sig("silu_c_done"), sig("ada_used"), sig("row_done")
        rows_out, rows_in, turned, masks_done = sig("rows_out"), sig("rows_in"), sig("turned"), sig("masks_done")
        start_vec = tmp[:, 3, 0:START_VEC]
        rows = work[:, :, :].rearrange("p a b -> p (a b)").rearrange("p (g n) -> p g n", g=2)
        with nc.Block(no_gpsimd_drain=True) as block:
            @block.sync
            def _(sp):
                for slot in range(RING):
                    sp.dma_start(raw[:, slot, :], stream[slot]).then_inc(landed[slot], 16)
                with sp.Fori(1, ADA_TILES // RING) as i:
                    for slot in range(RING):
                        sp.wait_ge(ada_used.sem, (i - 1) * RING + slot + 1)
                        sp.dma_start(raw[:, slot, :], stream[i * RING + slot]).then_inc(landed[slot], 16)
                for slot in range(RING):
                    sp.wait_ge(ada_used.sem, ADA_TILES - RING + slot + 1)
                    sp.dma_start(raw[:, slot, :], stream[ADA_TILES + slot]).then_inc(landed[slot], 16)
                for slot in range(RING):
                    sp.wait_ge(lo_done, slot + 1)
                    sp.dma_start(raw[:, slot, :], stream[ADA_TILES + RING + slot]).then_inc(landed[slot], 16)

            @block.gpsimd
            def _(pool):
                nc.gpsimd.memset(ones_one[:, :], 1.0)
                split_lo(pool, 0, RING)

            @block.scalar
            def _(act):
                act.dma_start(start_vec, vec_d[:, 0:START_VEC]).then_inc(params_in.sem, 16)
                act.wait_ge(params_in.sem, 16)
                nc.scalar.activation(silu_c[:, :, :].rearrange("p k s -> p (k s)"), start_vec[:, 0:16], ACT.Silu)\
                    .then_inc(silu_c_done.sem, 1)
                act.dma_start(vec[:, :], vec_d[:, START_VEC:N_VEC]).then_inc(params_in.sem, 16)
                act.dma_start(const[:, :], const_d[:, 0:KEPT_CONST]).then_inc(params_in.sem, 16)
                act.dma_start(h[:, :, :], x_d).then_inc(params_in.sem, 16)
                for g in range(ADA_TILES // ADA_GROUP):
                    act.wait_ge(row_done.sem, ADA_GROUP * (g + 1))
                    act.dma_start(ada_d[:, g * 3072:(g + 1) * 3072], rows[0:2, g % 2, :]).then_inc(rows_out.sem, 16)
                    act.wait_ge(rows_out.sem, 16 * (g + 1))
                act.dma_start(tmp[0:96, 0, 0:384].rearrange("r (q p) -> r q p", q=3),
                              ada_d.rearrange("s (l p) -> (s l) p", p=P).rearrange("(q r) p -> r q p", r=96))\
                    .then_inc(rows_in.sem, 16)
                for n in range(RING):
                    act.wait_ge(landed[n], 16 * (ADA_TILES // RING) + 16)
                    nc.scalar.copy(whi[:, n, :], raw[:, n, :]).then_inc(hi_done, 1)

            @block.vector
            def _(dve):
                nc.vector.memset(eps[:, 0:1], LN_EPS)
                nc.vector.memset(eps[:, 1:2], RMS_EPS)
                nc.vector.memset(eps[:, 2:3], 1.0)
                for g in range(ADA_TILES // ADA_GROUP):
                    if g >= 2:
                        dve.wait_ge(rows_out.sem, 16 * (g - 1))
                    with dve.Fori(0, ADA_GROUP // RING) as i:
                        for slot in range(RING):
                            dve.wait_ge(ada_used.sem, i * RING + (g * ADA_GROUP + slot + 1))
                            nc.vector.tensor_copy(rows[0:2, g % 2, bass.ds(i * (RING * 256) + slot * 256, 256)],
                                                  ps(slot)[0:2, 0:256]).then_inc(row_done.sem, 1)
                dve.wait_ge(turned.sem, 1)
                run = linked(dve, vlink)
                ada_b = start_vec[:, VEC_AT["ada_b"]:VEC_AT["ada_b"] + 144]
                for s in range(2):
                    m = mods[:, s].rearrange("p l m k -> p (l m k)")
                    run(nc.vector.tensor_tensor(m, ps(3)[:, s * 144:s * 144 + 144], ada_b, ALU.add))
                    for layer in range(2):
                        for part in (1, 4, 7):
                            run(nc.vector.tensor_scalar(mods[:, s, layer, part], mods[:, s, layer, part], 1.0, None, ALU.add))
                        for part in (2, 8):
                            run(nc.vector.tensor_scalar(mods[:, s, layer, part], mods[:, s, layer, part], 0.5, None, ALU.mult))

            @block.tensor
            def _(pe):
                pe.wait_ge(silu_c_done.sem, 1)

                def ada(g, slot):
                    if not isinstance(g, int):
                        pe.wait_ge(row_done.sem, g - (RING - 1))
                    pe.wait_ge(landed[slot], turn16)
                    for k in range(KD):
                        last = pe.matmul(ps(slot)[0:2, 0:256], silu_c[:, k, :], raw[:, slot, k * 256:k * 256 + 256],
                                         start=(k == 0), stop=(k == KD - 1))
                    last.then_inc(ada_used.sem, 1)

                for slot in range(RING):
                    turn16 = 16
                    ada(slot, slot)
                with pe.Fori(1, ADA_TILES // RING) as i:
                    for slot in range(RING):
                        turn16 = i * 16 + 16
                        ada(i * RING + slot, slot)
                pe.wait_ge(rows_in.sem, 16)
                pe.wait_ge(params_in.sem, 64)
                for q in range(3):
                    last = pe.transpose(ps(3)[:, q * 96:q * 96 + 96], tmp[0:96, 0, q * P:q * P + P], ident[0:96, 0:96])
                last.then_inc(turned.sem, 1)

        def ffn(name, layer, which, width):
            t0, _ = FIRST[name]
            part = 6 * which
            mx = Modulated(layer, part, width)
            w = slice(0, width)
            parts = []
            n = t0
            for first_block, blocks in ((0, HALF_A), (HALF_A, HALF_B)):
                parts.append((n, n + blocks, n + blocks + blocks // 2, act_gate.take(blocks), hid_f.take(blocks),
                              hid_h.take(blocks), hid_r.take(blocks),
                              Residual(n + blocks + blocks // 2, layer, part + 2, width)))
                n += blocks + blocks // 2
            t1 = n
            ln = LayerNorm(layer * 3 + 2 * which, width, parts[1][-1])
            outs = d_outs(width)

            def tensor(pe):
                for i, (g0, g1, d1, ag, hf, hh, hr, rs) in enumerate(parts):
                    def gate_up(n, slot, turn, u, hr=hr):
                        if not isinstance(u, int) or u >= RING:
                            pe.wait_ge(hid_r.sem, u + (hr - (RING - 1)))
                        c_unit(pe, n, slot, [ps(2 * slot)[:, w], ps(2 * slot + 1)[:, w]], w)
                    ready = mx.ready(pe) if i == 0 else None
                    if i == 1:
                        pe.wait_ge(res.sem, parts[0][-1].r + KD * parts[0][-1].s)
                    c_unit(pe, g0, g0 % RING, [ps(2 * (g0 % RING))[:, w], ps(2 * (g0 % RING) + 1)[:, w]], w, ready)
                    rest = (g1 - g0 - 1) // RING * RING
                    for u in range(1, 1 + RING):
                        gate_up(g0 + u, (g0 + u) % RING, None, u)
                    shifted_tiles(pe, g0 + 1 + RING, g1, lambda n, s, t, u, f=gate_up: f(n, s, t, u + (1 + RING)))
                    for d in range(g1, d1):
                        pe.wait_ge(hid_r.sem, hr + (g1 - g0))
                        d_unit(pe, d, d % RING, outs, lambda kk, j=d - g1: (hid[:, 0, 2 * j + kk, w], hid[:, 1, 2 * j + kk, w]),
                               d == g1, d_block if d == d1 - 1 else None)
                ln.pe(pe)

            def scalar(act):
                mx.act(act)
                for g0, g1, d1, ag, hf, hh, hr, rs in parts:
                    def gate(n, slot, turn, u, ag=ag, hf=hf):
                        split_next(act, n, slot, turn)
                        act.wait_ge(tile_used, n + 1)
                        if not isinstance(u, int) or u >= RING:
                            act.wait_ge(hid_f.sem, u + (hf - (RING - 1)))
                        nc.scalar.activation(work[:, slot, w], ps(2 * slot)[:, w], ACT.Silu).then_inc(act_gate.sem, 1)
                    for u in range(RING):
                        gate(g0 + u, (g0 + u) % RING, (g0 + u + ADA_TILES) // RING, u)
                    shifted_tiles(act, g0 + RING, g1, lambda n, s, t, u, f=gate: f(n, s, t, u + RING))
                    plain_splits(act, g1, d1)
                ln.act(act)

            def vector(dve):
                mx.dve(dve)
                dve.wait_ge(xm_a.sem, mx.a + KD)
                for i, (g0, g1, d1, ag, hf, hh, hr, rs) in enumerate(parts):
                    if i == 1:
                        dve.wait_ge(tile_used, parts[0][2])
                    def up(n, slot, turn, u, ag=ag, hf=hf, hh=hh, hr=hr):
                        dve.wait_ge(act_gate.sem, u + (ag + 1))
                        nc.vector.tensor_tensor(work[:, 3 + slot, w], work[:, slot, w], ps(2 * slot + 1)[:, w],
                                                ALU.mult).then_inc(hid_f.sem, 1)
                        dve.wait_ge(hid_f.sem, u + (hf + 1))
                        at = slice(u, u + 1) if isinstance(u, int) else bass.ds(u, 1)
                        nc.vector.tensor_scalar(hid[:, 0, at, w], work[:, 3 + slot:4 + slot, w], 1.0, None, ALU.mult)\
                            .then_inc(hid_h.sem, 1)
                        dve.wait_ge(hid_h.sem, u + (hh + 1))
                        nc.vector.tensor_tensor(hid[:, 1, at, w], work[:, 3 + slot:4 + slot, w],
                                                hid[:, 0, at, w].bitcast(F32), ALU.subtract).then_inc(hid_r.sem, 1)
                    each_tile(dve, g0, g1, up)
                    if i == 1:
                        dve.wait_ge(res.sem, parts[0][-1].r + KD * parts[0][-1].s)
                    rs.dve(dve)
                ln.dve(dve)

            stage(t0, t1, tensor, vector, scalar)

        def shifted_tiles(eng, t0, t1, body):
            if t1 > t0:
                each_tile(eng, t0, t1, body)

        q_of = [hid[:, a, 0:8, :] for a in range(2)]
        k_of = [hid[:, a, 8:10, :] for a in range(2)]
        v_of = [hid[:, a, 10:12, :].rearrange("p a b -> p (a b)").rearrange("p (t c) -> p t c", t=4) for a in range(2)]
        rope = work[:, 10:12, :].rearrange("p a b -> p (a b)")[:, 0:2 * SEQ + 128]
        sq_done, rms_done, head_f, swapped, rope_in = (sig("sq_done"), sig("rms_done"), sig("head_f"), sig("swapped"),
                                                       sig("rope_in"))
        head_std, head_r = sig("head_std"), sig("head_r")

        def attention_in():
            t0, t1 = FIRST["att_in"]
            mx = Modulated(0, 3, TOK)
            b_sq, b_rms, b_f, b_sw, b_r = sq_done.take(5), rms_done.take(5), head_f.take(5), swapped.take(5), head_r.take(6)
            b_std = head_std.take(5)

            def tensor(pe):
                for u in range(8):
                    if u < 5:
                        if u >= 2:
                            pe.wait_ge(head_f.sem, b_f + u - 1)
                        c_unit(pe, t0 + u, (t0 + u) % RING, [ps(2 * (u % 2)), ps(2 * (u % 2) + 1)],
                               ready=mx.ready(pe) if u == 0 else None)
                    if u == 5:
                        pe.wait_ge(head_f.sem, b_f + 4)
                        t_unit(pe, t0 + 5, (t0 + 5) % RING,
                               [ps(2 + t // 2)[:, t % 2 * 256:t % 2 * 256 + 256] for t in range(4)], 4, False)
                    if 1 <= u <= 5:
                        j = u - 1
                        pe.wait_ge(sq_done.sem, b_sq + j + 1)
                        if j >= 1:
                            pe.wait_ge(head_std.sem, b_std + j)
                        for b in range(2):
                            last = pe.matmul(ps(4 + b), ones_one[:, 0:P], work[:, b, :], start=True, stop=True)
                        last.then_inc(rms_done.sem, 1)
                    if 2 <= u <= 6:
                        j = u - 2
                        pe.wait_ge(head_f.sem, b_f + j + 1)
                        pe.wait_ge(rope_in.sem, 16)
                        if j >= 1:
                            pe.wait_ge(head_r.sem, b_r + j)
                        for b in range(2):
                            last = pe.matmul(ps(6)[:, b * 256:b * 256 + 256], rope[:, 2 * SEQ:2 * SEQ + 128], work[:, 4 + b, 0:SEQ],
                                             start=True, stop=True)
                        last.then_inc(swapped.sem, 1)

            def scalar(act):
                act.dma_start(rope, const_d[:, KEPT_CONST:KEPT_CONST + 2 * SEQ + 128]).then_inc(rope_in.sem, 16)
                mx.act(act)
                for u in range(6):
                    split_next(act, t0 + u, (t0 + u) % RING, (t0 + u + ADA_TILES) // RING)
                    if u < 5:
                        act.wait_ge(tile_used, t0 + u + 1)
                        if u >= 1:
                            act.wait_ge(rms_done.sem, b_rms + u)
                        nc.scalar.activation(work[:, 0:2, :], pair(u % 2)[:, :, :], ACT.Square).then_inc(sq_done.sem, 1)
                        act.wait_ge(rms_done.sem, b_rms + u + 1)
                        if u >= 1:
                            act.wait_ge(head_f.sem, b_f + u)
                        nc.scalar.activation(work[:, 2:4, :], pair(2)[:, :, :], ACT.Sqrt, bias=eps[:, 1:2], scale=1.0 / P)\
                            .then_inc(head_std.sem, 1)

            def vector(dve):
                mx.dve(dve)
                run = linked(dve, vlink)
                dve.wait_ge(rope_in.sem, 16)
                for u in range(5):
                    gain = v("q_gain") if u < 4 else v("k_gain")
                    dst = [q_of[a][:, 2 * u:2 * u + 2, :] if u < 4 else k_of[a] for a in range(2)]
                    dve.wait_ge(head_std.sem, b_std + u + 1)
                    run(nc.vector.reciprocal(work[:, 8:10, :], work[:, 2:4, :]))
                    if u >= 1:
                        dve.wait_ge(swapped.sem, b_sw + u)
                    nc.vector.scalar_tensor_tensor(out=work[:, 4:6, :], in0=pair(u % 2)[:, :, :], scalar=gain,
                                                   in1=work[:, 8:10, :], op0=ALU.mult, op1=ALU.mult)\
                        .then_inc(head_f.sem, 1)
                    dve.wait_ge(swapped.sem, b_sw + u + 1)
                    for b in range(2):
                        nc.vector.tensor_tensor(work[:, 6, b * 256:b * 256 + 256], ps(6)[:, b * 256:b * 256 + 256],
                                                rope[:, SEQ:2 * SEQ], ALU.mult)
                        run(nc.vector.tensor_tensor(work[:, 7, b * 256:b * 256 + 256], work[:, 4 + b, 0:SEQ],
                                                    rope[:, 0:SEQ], ALU.mult))
                    for b in range(2):
                        run(nc.vector.tensor_tensor(work[:, 4 + b, 0:SEQ], work[:, 7, b * 256:b * 256 + 256],
                                                    work[:, 6, b * 256:b * 256 + 256], ALU.add))
                    run(nc.vector.tensor_copy(dst[0], work[:, 4:6, :]))
                    nc.vector.tensor_tensor(dst[1], work[:, 4:6, :], dst[0].bitcast(F32), ALU.subtract)\
                        .then_inc(head_r.sem, 1)
                dve.wait_ge(tile_used, t1)
                vv = pair(1)[:, :, :].rearrange("p a (t c) -> p (a t) c", c=256)
                run(nc.vector.tensor_copy(v_of[0], vv))
                nc.vector.tensor_tensor(v_of[1], vv, v_of[0].bitcast(F32), ALU.subtract).then_inc(head_r.sem, 1)

            stage(t0, t1, tensor, vector, scalar)

        row_max, exp_done, prob_done, prob_t, prob_s, pv_done, o_done = (
            sig("row_max"), sig("exp_done"), sig("prob_done"), sig("prob_t"), sig("prob_s"), sig("pv_done"), sig("o_done"))
        score_done = sig("score_done")

        def attention_core():
            items = [(hd, s) for hd in range(8) for s in range(2)]
            n_items = len(items)
            b_sc, b_mx, b_ex, b_pr, b_pt, b_ps, b_pv, b_o = (
                score_done.take(n_items), row_max.take(n_items), exp_done.take(2 * n_items), prob_done.take(n_items),
                prob_t.take(n_items), prob_s.take(n_items), pv_done.take(n_items), o_done.take(n_items))
            t0 = FIRST["att_in"][1]

            def keys(s):
                return (0, 4) if s == 0 else (2, 4)

            def scores(pe, i):
                hd, s = items[i]
                k0, k1 = keys(s)
                if i >= 2:
                    pe.wait_ge(exp_done.sem, b_ex + 2 * (i - 1))
                kk = slice(k0 * P, k1 * P)
                for q in range(2):
                    at = slice(s * SEQ + q * P, s * SEQ + q * P + P)
                    last = mm3(pe, ps(2 * (i % 2) + q)[:, kk], q_of[0][:, hd, at], q_of[1][:, hd, at],
                               k_of[0][:, hd // 4, kk], k_of[1][:, hd // 4, kk], True)
                last.then_inc(score_done.sem, 1)

            def tensor(pe):
                scores(pe, 0)
                for i in range(n_items + 1):
                    if i + 1 < n_items:
                        scores(pe, i + 1)
                    if i < n_items:
                        k0, k1 = keys(items[i][1])
                        pe.wait_ge(prob_done.sem, b_pr + i + 1)
                        if i >= 1:
                            pe.wait_ge(prob_s.sem, b_ps + i)
                        for b in range(k0, k1):
                            for q in range(2):
                                at = (b - k0) * 256 + q * P
                                last = pe.transpose(ps(4 + at // 512)[:, at % 512:at % 512 + P],
                                                    work[:, 2 * (i % 2) + q, b * P:b * P + P], ident)
                        last.then_inc(prob_t.sem, 1)
                    if i >= 1:
                        j = i - 1
                        hd, s = items[j]
                        k0, k1 = keys(s)
                        pe.wait_ge(prob_s.sem, b_ps + j + 1)
                        if j >= 2:
                            pe.wait_ge(o_done.sem, b_o + j - 1)
                        c0 = hd // 4 * P
                        for b in range(k0, k1):
                            pt = slice((b - k0) * 256, (b - k0) * 256 + 256)
                            last = mm3(pe, ps(6 + j % 2)[:, 0:256], v_of[0][:, b, c0:c0 + P], v_of[1][:, b, c0:c0 + P],
                                       pt_of(j)[0][:, pt], pt_of(j)[1][:, pt], b == k0)
                        last.then_inc(pv_done.sem, 1)

            def pt_of(j):
                return [xm[:, a, 6:8, :].rearrange("p a b -> p (a b)") for a in range(2)]

            def scalar(act):
                for i, (hd, s) in enumerate(items):
                    kk = slice(keys(s)[0] * P, keys(s)[1] * P)
                    act.wait_ge(row_max.sem, b_mx + i + 1)
                    if i >= 2:
                        act.wait_ge(prob_t.sem, b_pt + i - 1)
                    for q in range(2):
                        nc.scalar.activation(work[:, 2 * (i % 2) + q, kk], ps(2 * (i % 2) + q)[:, kk], ACT.Exp,
                                             bias=small[:, 4 + 2 * (i % 2) + q:5 + 2 * (i % 2) + q], scale=ATT_SCALE,
                                             accum_out=small[:, 8 + 2 * (i % 2) + q:9 + 2 * (i % 2) + q])\
                            .then_inc(exp_done.sem, 1)

            def vector(dve):
                run = linked(dve, vlink)

                def maxima(i):
                    s = items[i][1]
                    kk = slice(keys(s)[0] * P, keys(s)[1] * P)
                    dve.wait_ge(score_done.sem, b_sc + i + 1)
                    a = 2 * (i % 2)
                    run(nc.vector.tensor_reduce(small[:, a:a + 2], pair(i % 2)[:, :, kk], AX_X, ALU.max))
                    nc.vector.tensor_scalar(small[:, 4 + a:6 + a], small[:, a:a + 2], -ATT_SCALE, None, ALU.mult)\
                        .then_inc(row_max.sem, 1)

                maxima(0)
                for i, (hd, s) in enumerate(items):
                    if i + 1 < n_items:
                        maxima(i + 1)
                    k0, k1 = keys(s)
                    kk = slice(k0 * P, k1 * P)
                    a = 2 * (i % 2)
                    dve.wait_ge(exp_done.sem, b_ex + 2 * (i + 1))
                    run(nc.vector.reciprocal(small[:, 12:14], small[:, 8 + a:10 + a]))
                    run(nc.vector.tensor_scalar(work[:, a, kk], work[:, a, kk], small[:, 12:13], None, ALU.mult))
                    nc.vector.tensor_scalar(work[:, a + 1, kk], work[:, a + 1, kk], small[:, 13:14], None, ALU.mult)\
                        .then_inc(prob_done.sem, 1)
                    dve.wait_ge(prob_t.sem, b_pt + i + 1)
                    if i >= 1:
                        dve.wait_ge(pv_done.sem, b_pv + i)
                    n = (k1 - k0) * 256
                    src = pair(2)[:, :, :].rearrange("p a b -> p (a b)")[:, 0:n]
                    run(nc.vector.tensor_copy(pt_of(i)[0][:, 0:n], src))
                    nc.vector.tensor_tensor(pt_of(i)[1][:, 0:n], src, pt_of(i)[0][:, 0:n].bitcast(F32), ALU.subtract)\
                        .then_inc(prob_s.sem, 1)
                    if i >= 1:
                        output(dve, i - 1, run)
                output(dve, n_items - 1, run)

            def output(dve, j, run):
                hd, s = items[j]
                dve.wait_ge(pv_done.sem, b_pv + j + 1)
                nc.vector.tensor_copy(work[:, 4 + hd, s * SEQ:s * SEQ + SEQ], ps(6 + j % 2)[:, 0:256])\
                    .then_inc(o_done.sem, 1)

            stage(t0, t0, tensor, vector, scalar)

        def project(name, layer, part, width, index, source):
            t0, t1 = FIRST[name]
            rs = Residual(t1, layer, part, width)
            ln = LayerNorm(index, width, rs)
            b_r = xm_r.take(KD)
            w = slice(0, width)
            outs = d_outs(width)

            def tensor(pe):
                for d in range(t0, t1):
                    pe.wait_ge(xm_r.sem, b_r + 2 * (d - t0) + 2)
                    d_unit(pe, d, d % RING, outs, lambda kk, j=d - t0: (xm[:, 0, 2 * j + kk, w], xm[:, 1, 2 * j + kk, w]),
                           d == t0, d_block if d == t1 - 1 else None)
                ln.pe(pe)

            def scalar(act):
                plain_splits(act, t0, t1)
                ln.act(act)

            def vector(dve):
                run = linked(dve, vlink)
                for k in range(KD):
                    run(nc.vector.tensor_copy(xm[:, 0, k, w], source(k)))
                    nc.vector.tensor_tensor(xm[:, 1, k, w], source(k), xm[:, 0, k, w].bitcast(F32), ALU.subtract)\
                        .then_inc(xm_r.sem, 1)
                rs.dve(dve)
                ln.dve(dve)

            stage(t0, t1, tensor, vector, scalar)

        flat_hid = [hid[:, a, :, :].rearrange("p a b -> p (a b)") for a in range(2)]
        mk = [flat_hid[a][:, 0:4 * TOK].rearrange("p (h t) -> p h t", h=4) for a in range(2)]
        mv = [flat_hid[a][:, 4 * TOK:12 * TOK].rearrange("p (t c) -> p t c", t=4) for a in range(2)]
        q_raw = work[:, 0:2, :].rearrange("p a b -> p (a b)").rearrange("p (h t) -> p h t", h=4)
        o_gate = work[:, 2:6, :].rearrange("p a b -> p (a b)").rearrange("p (k t) -> p k t", k=KD)
        mq = [xm[:, a, 0:2, :].rearrange("p a b -> p (a b)").rearrange("p (h t) -> p h t", h=4) for a in range(2)]
        gates_in, ml_evac, conv_act, o_act, abs_done, soft_done, stab_sum = (
            sig("gates_in"), sig("ml_evac"), sig("conv_act"), sig("o_act"), sig("abs_done"),
            sig("soft_done"), sig("stab_sum"))

        def mlstm_in():
            t0, t1 = FIRST["ml_in"]
            mx = Modulated(1, 3, TOK)
            lat = slice(0, SEQ)
            rows = slice(0, GATE_ROWS)

            def tensor(pe):
                for u in range(13):
                    if u == 4:
                        pe.wait_ge(gates_in.sem, 2)
                    if u >= 5:
                        pe.wait_ge(ml_evac.sem, u - 4)
                    a, n = 2 * (u % 4), t0 + u
                    if u < 3:
                        c_unit(pe, n, n % RING, [ps(a), ps(a + 1)], ready=mx.ready(pe) if u == 0 else None)
                    elif 5 <= u < 9:
                        t_unit(pe, n, n % RING, [ps(a + t // 2)[:, t % 2 * 256:t % 2 * 256 + 256] for t in range(4)],
                               4, False)
                    else:
                        c_unit(pe, n, n % RING, [ps(a)[:, lat], ps(a + 1)[:, lat]], lat)

            def scalar(act):
                run = linked(act, slink)
                mx.act(act)
                for u in range(13):
                    n = t0 + u
                    split_next(act, n, n % RING, (n + ADA_TILES) // RING)
                    act.wait_ge(tile_used, n + 1)
                    if u == 0:
                        nc.scalar.activation(work[rows, 10, :], ps(0)[rows, :], ACT.Identity, bias=v("gate_b", 0)[rows, :])\
                            .then_inc(gates_in.sem, 1)
                        nc.scalar.activation(work[rows, 11, :], ps(1)[rows, :], ACT.Identity, bias=v("gate_b", 1)[rows, :])\
                            .then_inc(gates_in.sem, 1)
                        act.wait_ge(abs_done.sem, 1)
                        run(nc.scalar.activation(tmp[rows, 1, :], tmp[rows, 0, :], ACT.Exp, scale=-1.0))
                        nc.scalar.activation(tmp[rows, 0, :], tmp[rows, 1, :], ACT.Ln, bias=eps[rows, 2:3])\
                            .then_inc(soft_done.sem, 1)
                        act.wait_ge(stab_sum.sem, 1)
                        run(nc.scalar.activation(work[rows, 11, SEQ:TOK], tmp[rows, 2, lat], ACT.Exp, scale=-1.0))
                    elif u < 5:
                        j = u - 1
                        act.wait_ge(ml_evac.sem, j + 1)
                        out = work[:, 8:10, :] if j < 2 else q_raw[:, 2 * (j - 2):2 * (j - 2) + 2, :]
                        src = work[:, 6:8, :] if j < 2 else work[:, 6:8, lat]
                        nc.scalar.activation(out, src, ACT.Silu).then_inc(conv_act.sem, 1)
                    elif u >= 9:
                        j = u - 9
                        nc.scalar.activation(o_gate[:, 2 * j:2 * j + 2, :], pair(u % 4)[:, :, lat], ACT.Sigmoid)\
                            .then_inc(o_act.sem, 1)

            def vector(dve):
                run = linked(dve, vlink)
                mx.dve(dve)
                f, b = slice(0, 4), slice(32, 36)
                dve.wait_ge(gates_in.sem, 2)
                nc.vector.scalar_tensor_tensor(out=tmp[rows, 0, :], in0=work[rows, 11, :], scalar=-1.0, in1=work[rows, 11, :], op0=ALU.mult, op1=ALU.max).then_inc(abs_done.sem, 1)
                run(nc.vector.memset(tmp[rows, 3, :], 0.0))
                dve.wait_ge(soft_done.sem, 1)
                run(nc.vector.scalar_tensor_tensor(out=tmp[rows, 2, :], in0=work[rows, 11, :], scalar=0.0,
                                                   in1=tmp[rows, 0, :], op0=ALU.min, op1=ALU.subtract))

                def scans(dst, src, op):
                    run(nc.vector.tensor_tensor_scan(dst[f, SEQ:TOK], ones_one[f, :], src[f, SEQ:TOK], 0.0, ALU.mult, op))
                    run(nc.vector.tensor_tensor_scan(dst[f, 0:SEQ], ones_one[f, :], src[f, 0:SEQ],
                                                     dst[f, TOK - 1:TOK], ALU.mult, op))
                    run(nc.vector.tensor_tensor_scan(dst[b, TOK - 1:SEQ - 1:-1], ones_one[b, :], src[b, TOK - 1:SEQ - 1:-1],
                                                     0.0, ALU.mult, op))
                    run(nc.vector.tensor_tensor_scan(dst[b, SEQ - 1::-1], ones_one[b, :], src[b, SEQ - 1::-1],
                                                     dst[b, SEQ:SEQ + 1], ALU.mult, op))
                scans(tmp[:, 3, :], tmp[:, 2, :], ALU.add)
                run(nc.vector.tensor_tensor(work[rows, 10, :], work[rows, 10, :], tmp[rows, 3, :], ALU.subtract))
                run(nc.vector.memset(tmp[rows, 1, :], 0.0))
                scans(tmp[:, 1, :], work[:, 10, :], ALU.max)
                run(nc.vector.tensor_copy(work[rows, 11, lat], tmp[rows, 1, lat]))
                nc.vector.tensor_tensor(tmp[rows, 2, lat], tmp[rows, 1, lat], tmp[rows, 3, lat], ALU.add)\
                    .then_inc(stab_sum.sem, 1)
                for j in range(4):
                    u = j + 1
                    width = TOK if j < 2 else SEQ
                    dve.wait_ge(tile_used, t0 + u + 1)
                    if j >= 1:
                        dve.wait_ge(conv_act.sem, j)
                    src = pair(u % 4)
                    for blk in range(2):
                        fb = 4 + 2 * j + blk if j < 2 else 2 * (j - 2) + blk
                        y = work[:, 6 + blk, :]
                        run(nc.vector.tensor_scalar(y[:, 0:width], src[:, blk, 0:width], v("ml_conv_w", KD + fb),
                                                    v("ml_conv_b", fb), ALU.mult, ALU.add))
                        for s in range(width // SEQ):
                            lo, hi = s * SEQ, s * SEQ + SEQ
                            run(nc.vector.scalar_tensor_tensor(out=y[:, lo + 1:hi], in0=src[:, blk, lo:hi - 1],
                                                               scalar=v("ml_conv_w", fb), in1=y[:, lo + 1:hi],
                                                               op0=ALU.mult, op1=ALU.add))
                            last = nc.vector.scalar_tensor_tensor(out=y[:, lo:hi - 1], in0=src[:, blk, lo + 1:hi],
                                                                  scalar=v("ml_conv_w", 2 * KD + fb), in1=y[:, lo:hi - 1],
                                                                  op0=ALU.mult, op1=ALU.add)
                            if not (blk == 1 and hi == width):
                                run(last)
                    last.then_inc(ml_evac.sem, 1)
                    if j < 2:
                        dve.wait_ge(conv_act.sem, j + 1)
                        dst = [mk[a][:, 2 * j:2 * j + 2, :] for a in range(2)]
                        run(nc.vector.tensor_copy(dst[0], work[:, 8:10, :]))
                        run(nc.vector.tensor_tensor(dst[1], work[:, 8:10, :], dst[0].bitcast(F32), ALU.subtract))
                for j in range(4):
                    u = 5 + j
                    dve.wait_ge(tile_used, t0 + u + 1)
                    vv = pair(u % 4)[:, :, :].rearrange("p a (t c) -> p (a t) c", c=256)
                    dst = [mv[a][:, :, j * 256:j * 256 + 256] for a in range(2)]
                    run(nc.vector.tensor_copy(dst[0], vv))
                    nc.vector.tensor_tensor(dst[1], vv, dst[0].bitcast(F32), ALU.subtract).then_inc(ml_evac.sem, 1)

            stage(t0, t1, tensor, vector, scalar)

        cols_turned, spread, ml_args, ml_exp, ml_prob, ml_turned, ml_split, ml_num, ml_var, ml_std, ml_hn, ml_hnt, ml_out = (
            sig(n) for n in ("cols_turned", "spread", "ml_args", "ml_exp", "ml_prob", "ml_turned", "ml_split", "ml_num",
                             "ml_var", "ml_std", "ml_hn", "ml_hnt", "ml_out"))
        cols_ready, select_in = sig("cols_ready"), sig("select_in")

        def mlstm_core():
            t0 = FIRST["ml_in"][1]
            items = [(hd, t) for hd in range(4) for t in range(2)]
            n_items = len(items)
            b_sc = score_done.take(n_items)
            rows = slice(0, GATE_ROWS)
            mpt = [xm[:, a, 2, :] for a in range(2)]
            select = tmp[0:GATE_ROWS, 1:3, :].rearrange("p a b -> p (a b)").rearrange("p (r c) -> p r c", r=8)
            gcol = tmp[:, 3, 0:256]

            def row(hd, back):
                return hd + 32 * back

            def tensor(pe):
                for m in range(4):
                    last = pe.transpose(ps(7)[:, m * 64:m * 64 + 64], work[rows, 11, m * P:m * P + P], ident[rows, rows])
                last.then_inc(cols_turned.sem, 1)
                pe.wait_ge(select_in.sem, 16)
                pe.wait_ge(cols_ready.sem, 1)

                def front(i):
                    hd, t = items[i]
                    if t == 0:
                        if i >= 2:
                            pe.wait_ge(ml_args.sem, i)
                        for back in range(2):
                            last = pe.matmul(ps(2 + back), select[:, hd + 4 * back, :], work[rows, 10, :],
                                             start=True, stop=True)
                        last.then_inc(spread.sem, 1)
                    if i >= 2:
                        pe.wait_ge(ml_prob.sem, i - 1)
                    at = slice(t * P, t * P + P)
                    mm3(pe, ps(i % 2), mq[0][:, hd, at], mq[1][:, hd, at], mk[0][:, hd, :], mk[1][:, hd, :], True)\
                        .then_inc(score_done.sem, 1)

                def middle(i):
                    pe.wait_ge(ml_prob.sem, i + 1)
                    if i >= 1:
                        pe.wait_ge(ml_split.sem, i)
                    for b in range(4):
                        last = pe.transpose(ps(4)[:, b * P:b * P + P], work[:, 8, b * P:b * P + P], ident)
                    last.then_inc(ml_turned.sem, 1)
                    pe.wait_ge(ml_split.sem, i + 1)
                    if i >= 2:
                        pe.wait_ge(ml_hn.sem, i - 1)
                    hd = items[i][0]
                    for b in range(4):
                        pt = slice(b * P, b * P + P)
                        vc = slice(hd * 256, hd * 256 + 256)
                        last = mm3(pe, ps(5 + i % 2)[:, 0:256], mpt[0][:, pt], mpt[1][:, pt],
                                   mv[0][:, b, vc], mv[1][:, b, vc], b == 0)
                    last.then_inc(ml_num.sem, 1)

                def back_end(i):
                    pe.wait_ge(ml_hn.sem, i + 1)
                    if i >= 1:
                        pe.wait_ge(ml_out.sem, i)
                    for b in range(2):
                        last = pe.transpose(ps(7)[:, b * P:b * P + P], tmp[:, 0, b * P:b * P + P], ident)
                    last.then_inc(ml_hnt.sem, 1)

                front(0)
                for i in range(n_items):
                    if i + 1 < n_items:
                        front(i + 1)
                    middle(i)
                    if i >= 1:
                        back_end(i - 1)
                back_end(n_items - 1)

            def scalar(act):
                act.dma_start(tmp[0:GATE_ROWS, 1:3, :].rearrange("p a b -> p (a b)"),
                              const_d[0:GATE_ROWS, CONST_AT["select"]:N_CONST]).then_inc(select_in.sem, 16)
                act.wait_ge(cols_ready.sem, 1)
                for i in range(n_items + 1):
                    if i < n_items:
                        hd, t = items[i]
                        act.wait_ge(ml_args.sem, i + 1)
                        for back in range(2):
                            c = t * 64 + row(hd, back)
                            nc.scalar.activation(work[:, 6 + back, :], work[:, 6 + back, :], ACT.Exp, bias=gcol[:, c:c + 1])\
                                .then_inc(ml_exp.sem, 1)
                    if i >= 1:
                        act.wait_ge(ml_var.sem, i)
                        nc.scalar.activation(small[:, 20:21], small[:, 19:20], ACT.Sqrt, bias=eps[:, 0:1])\
                            .then_inc(ml_std.sem, 1)

            def vector(dve):
                run = linked(dve, vlink)
                run(nc.vector.tensor_copy(mq[0], q_raw))
                run(nc.vector.tensor_tensor(mq[1], q_raw, mq[0].bitcast(F32), ALU.subtract))
                dve.wait_ge(cols_turned.sem, 1)
                run(nc.vector.tensor_scalar(gcol[:, 0:128], ps(7)[:, 0:128], -1.0, None, ALU.mult))
                nc.vector.tensor_copy(gcol[:, 128:256], ps(7)[:, 128:256]).then_inc(cols_ready.sem, 1)
                dve.wait_ge(cols_ready.sem, 1)

                def args(i):
                    hd, t = items[i]
                    dve.wait_ge(spread.sem, hd + 1)
                    for back in range(2):
                        run(nc.vector.tensor_copy(work[:, 6 + back, :], ps(2 + back)))
                    own = slice(t * P, t * P + P)
                    run(nc.vector.tensor_tensor(work[:, 6, own], work[:, 6, own], cst("tri_f", 128), ALU.add))
                    run(nc.vector.memset(work[:, 6 + t, (1 - t) * P:(1 - t) * P + P], MASKED))
                    nc.vector.tensor_tensor(work[:, 7, own], work[:, 7, own], cst("tri_b", 128), ALU.add)\
                        .then_inc(ml_args.sem, 1)

                def probs(i):
                    hd, t = items[i]
                    dve.wait_ge(score_done.sem, b_sc + i + 1)
                    dve.wait_ge(ml_exp.sem, 2 * i + 2)
                    if i >= 1:
                        dve.wait_ge(ml_turned.sem, i)
                    for back in range(2):
                        run(nc.vector.tensor_tensor_reduce(work[:, 8 + back, :], work[:, 6 + back, :], ps(i % 2), ML_SCALE, 0.0,
                                                           ALU.mult, ALU.add, small[:, back:back + 1]))
                    run(nc.vector.scalar_tensor_tensor(out=small[:, 2:4], in0=small[:, 0:2], scalar=-1.0, in1=small[:, 0:2], op0=ALU.mult, op1=ALU.max))
                    for back in range(2):
                        c = 128 + t * 64 + row(hd, back)
                        run(nc.vector.tensor_tensor(small[:, 2 + back:3 + back], small[:, 2 + back:3 + back],
                                                    gcol[:, c:c + 1], ALU.max))
                    run(nc.vector.reciprocal(small[:, 4:6], small[:, 2:4]))
                    run(nc.vector.tensor_scalar(work[:, 9, :], work[:, 9, :], small[:, 5:6], None, ALU.mult))
                    nc.vector.scalar_tensor_tensor(out=work[:, 8, :], in0=work[:, 8, :], scalar=small[:, 4:5],
                                                   in1=work[:, 9, :], op0=ALU.mult, op1=ALU.add).then_inc(ml_prob.sem, 1)

                def split(i):
                    dve.wait_ge(ml_turned.sem, i + 1)
                    if i >= 1:
                        dve.wait_ge(ml_num.sem, i)
                    run(nc.vector.tensor_copy(mpt[0], ps(4)))
                    nc.vector.tensor_tensor(mpt[1], ps(4), mpt[0].bitcast(F32), ALU.subtract).then_inc(ml_split.sem, 1)

                def norm(i):
                    num = ps(5 + i % 2)[:, 0:256]
                    dve.wait_ge(ml_num.sem, i + 1)
                    run(nc.vector.bn_stats(small[:, 8:14], num))
                    nc.vector.bn_aggr(small[:, 18:20], small[:, 8:14]).then_inc(ml_var.sem, 1)
                    dve.wait_ge(ml_std.sem, i + 1)
                    run(nc.vector.reciprocal(small[:, 21:22], small[:, 20:21]))
                    if i >= 1:
                        dve.wait_ge(ml_hnt.sem, i)
                    nc.vector.tensor_scalar(tmp[:, 0, 0:256], num, small[:, 18:19], small[:, 21:22], ALU.subtract, ALU.mult)\
                        .then_inc(ml_hn.sem, 1)

                def gated(i):
                    hd, t = items[i]
                    dve.wait_ge(ml_hnt.sem, i + 1)
                    for b in range(2):
                        fb = hd * 2 + b
                        g = o_gate[:, fb, t * P:t * P + P]
                        last = nc.vector.scalar_tensor_tensor(out=g, in0=ps(7)[:, b * P:b * P + P], scalar=v("ml_norm_g", fb),
                                                              in1=g, op0=ALU.mult, op1=ALU.mult)
                        if b == 0:
                            run(last)
                    last.then_inc(ml_out.sem, 1)

                args(0)
                for i in range(n_items):
                    probs(i)
                    if i + 1 < n_items:
                        args(i + 1)
                    split(i)
                    if i >= 1:
                        gated(i - 1)
                    norm(i)
                gated(n_items - 1)

            stage(t0, t0, tensor, vector, scalar)

        lat = slice(0, SEQ)
        spare = slice(SEQ, TOK)
        g8 = work[:, 0:4, :].rearrange("p a b -> p (a b)").rearrange("p (k t) -> p k t", k=KD)
        r8 = work[:, 4:8, :].rearrange("p a b -> p (a b)").rearrange("p (k t) -> p k t", k=KD)
        i8 = work[:, 8:12, :].rearrange("p a b -> p (a b)").rearrange("p (k t) -> p k t", k=KD)
        t8 = tmp[:, :, :].rearrange("p a b -> p (a b)").rearrange("p (k t) -> p k t", k=KD)
        dq = [flat_hid[a][:, 0:KD * SEQ].rearrange("p (h t) -> p h t", h=KD) for a in range(2)]
        dk = [flat_hid[a][:, KD * SEQ:2 * KD * SEQ].rearrange("p (h t) -> p h t", h=KD) for a in range(2)]
        dv = [flat_hid[a][:, 2 * KD * SEQ:3 * KD * SEQ].rearrange("p (t c) -> p t c", t=2) for a in range(2)]
        neg_sp, neg_lam, sub_gain = small[:, 48:56], small[:, 40:41], small[:, 41:42]
        lru_conv, gelu_sq, gelu_in, gelu_act, gelu_out, gates_done, xc_split = (
            sig(n) for n in ("lru_conv", "gelu_sq", "gelu_in", "gelu_act", "gelu_out", "gates_done", "xc_split"))
        scal_a, scal_b, lam_sum = sig("scal_a"), sig("scal_b"), sig("lam_sum")

        def lru_in():
            t0, t1 = FIRST["lru_in"]
            rms = RmsNorm("g_mix")

            def tensor(pe):
                rms.pe(pe)
                pe.wait_ge(scal_a.sem, 1)
                pe.matmul(ps(0)[:, 0:2], ones_one[:, 0:P], small[:, 42:44], start=True, stop=True).then_inc(lam_sum.sem, 1)
                pe.wait_ge(scal_b.sem, 1)
                for u in range(8):
                    n = t0 + u
                    c_unit(pe, n, n % RING, [ps(u)[:, b * 256:b * 256 + 256] for b in range(2)], lat,
                           rms.ready(pe) if u == 0 else None)
                n = t0 + 8
                pe.wait_ge(lo_done, n + 1)
                for kb in range(KD):
                    pe.wait_ge(xc_split.sem, kb + 1)
                    if kb >= 4:
                        pe.wait_ge(gelu_out.sem, kb - 3)
                    for g in range(2):
                        at = slice((2 * kb + g) * P, (2 * kb + g) * P + P)
                        last = mm3(pe, ps(kb)[:, g * 256:g * 256 + 256], whi[:, n % RING, at], wlo[:, n % RING, at],
                                   xm[:, 0, kb, spare], xm[:, 1, kb, spare], True)
                last.then_inc(tile_used, 1)

            def scalar(act):
                run = linked(act, slink)
                rms.act(act)
                act.wait_ge(lam_sum.sem, 1)
                nc.scalar.activation(small[:, 44:46], ps(0)[:, 0:2], ACT.Exp).then_inc(scal_b.sem, 1)
                run(nc.scalar.activation(small[:, 24:32], small[:, 32:40], ACT.Exp, scale=-1.0))
                nc.scalar.activation(small[:, 24:32], small[:, 24:32], ACT.Ln, bias=eps[:, 2:3]).then_inc(scal_b.sem, 1)
                for u in range(8):
                    n = t0 + u
                    split_next(act, n, n % RING, (n + ADA_TILES) // RING)
                    if u >= 4:
                        j = u - 4
                        act.wait_ge(tile_used, n + 1)
                        if j >= 1:
                            act.wait_ge(gelu_out.sem, j)
                        nc.scalar.activation(work[:, 8, :], ps(u), ACT.Square).then_inc(gelu_sq.sem, 1)
                        act.wait_ge(gelu_in.sem, j + 1)
                        nc.scalar.activation(work[:, 9, :], work[:, 8, :], ACT.Tanh, scale=GELU_C).then_inc(gelu_act.sem, 1)
                n = t0 + 8
                split_next(act, n, n % RING, (n + ADA_TILES) // RING)
                act.wait_ge(tile_used, n + 1)
                act.wait_ge(gelu_out.sem, 4)
                for kb in range(KD):
                    nc.scalar.activation(r8[:, kb, :], ps(kb)[:, 0:256], ACT.Sigmoid, bias=v("b_rg", kb))
                    last = nc.scalar.activation(i8[:, kb, :], ps(kb)[:, 256:512], ACT.Sigmoid, bias=v("b_ig", kb))
                last.then_inc(gates_done.sem, 1)

            def vector(dve):
                run = linked(dve, vlink)
                lam = v("lam", 0, 4)
                run(nc.vector.tensor_tensor(small[:, 42:43], lam[:, 0:1], lam[:, 1:2], ALU.mult))
                run(nc.vector.tensor_tensor(small[:, 43:44], lam[:, 2:3], lam[:, 3:4], ALU.mult))
                lru_l = v("lru_lambda", 0, 8)
                nc.vector.scalar_tensor_tensor(out=small[:, 32:40], in0=lru_l, scalar=-1.0, in1=lru_l, op0=ALU.mult, op1=ALU.max).then_inc(scal_a.sem, 1)
                rms.dve(dve)
                dve.wait_ge(scal_b.sem, 2)
                run(nc.vector.tensor_tensor(small[:, 46:47], small[:, 45:46], small[:, 44:45], ALU.subtract))
                run(nc.vector.tensor_scalar(neg_lam, small[:, 46:47], -LAM_INIT, None, ALU.add))
                run(nc.vector.tensor_scalar(neg_sp, lru_l, -1.0, 0.0, ALU.mult, ALU.max))
                run(nc.vector.tensor_tensor(neg_sp, neg_sp, small[:, 24:32], ALU.add))
                run(nc.vector.tensor_scalar(neg_sp, neg_sp, -LRU_C, None, ALU.mult))
                run(nc.vector.tensor_scalar(sub_gain, v("g_subln"), 1.0 - LAM_INIT, None, ALU.mult))
                for u in range(4):
                    dve.wait_ge(tile_used, t0 + u + 1)
                    for blk in range(2):
                        fb = 2 * u + blk
                        y = h[:, fb, spare]
                        src = ps(u)[:, blk * 256:blk * 256 + 256]
                        run(nc.vector.tensor_scalar(y, src, v("w_conv", 3 * KD + fb), v("b_conv", fb), ALU.mult, ALU.add))
                        for d in range(1, 4):
                            run(nc.vector.scalar_tensor_tensor(out=y[:, d:], in0=src[:, 0:SEQ - d],
                                                               scalar=v("w_conv", (3 - d) * KD + fb), in1=y[:, d:],
                                                               op0=ALU.mult, op1=ALU.add))
                        run(nc.vector.tensor_copy(xm[:, 0, fb, spare], y))
                        nc.vector.tensor_tensor(xm[:, 1, fb, spare], y, xm[:, 0, fb, spare].bitcast(F32), ALU.subtract)\
                            .then_inc(xc_split.sem, 1)
                for j in range(4):
                    dve.wait_ge(gelu_sq.sem, j + 1)
                    run(nc.vector.tensor_scalar(work[:, 8, :], work[:, 8, :], 0.044715, 1.0, ALU.mult, ALU.add))
                    nc.vector.tensor_tensor(work[:, 8, :], work[:, 8, :], ps(4 + j), ALU.mult).then_inc(gelu_in.sem, 1)
                    dve.wait_ge(gelu_act.sem, j + 1)
                    nc.vector.scalar_tensor_tensor(out=work[:, j, :], in0=work[:, 9, :], scalar=1.0, in1=ps(4 + j),
                                                   op0=ALU.add, op1=ALU.mult).then_inc(gelu_out.sem, 1)
                dve.wait_ge(gates_done.sem, 1)

            stage(t0, t1, tensor, vector, scalar)

        qkv_evac, lru_tanh, lru_ratio, lru_sqrt, lru_prod = (sig(n) for n in ("qkv_evac", "lru_tanh", "lru_ratio", "lru_sqrt",
                                                                            "lru_prod"))

        def qkv():
            t0, t1 = FIRST["qkv"]

            def tensor(pe):
                for u in range(12):
                    n = t0 + u
                    if u >= 8:
                        pe.wait_ge(qkv_evac.sem, u - 7)
                    outs = [ps(u % 8)[:, b * 256:b * 256 + 256] for b in range(2)]
                    if u < 8:
                        c_unit(pe, n, n % RING, outs, lat)
                    else:
                        t_unit(pe, n, n % RING, outs, 2, False)

            def scalar(act):
                for kb in range(KD):
                    nc.scalar.activation(t8[:, kb, :], r8[:, kb, :], ACT.Tanh, scale=neg_sp[:, kb:kb + 1])\
                        .then_inc(lru_tanh.sem, 1)
                act.wait_ge(lru_tanh.sem, KD)
                for kb in range(KD):
                    nc.scalar.activation(r8[:, kb, :], r8[:, kb, :], ACT.Exp, scale=neg_sp[:, kb:kb + 1])\
                        .then_inc(lru_tanh.sem, 1)
                n = t0
                split_next(act, n, n % RING, (n + ADA_TILES) // RING)
                for kb in range(KD):
                    act.wait_ge(lru_ratio.sem, kb + 1)
                    nc.scalar.activation(t8[:, kb, :], t8[:, kb, :], ACT.Sqrt).then_inc(lru_sqrt.sem, 1)
                for n in range(t0 + 1, t1):
                    split_next(act, n, n % RING, (n + ADA_TILES) // RING)

            def vector(dve):
                run = linked(dve, vlink)

                def evacuate(u):
                    dve.wait_ge(tile_used, t0 + u + 1)
                    if u < 8:
                        dst = [(dq if u < 4 else dk)[a][:, 2 * (u % 4):2 * (u % 4) + 2, :] for a in range(2)]
                    else:
                        dst = [dv[a][:, :, (u - 8) * 256:(u - 8) * 256 + 256] for a in range(2)]
                    src = ps(u % 8).rearrange("p (a b) -> p a b", a=2)
                    run(nc.vector.tensor_copy(dst[0], src))
                    nc.vector.tensor_tensor(dst[1], src, dst[0].bitcast(F32), ALU.subtract).then_inc(qkv_evac.sem, 1)

                for kb in range(KD):
                    dve.wait_ge(lru_tanh.sem, KD + kb + 1)
                    run(nc.vector.tensor_scalar(ratio[:, :], t8[:, kb, :], -1.0, 1.0, ALU.mult, ALU.add))
                    run(nc.vector.reciprocal(ratio[:, :], ratio[:, :]))
                    nc.vector.scalar_tensor_tensor(out=t8[:, kb, :], in0=t8[:, kb, :], scalar=-2.0, in1=ratio[:, :],
                                                   op0=ALU.mult, op1=ALU.mult).then_inc(lru_ratio.sem, 1)
                    run(nc.vector.tensor_tensor(i8[:, kb, :], i8[:, kb, :], h[:, kb, spare], ALU.mult))
                for kb in range(KD):
                    dve.wait_ge(lru_sqrt.sem, kb + 1)
                    run(nc.vector.tensor_tensor(i8[:, kb, :], i8[:, kb, :], t8[:, kb, :], ALU.mult))
                    run(nc.vector.tensor_tensor_scan(t8[:, kb, :], r8[:, kb, :], i8[:, kb, :], 0.0, ALU.mult, ALU.add))
                    run(nc.vector.scalar_tensor_tensor(out=g8[:, kb, :], in0=t8[:, kb, :], scalar=0.5, in1=g8[:, kb, :],
                                                       op0=ALU.mult, op1=ALU.mult))
                    evacuate(kb)
                for u in range(KD, 12):
                    evacuate(u)

            stage(t0, t1, tensor, vector, scalar)

        df = {n: sig(n) for n in ("df_scores", "df_max", "df_exp", "df_prob", "df_turned", "df_split", "df_pv", "df_sq",
                                  "df_ms", "df_std", "df_out", "ab_done")}

        def diff_attention():
            t0, t1 = FIRST["gates_ab"]
            s = {n: x.sem for n, x in df.items()}
            pt = [xm[:, a, 0:2, spare] for a in range(2)]

            def tensor(pe):
                def scores(i):
                    if i >= 2:
                        pe.wait_ge(s["df_max"], i - 1)
                    for q in range(2):
                        at = slice(q * P, q * P + P)
                        for c in range(2):
                            r = slice(c * 64, c * 64 + 64)
                            last = mm3(pe, ps(2 * (i % 2) + c)[:, q * 256:q * 256 + 256], dq[0][r, i, at], dq[1][r, i, at],
                                       dk[0][r, i, :], dk[1][r, i, :], True)
                    last.then_inc(s["df_scores"], 1)

                def mean_square(i):
                    pe.wait_ge(s["df_sq"], i + 1)
                    if i >= 1:
                        pe.wait_ge(s["df_std"], i)
                    pe.matmul(ps(6)[:, 0:256], ones_one[:, 0:P], sq_buf[:, :], start=True, stop=True)\
                        .then_inc(s["df_ms"], 1)

                scores(0)
                for i in range(8):
                    if i < 7:
                        scores(i + 1)
                    n = t0 + i
                    if i >= 1:
                        pe.wait_ge(s["ab_done"], i)
                    c_unit(pe, n, n % RING, [ps(7)[:, b * 256:b * 256 + 256] for b in range(2)], lat)
                    pe.wait_ge(s["df_prob"], i + 1)
                    if i >= 1:
                        pe.wait_ge(s["df_split"], i)
                    for b in range(2):
                        for q in range(2):
                            last = pe.transpose(ps(4)[:, b * 256 + q * P:b * 256 + q * P + P],
                                                dsm(i)[:, q, 0, b * P:b * P + P], ident)
                    last.then_inc(s["df_turned"], 1)
                    if i >= 1:
                        mean_square(i - 1)
                        pe.wait_ge(s["df_out"], i)
                    pe.wait_ge(s["df_split"], i + 1)
                    for b in range(2):
                        last = mm3(pe, ps(5)[:, 0:256], dv[0][:, b, i * P:i * P + P], dv[1][:, b, i * P:i * P + P],
                                   pt[0][:, b, :], pt[1][:, b, :], b == 0)
                    last.then_inc(s["df_pv"], 1)
                mean_square(7)

            def dsm(i):
                return tmp[:, 2 * (i % 2):2 * (i % 2) + 2, :].rearrange("p c (q k) -> p q c k", q=2)

            def scalar(act):
                def exps(i):
                    act.wait_ge(s["df_max"], i + 1)
                    for q in range(2):
                        for c in range(2):
                            j = 2 * q + c
                            nc.scalar.activation(dsm(i)[:, q, c, :], dsm(i)[:, q, c, :], ACT.Exp,
                                                 bias=small[:, 8 + j:9 + j], scale=DIFF_SCALE,
                                                 accum_out=small[:, 12 + j:13 + j]).then_inc(s["df_exp"], 1)

                exps(0)
                for i in range(8):
                    n = t0 + i
                    split_next(act, n, n % RING, (n + ADA_TILES) // RING)
                    act.wait_ge(tile_used, n + 1)
                    dst = (r8 if i < 4 else i8)[:, 2 * (i % 4):2 * (i % 4) + 2, :]
                    nc.scalar.activation(dst, ps(7).rearrange("p (a b) -> p a b", a=2), ACT.Sigmoid).then_inc(s["ab_done"], 1)
                    if i < 7:
                        exps(i + 1)
                    if i >= 1:
                        root(act, i - 1)
                    act.wait_ge(s["df_pv"], i + 1)
                    nc.scalar.activation(sq_buf[:, :], ps(5)[:, 0:256], ACT.Square).then_inc(s["df_sq"], 1)
                root(act, 7)

            def root(act, i):
                act.wait_ge(s["df_ms"], i + 1)
                nc.scalar.activation(sq_buf[:, :], ps(6)[:, 0:256], ACT.Sqrt, bias=eps[:, 0:1], scale=1.0 / P).then_inc(s["df_std"], 1)

            def vector(dve):
                run = linked(dve, vlink)

                def front(i):
                    m = dsm(i)
                    dve.wait_ge(s["df_scores"], i + 1)
                    run(nc.vector.tensor_copy(tmp[:, 2 * (i % 2):2 * (i % 2) + 2, :], pair(i % 2)[:, :, :]))
                    for q in range(2):
                        for c in range(2):
                            own = m[:, q, c, q * P:q * P + P]
                            run(nc.vector.tensor_tensor(own, own, cst("tri_f", 128), ALU.add))
                    run(nc.vector.memset(m[:, 0, :, P:2 * P], MASKED))
                    run(nc.vector.tensor_reduce(small[:, 4:8].rearrange("p (q c) -> p q c", q=2), m, AX_X, ALU.max))
                    nc.vector.tensor_scalar(small[:, 8:12], small[:, 4:8], -DIFF_SCALE, None, ALU.mult)\
                        .then_inc(s["df_max"], 1)

                def output(i):
                    dve.wait_ge(s["df_std"], i + 1)
                    run(nc.vector.reciprocal(ratio[:, :], sq_buf[:, :]))
                    nc.vector.scalar_tensor_tensor(out=h[:, i, spare], in0=ps(5)[:, 0:256], scalar=sub_gain,
                                                   in1=ratio[:, :], op0=ALU.mult, op1=ALU.mult).then_inc(s["df_out"], 1)

                front(0)
                for i in range(8):
                    m = dsm(i)
                    dve.wait_ge(s["df_exp"], 4 * i + 4)
                    run(nc.vector.reciprocal(small[:, 16:20], small[:, 12:16]))
                    for q in range(2):
                        j = 16 + 2 * q
                        run(nc.vector.tensor_tensor(small[:, j + 1:j + 2], small[:, j + 1:j + 2], neg_lam, ALU.mult))
                        run(nc.vector.tensor_scalar(m[:, q, 1, :], m[:, q, 1, :], small[:, j + 1:j + 2], None, ALU.mult))
                        last = nc.vector.scalar_tensor_tensor(out=m[:, q, 0, :], in0=m[:, q, 0, :], scalar=small[:, j:j + 1],
                                                              in1=m[:, q, 1, :], op0=ALU.mult, op1=ALU.add)
                        if q == 0:
                            run(last)
                    last.then_inc(s["df_prob"], 1)
                    if i < 7:
                        front(i + 1)
                    dve.wait_ge(s["df_turned"], i + 1)
                    if i >= 1:
                        output(i - 1)
                    src = ps(4).rearrange("p (a b) -> p a b", a=2)
                    run(nc.vector.tensor_copy(pt[0], src))
                    nc.vector.tensor_tensor(pt[1], src, pt[0].bitcast(F32), ALU.subtract).then_inc(s["df_split"], 1)
                output(7)

            stage(t0, t1, tensor, vector, scalar)

        dx_out, mix_half, mix_in = (sig(n) for n in ("dx_out", "mix_half", "mix_in"))

        def mix():
            t0 = FIRST["lru_br"][0]
            t1 = FIRST["w_out"][1]
            rs = Residual(t1, None, 0, SEQ)
            b_d = d_block.take(2 * (KD - 1)) if False else None
            low = [ps(ko // 2)[:, ko % 2 * SEQ:ko % 2 * SEQ + SEQ] for ko in range(KD)]
            high = d_outs(SEQ)

            def tensor(pe):
                for d in range(4):
                    n = t0 + d
                    pe.wait_ge(dx_out.sem, 2 * d + 2)
                    d_unit(pe, n, n % RING, high, lambda kk, j=d: (xm[:, 0, 2 * j + kk, lat], xm[:, 1, 2 * j + kk, lat]), d == 0)
                for d in range(4):
                    n = t0 + 4 + d
                    pe.wait_ge(dx_out.sem, KD + 2 * d + 2)
                    d_unit(pe, n, n % RING, low, lambda kk, j=d: (xm[:, 0, 2 * j + kk, spare], xm[:, 1, 2 * j + kk, spare]), d == 0)
                for d in range(4):
                    n = t0 + 8 + d
                    pe.wait_ge(mix_in.sem, 2 * d + 2)
                    d_unit(pe, n, n % RING, high, lambda kk, j=d: (xm[:, 0, 2 * j + kk, lat], xm[:, 1, 2 * j + kk, lat]), d == 0,
                           d_block if d == 3 else None)

            def scalar(act):
                plain_splits(act, t0, t1)

            def vector(dve):
                run = linked(dve, vlink)
                for cols, src in ((lat, lambda k: g8[:, k, :]), (spare, lambda k: h[:, k, spare])):
                    for k in range(KD):
                        run(nc.vector.tensor_copy(xm[:, 0, k, cols], src(k)))
                        nc.vector.tensor_tensor(xm[:, 1, k, cols], src(k), xm[:, 0, k, cols].bitcast(F32), ALU.subtract)\
                            .then_inc(dx_out.sem, 1)
                dve.wait_ge(tile_used, t0 + 4)
                for k in range(KD):
                    run(nc.vector.tensor_tensor(i8[:, k, :], i8[:, k, :], high[k], ALU.mult))
                dve.wait_ge(tile_used, t0 + 8)
                for k in range(KD):
                    run(nc.vector.tensor_tensor(r8[:, k, :], r8[:, k, :], low[k], ALU.mult))
                    run(nc.vector.tensor_tensor(r8[:, k, :], r8[:, k, :], i8[:, k, :], ALU.add))
                    run(nc.vector.tensor_copy(xm[:, 0, k, lat], r8[:, k, :]))
                    nc.vector.tensor_tensor(xm[:, 1, k, lat], r8[:, k, :], xm[:, 0, k, lat].bitcast(F32), ALU.subtract)\
                        .then_inc(mix_in.sem, 1)
                rs.dve(dve)

            stage(t0, t1, tensor, vector, scalar)

        route = work[:, 8, 0:128].rearrange("p (t c) -> p t c", t=2)
        comb = work[:, 8, 128:192].rearrange("p (t c) -> p t c", t=2)
        comb_t, comb_e = work[0:EXPERTS, 9, 0:256], work[0:EXPERTS, 9, 256:512]
        rt_max, rt_exp, rt_comb, rt_turned = sig("rt_max"), sig("rt_exp"), sig("rt_comb"), sig("rt_turned")

        def router():
            t0, t1 = FIRST["router"]
            rms = RmsNorm("g_moe")

            def tensor(pe):
                rms.pe(pe)
                pe.wait_ge(xm_r.sem, rms.x + KD)
                t_unit(pe, t0, t0 % RING, [ps(2)[:, 0:256], ps(2)[:, 256:512]], 2, False)
                pe.wait_ge(rt_comb.sem, 1)
                for t in range(2):
                    last = pe.transpose(ps(3)[0:EXPERTS, t * P:t * P + P], comb[:, t, :], ident)
                last.then_inc(rt_turned.sem, 1)

            def scalar(act):
                rms.act(act)
                split_next(act, t0, t0 % RING, (t0 + ADA_TILES) // RING)
                for t in range(2):
                    a = small[:, 20 * t:20 * t + 20]
                    act.wait_ge(rt_max.sem, 2 * t + 1)
                    nc.scalar.activation(a[:, 12:16], route[:, t, 0:4], ACT.Exp, bias=a[:, 8:9], accum_out=a[:, 9:10])\
                        .then_inc(rt_exp.sem, 1)
                    act.wait_ge(rt_max.sem, 2 * t + 2)
                    nc.scalar.activation(a[:, 10:11], a[:, 1:2], ACT.Exp, bias=a[:, 8:9]).then_inc(rt_exp.sem, 1)

            def vector(dve):
                run = linked(dve, vlink)
                rms.dve(dve)
                dve.wait_ge(tile_used, t1)
                for t in range(2):
                    a, r, iota = small[:, 20 * t:20 * t + 20], route[:, t, :], cst("iota", 8)
                    idx_f = a[:, 16:18]
                    idx = r[:, 56:64].bitcast(U32)
                    run(nc.vector.tensor_tensor(r[:, 0:36], ps(2)[:, t * 256:t * 256 + 36], v("b_rt", 0, 36), ALU.add))
                    run(nc.vector.memset(r[:, 40:48], MASKED))
                    run(nc.vector.tensor_copy(r[:, 40:44], r[:, 0:4]))
                    run(nc.vector.max(a[:, 0:8], r[:, 40:48]))
                    run(nc.vector.max_index(idx, a[:, 0:8], r[:, 40:48]))
                    run(nc.vector.tensor_copy(idx_f[:, 0:1], idx[:, 0:1]))
                    run(nc.vector.tensor_scalar(r[:, 48:56], iota, idx_f[:, 0:1], None, ALU.is_equal))
                    nc.vector.tensor_scalar(a[:, 8:9], a[:, 0:1], -1.0, None, ALU.mult).then_inc(rt_max.sem, 1)
                    dve.wait_ge(rt_exp.sem, 2 * t + 1)
                    run(nc.vector.tensor_scalar(r[:, 40:48], r[:, 4:12], r[:, 48:49], None, ALU.mult))
                    for g in range(1, GROUPS):
                        run(nc.vector.scalar_tensor_tensor(out=r[:, 40:48], in0=r[:, 4 + 8 * g:12 + 8 * g],
                                                           scalar=r[:, 48 + g:49 + g], in1=r[:, 40:48],
                                                           op0=ALU.mult, op1=ALU.add))
                    run(nc.vector.max(a[:, 0:8], r[:, 40:48]))
                    run(nc.vector.max_index(idx, a[:, 0:8], r[:, 40:48]))
                    run(nc.vector.tensor_copy(idx_f, idx[:, 0:2]))
                    nc.vector.tensor_scalar(a[:, 8:9], a[:, 0:1], -1.0, None, ALU.mult).then_inc(rt_max.sem, 1)
                    dve.wait_ge(rt_exp.sem, 2 * t + 2)
                    run(nc.vector.tensor_scalar(a[:, 11:12], a[:, 10:11], 1.0, None, ALU.add))
                    run(nc.vector.tensor_tensor(a[:, 11:12], a[:, 11:12], a[:, 9:10], ALU.mult))
                    run(nc.vector.reciprocal(a[:, 12:13], a[:, 11:12]))
                    run(nc.vector.tensor_tensor(a[:, 13:14], a[:, 12:13], a[:, 10:11], ALU.mult))
                    run(nc.vector.tensor_scalar(r[:, 40:48], iota, idx_f[:, 0:1], a[:, 12:13], ALU.is_equal, ALU.mult))
                    run(nc.vector.tensor_scalar(r[:, 4:12], iota, idx_f[:, 1:2], a[:, 13:14], ALU.is_equal, ALU.mult))
                    run(nc.vector.tensor_tensor(r[:, 40:48], r[:, 40:48], r[:, 4:12], ALU.add))
                    for g in range(GROUPS):
                        last = nc.vector.tensor_scalar(comb[:, t, 8 * g:8 * g + 8], r[:, 40:48], r[:, 48 + g:49 + g], None,
                                                       ALU.mult)
                        if not (t == 1 and g == GROUPS - 1):
                            run(last)
                last.then_inc(rt_comb.sem, 1)
                dve.wait_ge(rt_turned.sem, 1)
                run(nc.vector.tensor_copy(comb_t, ps(3)[0:EXPERTS, 0:256]))

            stage(t0, t1, tensor, vector, scalar)

        ex_weight, ex_spread, ex_gate, ex_f, ex_h, ex_r, acc_clear = (
            sig(n) for n in ("ex_weight", "ex_spread", "ex_gate", "ex_f", "ex_h", "ex_r", "acc_clear"))
        ex_scaled = sig("ex_scaled")

        def experts():
            t0, t1 = FIRST["experts"]
            rs = Residual(t1, None, 0, SEQ)
            outs = d_outs(SEQ)
            eh = [flat_hid[a][:, 0:8 * SEQ].rearrange("p (b k t) -> p b k t", b=2, k=4) for a in range(2)]

            def up_tile(e, j):
                return t0 + j if isinstance(e, int) and e == 0 else e * 6 + (t0 - 2 + j)

            def down_tile(e, j):
                return e * 6 + (t0 + 8 + j) if not (isinstance(e, int) and e == EXPERTS - 1) else t1 - 2 + j

            def up_slot(first, j):
                return (t0 + j) % RING if first else (t0 - 2 + j) % RING

            def down_slot(last, j):
                return (t1 - 2 + j) % RING if last else (t0 + 8 + j) % RING

            def turn(n_expr_base, e):
                return e * 2 + (n_expr_base + ADA_TILES) // RING

            def over_experts(eng, up, down):
                up(0, 0)
                with eng.Fori(0, (EXPERTS - 2) // 2) as i:
                    for b in (1, 0):
                        e = i * 2 + (1 if b else 2)
                        up(e, b)
                        down(i * 2 + (0 if b else 1), 1 - b)
                up(EXPERTS - 1, 1)
                down(EXPERTS - 2, 0)
                down(EXPERTS - 1, 1)

            def tensor(pe):
                def up(e, b):
                    first = isinstance(e, int) and e == 0
                    pe.wait_ge(ex_weight.sem, e + 1)
                    if not first:
                        pe.wait_ge(ex_r.sem, e * 4)
                    pe.matmul(ps(3)[:, lat], ones_one[0:EXPERTS, 0:P], comb_e, start=True, stop=True)\
                        .then_inc(ex_spread.sem, 1)
                    for j in range(4):
                        slot = up_slot(first, j)
                        if not (first and j < RING):
                            pe.wait_ge(ex_f.sem, e * 4 + (j - RING + 1))
                        c_unit(pe, up_tile(e, j), slot, [ps(bank_of(j, b))[:, c * 256:c * 256 + 256] for c in range(2)], lat)

                def down(e, b):
                    last = isinstance(e, int) and e == EXPERTS - 1
                    pe.wait_ge(ex_r.sem, e * 4 + 4)
                    for j in range(2):
                        d_unit(pe, down_tile(e, j), down_slot(last, j), outs,
                               lambda kk: (eh[0][:, b, 2 * j + kk, :], eh[1][:, b, 2 * j + kk, :]), False,
                               d_block if last and j == 1 else None)
                pe.wait_ge(acc_clear.sem, 1)
                over_experts(pe, up, down)

            def bank_of(j, b):
                return j % RING

            def scalar(act):
                def up(e, b):
                    first = isinstance(e, int) and e == 0
                    for j in range(4):
                        n = up_tile(e, j)
                        base = t0 + j if first else t0 - 2 + j
                        split_next(act, n, base % RING, turn(base, e))
                        act.wait_ge(tile_used, n + 1)
                        if not (first and j < 2):
                            act.wait_ge(ex_scaled.sem, e * 4 + (j - 1))
                        nc.scalar.activation(work[:, j % 2, lat], ps(bank_of(j, b))[:, lat], ACT.Silu)\
                            .then_inc(ex_gate.sem, 1)

                def down(e, b):
                    last = isinstance(e, int) and e == EXPERTS - 1
                    for j in range(2):
                        n = down_tile(e, j)
                        if last:
                            split_next(act, n, n % RING, (n + ADA_TILES) // RING)
                        else:
                            base = t0 + 8 + j
                            split_next(act, n, base % RING, turn(base, e))
                over_experts(act, up, down)

            def vector(dve):
                for b in range(4):
                    last = nc.vector.memset(ps(4 + b), 0.0)
                last.then_inc(acc_clear.sem, 1)

                def weigh(e):
                    nc.vector.tensor_scalar(comb_e, comb_t, ident[0:EXPERTS, e:e + 1] if isinstance(e, int)
                                            else const[0:EXPERTS, bass.ds(e, 1)], None, ALU.mult).then_inc(ex_weight.sem, 1)

                def up(e, b):
                    for j in range(4):
                        bk = ps(bank_of(j, b))
                        if j == 0:
                            dve.wait_ge(ex_spread.sem, e + 1)
                        dve.wait_ge(ex_gate.sem, e * 4 + (j + 1))
                        nc.vector.tensor_tensor(work[:, 2 + j % 2, lat], work[:, j % 2, lat], ps(3)[:, lat], ALU.mult)\
                            .then_inc(ex_scaled.sem, 1)
                        dve.wait_ge(ex_scaled.sem, e * 4 + (j + 1))
                        nc.vector.tensor_tensor(work[:, 4 + j % 2, lat], work[:, 2 + j % 2, lat], bk[:, 256:512], ALU.mult)\
                            .then_inc(ex_f.sem, 1)
                        dve.wait_ge(ex_f.sem, e * 4 + (j + 1))
                        nc.vector.tensor_copy(eh[0][:, b, j, :], work[:, 4 + j % 2, lat]).then_inc(ex_h.sem, 1)
                        dve.wait_ge(ex_h.sem, e * 4 + (j + 1))
                        nc.vector.tensor_tensor(eh[1][:, b, j, :], work[:, 4 + j % 2, lat], eh[0][:, b, j, :].bitcast(F32),
                                                ALU.subtract).then_inc(ex_r.sem, 1)
                        if j == 0 and not (isinstance(e, int) and e == EXPERTS - 1):
                            weigh(e + 1)
                weigh(0)
                up(0, 0)
                with dve.Fori(0, (EXPERTS - 2) // 2) as i:
                    for b in (1, 0):
                        up(i * 2 + (1 if b else 2), b)
                up(EXPERTS - 1, 1)
                rs.dve(dve)

            stage(t0, t1, tensor, vector, scalar)

        p_in, p_split, ple_gate, ple_mul = sig("p_in"), sig("p_split"), sig("ple_gate"), sig("ple_mul")
        out_ready, out_sent = sig("out_ready"), sig("out_sent")
        x_sq = sig("x_sq")

        def ple():
            t0, t1 = FIRST["ple"]
            rms = RmsNorm("g_ple")
            b_res = res.take(KD)
            outs = d_outs(SEQ)
            p_raw = work[:, 10, :].rearrange("p (k t) -> p k t", k=2)

            def tensor(pe):
                pe.wait_ge(p_split.sem, 1)
                d_unit(pe, t0, t0 % RING, outs, lambda kk: (xm[:, 0, kk, spare], xm[:, 1, kk, spare]), True)
                rms.pe(pe)
                for u in range(4):
                    n = t0 + 1 + u
                    c_unit(pe, n, n % RING, [ps(u)[:, b * 256:b * 256 + 256] for b in range(2)], lat,
                           rms.ready(pe) if u == 0 else None)

            def scalar(act):
                act.dma_start(p_raw, p_d).then_inc(p_in.sem, 16)
                split_next(act, t0, t0 % RING, (t0 + ADA_TILES) // RING)
                rms.act(act)
                for u in range(4):
                    n = t0 + 1 + u
                    split_next(act, n, n % RING, (n + ADA_TILES) // RING)
                    act.wait_ge(tile_used, n + 1)
                    nc.scalar.activation(g8[:, 2 * u:2 * u + 2, :],
                                         ps(u).rearrange("p (a b) -> p a b", a=2), ACT.Sigmoid).then_inc(ple_gate.sem, 1)

            def vector(dve):
                run = linked(dve, vlink)
                dve.wait_ge(p_in.sem, 16)
                run(nc.vector.tensor_copy(xm[:, 0, 0:2, spare], p_raw))
                nc.vector.tensor_tensor(xm[:, 1, 0:2, spare], p_raw, xm[:, 0, 0:2, spare].bitcast(F32), ALU.subtract)\
                    .then_inc(p_split.sem, 1)
                rms.dve(dve)
                for k in range(KD):
                    if k % 2 == 0:
                        dve.wait_ge(ple_gate.sem, k // 2 + 1)
                    run(nc.vector.tensor_tensor(g8[:, k, :], g8[:, k, :], outs[k], ALU.mult))
                    nc.vector.tensor_tensor(h[:, k, lat], h[:, k, lat], g8[:, k, :], ALU.add).then_inc(res.sem, 1)

            stage(t0, t1, tensor, vector, scalar)

        def last_norm():
            rms = RmsNorm("g_final")

            def scalar(act):
                rms.act(act)
                act.wait_ge(out_ready.sem, 1)
                act.dma_start(out_d, work[:, 0:KD, lat]).then_inc(out_sent.sem, 16)
                act.wait_ge(out_sent.sem, 16)

            def vector(dve):
                rms.dve(dve, split=False)
                nc.vector.tensor_copy(small[:, 0:1], small[:, 1:2]).then_inc(out_ready.sem, 1)

            stage(TILES, TILES, rms.pe, vector, scalar)

        ffn("ffn00", 0, 0, TOK)
        attention_in()
        attention_core()
        project("att_out", 0, 5, TOK, 1, lambda k: work[:, 4 + k, :])
        ffn("ffn01", 0, 1, TOK)
        ffn("ffn10", 1, 0, TOK)
        mlstm_in()
        mlstm_core()
        project("ml_out", 1, 5, SEQ, 4, lambda k: o_gate[:, k, :])
        ffn("ffn11", 1, 1, SEQ)
        lru_in()
        qkv()
        diff_attention()
        mix()
        router()
        experts()
        ple()
        last_norm()


def column_tile(w, cols):
    return w[:, cols].reshape(KD, P, 256).transpose(1, 0, 2).reshape(P, TILE)


def row_tile(w, r):
    return w[r * 256:r * 256 + 256].reshape(2, P, D).transpose(1, 0, 2).reshape(P, TILE)


def pack_stream(a):
    out = np.zeros((ADA_TILES + TILES, P, TILE), np.float32)
    n = 0

    def add(tile):
        nonlocal n
        out[n] = tile
        n += 1

    def columns(w, first=0, count=None):
        for c in range(first, first + (count or w.shape[1] // 256)):
            add(column_tile(w, slice(c * 256, c * 256 + 256)))

    def rows(w):
        for r in range(w.shape[0] // 256):
            add(row_tile(w, r))

    def gate_up(w_gate, w_up, j):
        at = slice(j * P, j * P + P)
        add(column_tile(np.concatenate([w_gate[:, at], w_up[:, at]], axis=1), slice(0, 256)))

    def ffn(w_in, w_out):
        for first, count in ((0, HALF_A), (HALF_A, HALF_B)):
            for j in range(first, first + count):
                gate_up(w_in[:, :FF], w_in[:, FF:], j)
            for r in range(first // 2, (first + count) // 2):
                add(row_tile(w_out, r))

    for layer in range(2):
        columns(a["ada_w"][layer])
    ffn(a["ffn_w_in"][0, 0], a["ffn_w_out"][0, 0])
    columns(a["att_w_in"][0])
    rows(a["att_w_out"][0])
    ffn(a["ffn_w_in"][0, 1], a["ffn_w_out"][0, 1])
    ffn(a["ffn_w_in"][1, 0], a["ffn_w_out"][1, 0])
    w = a["ml_w_in"][0]
    gates = np.zeros((D, 256), np.float32)
    gates[:, 0:4], gates[:, 32:36] = w[:, 3072:3076], w[:, 3080:3084]
    gates[:, 128:132], gates[:, 160:164] = w[:, 3076:3080], w[:, 3084:3088]
    columns(gates)
    columns(w, 2, 2)
    columns(w, 0, 2)
    columns(w, 4, 4)
    columns(w, 8, 4)
    rows(a["ml_w_out"][0])
    ffn(a["ffn_w_in"][1, 1], a["ffn_w_out"][1, 1])
    w = a["w_in_2"][0]
    columns(w, 12, 4)
    columns(w, 16, 4)
    block = np.zeros((P, KD, 2, P), np.float32)
    for g, name in enumerate(("w_rg_2", "w_ig_2")):
        for b in range(16):
            at = slice(b % 2 * 64, b % 2 * 64 + 64)
            block[at, b // 2, g, at] = a[name][0, b]
    add(block.reshape(P, TILE))
    columns(w, 0, 4)
    columns(w, 4, 4)
    columns(w, 8, 4)
    columns(w, 20, 8)
    rows(a["w_lru_br_2"][0])
    rows(a["w_attn_br_2"][0])
    rows(a["w_out_2"][0])
    router = np.zeros((D, 256), np.float32)
    router[:, 0:GROUPS] = a["w_rt_group_2"][0]
    router[:, GROUPS:GROUPS + EXPERTS] = a["w_rt_expert_2"][0].transpose(1, 0, 2).reshape(D, EXPERTS)
    columns(router)
    wg, wu, wd = a["w_e_gate_2"][0], a["w_e_up_2"][0], a["w_e_down_2"][0]
    for e in range(EXPERTS + 1):
        if e < EXPERTS:
            for j in range(4):
                gate_up(wg[e], wu[e], j)
        if e >= 1:
            rows(wd[e - 1])
    rows(a["w_ple_proj_2"][0])
    columns(a["w_ple_gate_2"][0])
    assert n == ADA_TILES + TILES
    return out


def pack_vectors(a):
    def blocks(x):
        return np.asarray(x).reshape(-1, P).T

    def gates(x):
        out = np.zeros((P, 2), np.float32)
        out[0:4, 0], out[32:36, 0] = x[0:4], x[8:12]
        out[0:4, 1], out[32:36, 1] = x[4:8], x[12:16]
        return out

    lam = np.zeros((P, 4), np.float32)
    for i, name in enumerate(("lam_q1_2", "lam_k1_2", "lam_q2_2", "lam_k2_2")):
        lam[0:64, i] = a[name][0]
    parts = {
        "c": np.stack([a["c"][0], a["c_ctx"]], 1).reshape(KD, P, 2).transpose(1, 0, 2).reshape(P, 16),
        "ada_b": blocks(a["ada_b"]), "ln_g": blocks(a["ln_g"]), "ln_b": blocks(a["ln_b"]),
        "q_gain": blocks(a["att_q_gain"]), "k_gain": blocks(a["att_k_gain"]),
        "ml_conv_w": blocks(a["ml_conv_w"]), "ml_conv_b": blocks(a["ml_conv_b"]), "ml_norm_g": blocks(a["ml_norm_g"]),
        "gate_b": gates(a["ml_gate_b"][0]),
        "g_mix": blocks(a["g_mix_2"]), "g_moe": blocks(a["g_moe_2"]), "g_ple": blocks(a["g_ple_2"]),
        "g_final": blocks(a["g_final_2"]), "g_subln": blocks(a["g_subln_2"]),
        "w_conv": blocks(a["w_conv_2"]), "b_conv": blocks(a["b_conv_2"]), "b_rg": blocks(a["b_rg_2"]),
        "b_ig": blocks(a["b_ig_2"]), "lru_lambda": blocks(a["lru_lambda_2"]), "lam": lam,
        "b_rt": np.tile(np.concatenate([a["b_rt_group_2"].reshape(-1), a["b_rt_expert_2"].reshape(-1)]), (P, 1)),
    }
    return np.ascontiguousarray(np.concatenate([parts[name] for name, _ in VECTORS], axis=1))


def pack_constants():
    i = np.arange(P)
    inv = (np.float32(10000.0) ** (-np.arange(32, dtype=np.float32) / np.float32(32))).astype(np.float32)
    t = np.arange(SEQ)
    ang = np.where((i < 64)[:, None], (t // 64)[None, :], (t % 64)[None, :]).astype(np.float32) * inv[i % 32][:, None]
    sign = np.where(i % 64 < 32, -1.0, 1.0)[:, None]
    select = np.zeros((P, 8, P), np.float32)
    for hd in range(4):
        select[hd, hd], select[32 + hd, 4 + hd] = 1.0, 1.0
    parts = {
        "ident": np.eye(P), "tri_f": np.where(i[None, :] <= i[:, None], 0.0, MASKED),
        "tri_b": np.where(i[None, :] >= i[:, None], 0.0, MASKED), "iota": np.tile(np.arange(8.0), (P, 1)),
        "cos": np.cos(ang), "sin": sign * np.sin(ang), "swap": np.eye(P)[i ^ 32], "select": select.reshape(P, -1),
    }
    return np.ascontiguousarray(np.concatenate([parts[name] for name, _ in CONSTS], axis=1).astype(np.float32))


def kernel(**inputs):
    import concourse.bacc as bacc
    from concourse.bass_utils import run_bass_kernel_spmd

    a = {name: np.asarray(x) for name, x in inputs.items()}
    arrays = {
        "stream": pack_stream(a),
        "vectors": pack_vectors(a),
        "constants": pack_constants(),
        "x_t": np.ascontiguousarray(np.concatenate([a["x"][0], a["ctx"][0]]).T.reshape(KD, P, TOK).transpose(1, 0, 2)),
        "p_t": np.ascontiguousarray(a["p_2"][0, 0].T.reshape(2, P, SEQ).transpose(1, 0, 2)),
    }
    nc = bacc.Bacc("TRN2", target_bir_lowering=False, num_devices=1)
    args = [nc.dram_tensor(name, x.shape, F32, kind="ExternalInput").ap() for name, x in arrays.items()]
    ada_rows = nc.dram_tensor("ada_rows", (2, 2 * N_MOD * D), F32, kind="Internal").ap()
    out = nc.dram_tensor("out", (P, KD, SEQ), F32, kind="ExternalOutput").ap()
    program(nc, *args, ada_rows, out)
    r = run_bass_kernel_spmd(nc, [arrays], core_ids=[0])
    y = r.results[0]["out"]
    return np.ascontiguousarray(y.transpose(1, 0, 2).reshape(D, SEQ).T).reshape(1, SEQ, D)
```

```python
from contextlib import ExitStack

import numpy as np

import concourse.bass as bass
from concourse import mybir

P = 128
D = 1024
KD = D // P
SEQ = 256
CTX = 256
TOK = SEQ + CTX
FF = 2816
FFB = FF // P
HALF_A, HALF_B = 12, 10
TILE = 2048
RING = 3
N_MOD = 9
ADA_GROUP = 12
ADA_TILES = 2 * ADA_GROUP
LATE_GROUPS = 4
EXPERTS, GROUPS, PER_GROUP, EFF = 32, 4, 8, 512
FEW = 128
FFN_TILES = FFB + FFB // 2
ALPHA = (2.0 * 2) ** 0.25
LN_EPS, RMS_EPS, SUBLN_EPS = 1e-5, 1e-6, 1e-5
ATT_SCALE = 128 ** -0.5
ML_SCALE = 128 ** -0.5
DIFF_SCALE = 64 ** -0.5
LAM_INIT = 0.8 - 0.6
LRU_C = 8.0
MASKED = -1e30
GELU_C = (2.0 / np.pi) ** 0.5

PLAN = [
    ("ffn00", FFN_TILES), ("att_in", 6 + ADA_GROUP), ("att_core", 2 * ADA_GROUP), ("att_out", 4), ("ffn01", FFN_TILES),
    ("ffn10", FFN_TILES), ("ml_in", 13), ("ml_core", ADA_GROUP), ("ml_out", 4), ("ffn11", FFN_TILES),
    ("lru_in", 9), ("qkv", 12), ("gates_ab", 8), ("lru_br", 4), ("attn_br", 4), ("w_out", 4),
    ("router", 1), ("experts", EXPERTS * 6), ("ple", 5),
]
FIRST = {}
_n = 0
for _name, _count in PLAN:
    FIRST[_name] = (_n, _n + _count)
    _n += _count
TILES = _n

VECTORS = [
    ("c", 16), ("ada_b", 144), ("ln_g", 48), ("ln_b", 48), ("q_gain", 1), ("k_gain", 1),
    ("ml_conv_w", 24), ("ml_conv_b", 8), ("ml_norm_g", 8), ("gate_b", 2),
    ("g_mix", 8), ("g_moe", 8), ("g_ple", 8), ("g_final", 8), ("g_subln", 1),
    ("w_conv", 32), ("b_conv", 8), ("b_rg", 8), ("b_ig", 8), ("lru_lambda", 8), ("lam", 4), ("b_rt", 36),
]
VEC_AT = {}
_n = 0
for _name, _count in VECTORS:
    VEC_AT[_name] = _n
    _n += _count
N_VEC = _n

CONSTS = [("ident", 128), ("tri_f", 128), ("tri_b", 128), ("iota", 8),
          ("cos", SEQ), ("sin", SEQ), ("swap", 128), ("select", 8 * 128), ("slots", 4 * P)]
CONST_AT = {}
_n = 0
for _name, _count in CONSTS:
    CONST_AT[_name] = _n
    _n += _count
N_CONST = _n
KEPT_CONST = CONST_AT["cos"]
START_VEC = VEC_AT["ln_g"]

GATE_ROWS = 64
F32 = mybir.dt.float32
F32R = mybir.dt.float32r
U32 = mybir.dt.uint32
ALU = mybir.AluOpType
ACT = mybir.ActivationFunctionType
AX_X = mybir.AxisListType.X


class Signal:

    def __init__(self, sem):
        self.sem, self.n = sem, 0

    def take(self, k):
        self.n += k
        return self.n - k


def program(nc, stream, vec_d, const_d, x_d, p_d, ada_d, late_d, out_d):
    ctx = ExitStack()
    with ctx:
        def sb(name, shape, dt=F32):
            return ctx.enter_context(nc.sbuf_tensor(name, shape, dt))

        def sig(name):
            return Signal(ctx.enter_context(nc.semaphore(name)))

        raw = sb("raw", [P, RING, TILE])
        whi = sb("whi", [P, RING, TILE], F32R)
        wlo = sb("wlo", [P, RING, TILE], F32R)
        h = sb("h", [P, KD, TOK])
        xm = sb("xm", [P, 2, KD, TOK], F32R)
        hid = sb("hid", [P, 2, HALF_A, TOK], F32R)
        work = sb("work", [P, 12, TOK])
        tmp = sb("tmp", [P, 4, TOK])
        vec = sb("vec", [P, N_VEC - START_VEC])
        const = sb("const", [P, KEPT_CONST])
        mods = sb("mods", [P, 2, 2, N_MOD, KD])
        ones_one = sb("ones_one", [P, SEQ])
        ratio = sb("ratio", [P, SEQ])
        eps = sb("eps", [P, 3])
        silu_c = sb("silu_c", [P, KD, 2])
        split_c = sb("split_c", [P, KD, 4], F32R)
        small = sb("small", [P, 64])
        idx8 = sb("idx8", [P, 2, 2, 8], U32)
        bank = [ctx.enter_context(nc.psum_tensor(f"bank{i}", [P, 2, 512], F32)) for i in range(4)]

        def ps(i):
            return bank[i // 2][:, i % 2, :]

        def pair(i):
            return bank[i]

        def v(name, i=0, n=1):
            a = VEC_AT[name] + i - START_VEC
            return vec[:, a:a + n]

        def cst(name, w, i=0):
            a = CONST_AT[name] + i * w
            return const[:, a:a + w]

        ident = cst("ident", 128)

        def mod(layer, part, s, k):
            return mods[:, s, layer, part, k:k + 1]

        landed = [ctx.enter_context(nc.semaphore(f"landed{i}")) for i in range(RING)]
        hi_done = ctx.enter_context(nc.semaphore("hi_done"))
        lo_done = ctx.enter_context(nc.semaphore("lo_done"))
        tile_used = ctx.enter_context(nc.semaphore("tile_used"))

        def each_tile(eng, t0, t1, body):
            turns = (t1 - t0) // RING
            done = 0
            if turns >= 2:
                with eng.Fori(0, turns) as i:
                    for j in range(RING):
                        body(i * RING + (t0 + j), (t0 + j) % RING, i + (t0 + j + ADA_TILES) // RING, i * RING + j)
                done = turns * RING
            for n in range(t0 + done, t1):
                body(n, n % RING, (n + ADA_TILES) // RING, n - t0)

        lo_half = ctx.enter_context(nc.semaphore("lo_half"))
        SHARED, SHARED_END = FIRST["experts"][0] + RING, FIRST["experts"][1]
        HALF = TILE // 2

        def ranges(t0, t1):
            cuts = [t0, min(max(SHARED, t0), t1), min(max(SHARED_END, t0), t1), t1]
            return [(cuts[i], cuts[i + 1], i == 1) for i in range(3) if cuts[i] < cuts[i + 1]]

        def load_tiles(sp, t0, t1):
            for a, b, shared in ranges(t0 - RING, t1 - RING):
                def load(m, slot, turn, _, shared=shared):
                    pool_count, dve_count = sp.to_reg(m + 1), sp.to_reg(m - (SHARED - 1)) if shared else None
                    sp.wait_ge(lo_done, pool_count)
                    if shared:
                        sp.wait_ge(lo_half, dve_count)
                    sp.dma_start(raw[:, slot, :], stream[m + (ADA_TILES + RING)]).then_inc(landed[slot], 16)
                each_tile(sp, a, b, load)

        def split_lo(pool, t0, t1):
            for a, b, shared in ranges(t0, t1):
                def lo(n, slot, turn, _, part=slice(HALF if shared else 0, TILE)):
                    pool.wait_ge(hi_done, n + 1)
                    nc.gpsimd.tensor_tensor(wlo[:, slot, part], raw[:, slot, part], whi[:, slot, part].bitcast(F32),
                                            ALU.subtract).then_inc(lo_done, 1)
                each_tile(pool, a, b, lo)

        def split_half(dve, m, slot):
            dve.wait_ge(hi_done, m + 1)
            nc.vector.tensor_tensor(wlo[:, slot, 0:HALF], raw[:, slot, 0:HALF], whi[:, slot, 0:HALF].bitcast(F32),
                                    ALU.subtract).then_inc(lo_half, 1)

        def tile_ready(pe, n, shared=False):
            pe.wait_ge(lo_done, n + 1)
            if shared:
                pe.wait_ge(lo_half, n - (SHARED - 1))

        def split_hi(act, n, slot, turn):
            act.wait_ge(tile_used, n - (RING - 1))
            act.wait_ge(landed[slot], turn * 16 + 16)
            nc.scalar.copy(whi[:, slot, :], raw[:, slot, :]).then_inc(hi_done, 1)

        def split_next(act, n, slot, turn):
            if isinstance(n, int) and n + RING >= TILES:
                act.wait_ge(tile_used, n + 1)
                return
            split_hi(act, n + RING, slot, turn + 1)

        def plain_splits(act, t0, t1):
            each_tile(act, t0, t1, lambda n, slot, turn, _: split_next(act, n, slot, turn))

        def mm3(pe, out, w_hi, w_lo, x_hi, x_lo, start):
            pe.matmul(out, w_hi, x_hi, start=start, stop=False, skip_group_check=True)
            pe.matmul(out, w_hi, x_lo, start=False, stop=False, skip_group_check=True)
            return pe.matmul(out, w_lo, x_hi, start=False, stop=True, skip_group_check=True)

        def c_unit(pe, n, slot, outs, cols=slice(0, TOK), ready=None, start=True, shared=False):
            tile_ready(pe, n, shared)
            order = [(b, k) for b in range(2) for k in range(KD)]
            if ready is not None and cols == slice(0, TOK):
                order = [(b, k) for k in range(KD) for b in range(2)]
            for b, k in order:
                if ready is not None and b == 0:
                    ready(k)
                at = slice(k * 256 + b * P, k * 256 + b * P + P)
                last = mm3(pe, outs[b], whi[:, slot, at], wlo[:, slot, at],
                           xm[:, 0, k, cols], xm[:, 1, k, cols], start and k == 0)
            last.then_inc(tile_used, 1)

        def t_unit(pe, n, slot, outs, blocks, fresh):
            pe.wait_ge(lo_done, n + 1)
            for t in range(blocks):
                at = slice(t * P, t * P + P)
                for k in range(KD):
                    w = slice(k * 256, k * 256 + 256)
                    start = k == 0 and t % 2 == 0 if fresh else k == 0
                    last = mm3(pe, outs[t], xm[:, 0, k, at], xm[:, 1, k, at],
                               whi[:, slot, w], wlo[:, slot, w], start)
            last.then_inc(tile_used, 1)

        def d_unit(pe, n, slot, outs, xs, first, signal=None, shared=False):
            tile_ready(pe, n, shared)

            def one(kk, ko):
                at = slice(kk * D + ko * P, kk * D + ko * P + P)
                x_hi, x_lo = xs(kk)
                width = x_hi.shape[-1]
                start = first and kk == 0 and (width == TOK or ko % 2 == 0)
                return mm3(pe, outs[ko], whi[:, slot, at], wlo[:, slot, at], x_hi, x_lo, start)

            if signal is None:
                for kk in range(2):
                    for ko in range(KD):
                        last = one(kk, ko)
            else:
                for ko in range(KD):
                    for kk in range(2):
                        last = one(kk, ko)
                    if ko < KD - 1:
                        last.then_inc(signal.sem, 1)
            last.then_inc(tile_used, 1)

        def d_outs(width):
            if width == TOK:
                return [ps(ko) for ko in range(KD)]
            return [ps(4 + ko // 2)[:, ko % 2 * SEQ:ko % 2 * SEQ + SEQ] for ko in range(KD)]

        late_copied, late_in, late_sum, late_added = (
            sig(n) for n in ("late_copied", "late_in", "late_sum", "late_added"))
        late_stored = [sig(f"late_stored{b}") for b in range(2)]

        def late_unit(pe, n, i, out):
            if i >= 1:
                pe.wait_ge(late_copied.sem, i)
            pe.wait_ge(lo_done, n + 1)
            for k in range(KD):
                at = slice(k * 256, k * 256 + 256)
                for w in (whi, wlo):
                    last = pe.matmul(out[0:4, 0:256], split_c[:, k, :], w[:, n % RING, at],
                                     start=(k == 0 and w is whi), stop=(k == KD - 1 and w is wlo))
            last.then_inc(tile_used, 1)

        def late_rows(act, n, i, out, buffers):
            act.wait_ge(tile_used, n + 1)
            if i >= 2:
                act.wait_ge(late_stored[i % 2].sem, 16 * (i // 2))
            b = slice(i % 2 * 256, i % 2 * 256 + 256)
            nc.scalar.copy(buffers[0:4, b], out[0:4, 0:256]).then_inc(late_copied.sem, 1)
            split_next(act, n, n % RING, (n + ADA_TILES) // RING)
            act.wait_ge(late_copied.sem, i + 1)
            j = i % ADA_GROUP
            act.dma_start(late_d[i // ADA_GROUP, :, j * 256:j * 256 + 256], buffers[0:4, b])\
                .then_inc(late_stored[i % 2].sem, 16)

        def late_back(act, g0, g1, dst):
            for b in range(2):
                act.wait_ge(late_stored[b].sem, 16 * ADA_GROUP * g1 // 2)
            act.dma_start(dst.rearrange("p (g c) -> p g c", c=P),
                          late_d[g0:g1].rearrange("g r (l p) -> (r l) g p", p=P)).then_inc(late_in.sem, 16)

        def late_turn(pe, groups, src):
            pe.wait_ge(late_in.sem, late_in.take(16) + 16)
            for g in range(groups):
                for half in range(2):
                    last = pe.matmul(ps(7)[:, g * 48:g * 48 + 48], src[:, g * P:g * P + P],
                                     ident[0:96, half * 48:half * 48 + 48], start=(half == 0), stop=(half == 1),
                                     skip_group_check=True)
            last.then_inc(late_sum.sem, 1)

        def adjust(run, layer, parts):
            for s in range(2):
                for part in parts:
                    m = mods[:, s, layer, part]
                    if part % 3 == 1:
                        run(nc.vector.tensor_scalar(m, m, 1.0, None, ALU.add))
                    if part in (2, 8):
                        run(nc.vector.tensor_scalar(m, m, 0.5, None, ALU.mult))

        def late_add(dve, run, g0, g1):
            n = late_sum.take(1)
            dve.wait_ge(late_sum.sem, n + 1)
            sums = ps(7)[:, 0:48 * (g1 - g0)].rearrange("p (g s l) -> p g s l", s=2, l=24)
            for s in range(2):
                m = mods[:, s].rearrange("p l m k -> p (l m k)")[:, 48 + 24 * g0:48 + 24 * g1]\
                    .rearrange("p (g l) -> p g l", l=24)
                last = nc.vector.tensor_tensor(m, m, sums[:, :, s, :], ALU.add)
                if s == 0:
                    run(last)
            last.then_inc(late_added.sem, 1)
            dve.wait_ge(late_added.sem, n + 1)
            return n + 1

        xm_f, xm_h, xm_r, xm_a = sig("xm_f"), sig("xm_h"), sig("xm_r"), sig("xm_a")
        act_gate, hid_f, hid_h, hid_r = sig("act_gate"), sig("hid_f"), sig("hid_h"), sig("hid_r")
        d_block, res = sig("d_block"), sig("res")
        mean_done, cent, squared, var_step, std_done = (sig("mean_done"), sig("cent"), sig("squared"),
                                                        sig("var_step"), sig("std_done"))
        rstd_done, normed, affine = sig("rstd_done"), sig("normed"), sig("affine")
        vlink, slink = sig("vlink"), sig("slink")

        def linked(eng, link):
            def run(ins):
                ins.then_inc(link.sem, 1)
                link.n += 1
                eng.wait_ge(link.sem, link.n)
            return run

        carried = []

        class Modulated:

            def __init__(self, layer, part, width):
                self.layer, self.part, self.width, self.s = layer, part, width, width // SEQ
                self.f, self.h, self.r, self.a = (xm_f.take(KD * self.s), xm_h.take(KD), xm_r.take(KD),
                                                  xm_a.take(KD))
                self.norm = carried.pop() if carried else None
                self.g = affine.take(KD) if self.norm else None

            def act(self, act):
                if self.norm:
                    self.norm.gain(act, 0)
                for k in range(KD):
                    if self.norm:
                        if k + 1 < KD:
                            self.norm.gain(act, k + 1)
                        act.wait_ge(affine.sem, self.g + k + 1)
                    if k >= 2:
                        act.wait_ge(xm_r.sem, self.r + k - 1)
                    for s in range(self.s):
                        at = slice(s * SEQ, s * SEQ + SEQ)
                        nc.scalar.activation(tmp[:, k % 2, at], h[:, k, at], ACT.Identity,
                                             bias=mod(self.layer, self.part, s, k),
                                             scale=mod(self.layer, self.part + 1, s, k)).then_inc(xm_f.sem, 1)

            def dve(self, dve):
                w = slice(0, self.width)
                if self.norm:
                    for k in range(3):
                        self.norm.divide(k)
                for k in range(KD):
                    if self.norm and k + 3 < KD:
                        self.norm.divide(k + 3)
                    dve.wait_ge(xm_f.sem, self.f + self.s * (k + 1))
                    nc.vector.tensor_copy(xm[:, 0, k, w], tmp[:, k % 2, w]).then_inc(xm_h.sem, 1)
                    dve.wait_ge(xm_h.sem, self.h + k + 1)
                    nc.vector.tensor_tensor(xm[:, 1, k, w], tmp[:, k % 2, w], xm[:, 0, k, w].bitcast(F32),
                                            ALU.subtract).then_inc(xm_r.sem, 1)
                    nc.vector.tensor_scalar(h[:, k, w], h[:, k, w], ALPHA, None, ALU.mult).then_inc(xm_a.sem, 1)

            def ready(self, pe):
                return lambda k: pe.wait_ge(xm_r.sem, self.r + k + 1)

        class Residual:

            def __init__(self, t1, layer, part, width):
                self.t1, self.layer, self.part, self.width, self.s = t1, layer, part, width, width // SEQ
                self.d, self.r = d_block.take(KD - 1), res.take(KD * self.s)

            def dve(self, dve):
                outs = d_outs(self.width)
                for ko in range(KD):
                    whole = ko if self.width == TOK else ko | 1
                    if whole < KD - 1:
                        dve.wait_ge(d_block.sem, self.d + whole + 1)
                    else:
                        dve.wait_ge(tile_used, self.t1)
                    for s in range(self.s):
                        at = slice(s * SEQ, s * SEQ + SEQ)
                        gate = mod(self.layer, self.part, s, ko) if self.layer is not None else 1.0
                        nc.vector.scalar_tensor_tensor(out=h[:, ko, at], in0=outs[ko][:, at], scalar=gate,
                                                       in1=h[:, ko, at], op0=ALU.mult, op1=ALU.add)\
                            .then_inc(res.sem, 1)

        class LayerNorm:

            def __init__(self, index, width, after, whole=False):
                self.whole = whole
                if not whole:
                    carried.append(self)
                self.index, self.width, self.after = index, width, after
                self.m, self.c, self.q = mean_done.take(1), cent.take(KD), squared.take(KD)
                self.v, self.s, self.r, self.n = var_step.take(KD), std_done.take(1), rstd_done.take(1), normed.take(KD)

            def pe(self, pe):
                w = slice(0, self.width)
                for k in range(KD):
                    pe.wait_ge(res.sem, self.after.r + self.after.s * (k + 1))
                    last = pe.matmul(ps(0)[:, w], ones_one[:, 0:P], h[:, k, w], start=(k == 0), stop=(k == KD - 1))
                last.then_inc(mean_done.sem, 1)
                for k in range(KD):
                    pe.wait_ge(squared.sem, self.q + k + 1)
                    pe.matmul(ps(1)[:, w], ones_one[:, 0:P], tmp[:, k % 2, w], start=(k == 0),
                              stop=(k == KD - 1)).then_inc(var_step.sem, 1)

            def dve(self, dve):
                w = slice(0, self.width)
                dve.wait_ge(mean_done.sem, self.m + 1)
                for k in range(KD):
                    nc.vector.scalar_tensor_tensor(out=h[:, k, w], in0=ps(0)[:, w], scalar=-1.0 / D, in1=h[:, k, w],
                                                   op0=ALU.mult, op1=ALU.add).then_inc(cent.sem, 1)
                dve.wait_ge(std_done.sem, self.s + 1)
                nc.vector.reciprocal(tmp[:, 3, w], tmp[:, 2, w]).then_inc(rstd_done.sem, 1)
                dve.wait_ge(rstd_done.sem, self.r + 1)
                if self.whole:
                    for k in range(KD):
                        self.divide(k)

            def divide(self, k):
                w = slice(0, self.width)
                nc.vector.tensor_tensor(h[:, k, w], h[:, k, w], tmp[:, 3, w], ALU.mult).then_inc(normed.sem, 1)

            def gain(self, act, k):
                w = slice(0, self.width)
                act.wait_ge(normed.sem, self.n + k + 1)
                nc.scalar.activation(h[:, k, w], h[:, k, w], ACT.Identity, bias=v("ln_b", self.index * KD + k),
                                     scale=v("ln_g", self.index * KD + k)).then_inc(affine.sem, 1)

            def act(self, act):
                w = slice(0, self.width)
                for k in range(KD):
                    act.wait_ge(cent.sem, self.c + k + 1)
                    if k >= 2:
                        act.wait_ge(var_step.sem, self.v + k - 1)
                    nc.scalar.activation(tmp[:, k % 2, w], h[:, k, w], ACT.Square).then_inc(squared.sem, 1)
                act.wait_ge(var_step.sem, self.v + KD)
                nc.scalar.activation(tmp[:, 2, w], ps(1)[:, w], ACT.Sqrt, bias=eps[:, 0:1], scale=1.0 / D)\
                    .then_inc(std_done.sem, 1)
                if self.whole:
                    affine.take(KD)
                    for k in range(KD):
                        self.gain(act, k)

        class RmsNorm:

            def __init__(self, gain, after=None):
                self.gain = gain
                self.q, self.v, self.s, self.r, self.x = (squared.take(KD), var_step.take(KD), std_done.take(1),
                                                          rstd_done.take(1), xm_r.take(KD))
                self.after = after

            def act(self, act):
                w = slice(0, SEQ)
                for k in range(KD):
                    if self.after is not None:
                        act.wait_ge(res.sem, self.after.r + k + 1)
                    if k >= 2:
                        act.wait_ge(var_step.sem, self.v + k - 1)
                    nc.scalar.activation(tmp[:, k % 2, w], h[:, k, w], ACT.Square).then_inc(squared.sem, 1)
                act.wait_ge(var_step.sem, self.v + KD)
                nc.scalar.activation(tmp[:, 2, w], ps(1)[:, w], ACT.Sqrt, bias=eps[:, 1:2], scale=1.0 / D)\
                    .then_inc(std_done.sem, 1)

            def pe(self, pe):
                w = slice(0, SEQ)
                for k in range(KD):
                    pe.wait_ge(squared.sem, self.q + k + 1)
                    pe.matmul(ps(1)[:, w], ones_one[:, 0:P], tmp[:, k % 2, w], start=(k == 0),
                              stop=(k == KD - 1)).then_inc(var_step.sem, 1)

            def dve(self, dve, split=True, keep=False):
                w = slice(0, SEQ)
                run = linked(dve, vlink)
                dve.wait_ge(std_done.sem, self.s + 1)
                nc.vector.reciprocal(tmp[:, 3, w], tmp[:, 2, w]).then_inc(rstd_done.sem, 1)
                dve.wait_ge(rstd_done.sem, self.r + 1)
                for k in range(KD):
                    out = g8[:, k, :] if keep else tmp[:, k % 2, w] if split else work[:, k, w]
                    run(nc.vector.scalar_tensor_tensor(out=out, in0=h[:, k, w], scalar=v(self.gain, k),
                                                       in1=tmp[:, 3, w], op0=ALU.mult, op1=ALU.mult))
                    if split:
                        run(nc.vector.tensor_copy(xm[:, 0, k, w], out))
                        nc.vector.tensor_tensor(xm[:, 1, k, w], out, xm[:, 0, k, w].bitcast(F32),
                                                ALU.subtract).then_inc(xm_r.sem, 1)

            def ready(self, pe):
                return lambda k: pe.wait_ge(xm_r.sem, self.x + k + 1)

        def stage(t0, t1, tensor, vector, scalar):
            with nc.Block(no_gpsimd_drain=True) as block:
                @block.sync
                def _(sp):
                    load_tiles(sp, min(t0 + 2 * RING, TILES) if t0 else RING, min(t1 + 2 * RING, TILES))

                @block.gpsimd
                def _(pool):
                    split_lo(pool, min(t0 + RING, TILES) if t0 else 0, min(t1 + RING, TILES))

                @block.scalar
                def _(act):
                    scalar(act)

                @block.vector
                def _(dve):
                    vector(dve)

                @block.tensor
                def _(pe):
                    tensor(pe)

        params_in, silu_c_done, ada_used, row_done = sig("params_in"), sig("silu_c_done"), sig("ada_used"), sig("row_done")
        rows_out, rows_in, turned, masks_done = sig("rows_out"), sig("rows_in"), sig("turned"), sig("masks_done")
        start_vec = tmp[:, 3, 0:START_VEC]
        rows = work[:, :, :].rearrange("p a b -> p (a b)").rearrange("p (g n) -> p g n", g=2)
        with nc.Block(no_gpsimd_drain=True) as block:
            @block.sync
            def _(sp):
                for slot in range(RING):
                    sp.dma_start(raw[:, slot, :], stream[slot]).then_inc(landed[slot], 16)
                with sp.Fori(1, ADA_TILES // RING) as i:
                    for slot in range(RING):
                        sp.wait_ge(ada_used.sem, (i - 1) * RING + slot + 1)
                        sp.dma_start(raw[:, slot, :], stream[i * RING + slot]).then_inc(landed[slot], 16)
                for slot in range(RING):
                    sp.wait_ge(ada_used.sem, ADA_TILES - RING + slot + 1)
                    sp.dma_start(raw[:, slot, :], stream[ADA_TILES + slot]).then_inc(landed[slot], 16)

            @block.gpsimd
            def _(pool):
                nc.gpsimd.memset(ones_one[:, :], 1.0)

            @block.scalar
            def _(act):
                act.dma_start(start_vec, vec_d[:, 0:START_VEC]).then_inc(params_in.sem, 16)
                act.wait_ge(params_in.sem, 16)
                nc.scalar.activation(silu_c[:, :, :].rearrange("p k s -> p (k s)"), start_vec[:, 0:16], ACT.Silu)\
                    .then_inc(silu_c_done.sem, 1)
                act.dma_start(vec[:, :], vec_d[:, START_VEC:N_VEC]).then_inc(params_in.sem, 16)
                act.dma_start(const[:, :], const_d[:, 0:KEPT_CONST]).then_inc(params_in.sem, 16)
                act.dma_start(h[:, :, :], x_d).then_inc(params_in.sem, 16)
                for g in range(ADA_TILES // ADA_GROUP):
                    act.wait_ge(row_done.sem, ADA_GROUP * (g + 1))
                    act.dma_start(ada_d[:, g * 3072:(g + 1) * 3072], rows[0:2, g % 2, :]).then_inc(rows_out.sem, 16)
                    act.wait_ge(rows_out.sem, 16 * (g + 1))
                act.dma_start(tmp[0:96, 0, 0:P],
                              ada_d.rearrange("s (l p) -> (s l) p", p=P))\
                    .then_inc(rows_in.sem, 16)
                for n in range(RING):
                    act.wait_ge(landed[n], 16 * (ADA_TILES // RING) + 16)
                    nc.scalar.copy(whi[:, n, :], raw[:, n, :]).then_inc(hi_done, 1)

            @block.vector
            def _(dve):
                nc.vector.memset(eps[:, 0:1], LN_EPS)
                nc.vector.memset(eps[:, 1:2], RMS_EPS)
                nc.vector.memset(eps[:, 2:3], 1.0)
                run = linked(dve, vlink)
                dve.wait_ge(silu_c_done.sem, 1)
                run(nc.vector.tensor_copy(split_c[:, :, 0:2], silu_c[:, :, :]))
                run(nc.vector.tensor_tensor(split_c[:, :, 2:4], silu_c[:, :, :], split_c[:, :, 0:2].bitcast(F32),
                                            ALU.subtract))
                for s in range(2):
                    run(nc.vector.tensor_copy(mods[:, s].rearrange("p l m k -> p (l m k)"),
                                              start_vec[:, VEC_AT["ada_b"]:VEC_AT["ada_b"] + 144]))
                for g in range(ADA_TILES // ADA_GROUP):
                    with dve.Fori(0, ADA_GROUP // RING) as i:
                        for slot in range(RING):
                            dve.wait_ge(ada_used.sem, i * RING + (g * ADA_GROUP + slot + 1))
                            nc.vector.tensor_copy(rows[0:2, g % 2, bass.ds(i * (RING * 256) + slot * 256, 256)],
                                                  ps(slot)[0:2, 0:256]).then_inc(row_done.sem, 1)
                dve.wait_ge(turned.sem, 1)
                for s in range(2):
                    m = mods[:, s, 0].rearrange("p m k -> p (m k)")[:, 0:48]
                    run(nc.vector.tensor_tensor(m, m, ps(3)[:, s * 48:s * 48 + 48], ALU.add))
                adjust(run, 0, range(6))

            @block.tensor
            def _(pe):
                pe.wait_ge(silu_c_done.sem, 1)

                def ada(g, slot):
                    if not isinstance(g, int):
                        pe.wait_ge(row_done.sem, g - (RING - 1))
                    pe.wait_ge(landed[slot], turn16)
                    for k in range(KD):
                        last = pe.matmul(ps(slot)[0:2, 0:256], silu_c[:, k, :], raw[:, slot, k * 256:k * 256 + 256],
                                         start=(k == 0), stop=(k == KD - 1))
                    last.then_inc(ada_used.sem, 1)

                for slot in range(RING):
                    turn16 = 16
                    ada(slot, slot)
                with pe.Fori(1, ADA_TILES // RING) as i:
                    for slot in range(RING):
                        turn16 = i * 16 + 16
                        ada(i * RING + slot, slot)
                pe.wait_ge(rows_in.sem, 16)
                pe.wait_ge(params_in.sem, 64)
                pe.transpose(ps(3)[:, 0:96], tmp[0:96, 0, 0:P], ident[0:96, 0:96]).then_inc(turned.sem, 1)

        def ffn(name, layer, which, width):
            t0, _ = FIRST[name]
            part = 6 * which
            mx = Modulated(layer, part, width)
            w = slice(0, width)
            parts = []
            n = t0
            for first_block, blocks in ((0, HALF_A), (HALF_A, HALF_B)):
                parts.append((n, n + blocks, n + blocks + blocks // 2, act_gate.take(blocks), hid_f.take(blocks),
                              hid_h.take(blocks), hid_r.take(blocks),
                              Residual(n + blocks + blocks // 2, layer, part + 2, width)))
                n += blocks + blocks // 2
            t1 = n
            ln = LayerNorm(layer * 3 + 2 * which, width, parts[1][-1], whole=(name == "ffn11"))
            outs = d_outs(width)

            def tensor(pe):
                for i, (g0, g1, d1, ag, hf, hh, hr, rs) in enumerate(parts):
                    def gate_up(n, slot, turn, u, hr=hr):
                        if not isinstance(u, int) or u >= RING:
                            pe.wait_ge(hid_r.sem, u + (hr - (RING - 1)))
                        c_unit(pe, n, slot, [ps(2 * slot)[:, w], ps(2 * slot + 1)[:, w]], w)
                    ready = mx.ready(pe) if i == 0 else None
                    if i == 1:
                        pe.wait_ge(res.sem, parts[0][-1].r + KD * parts[0][-1].s)
                    c_unit(pe, g0, g0 % RING, [ps(2 * (g0 % RING))[:, w], ps(2 * (g0 % RING) + 1)[:, w]], w, ready)
                    rest = (g1 - g0 - 1) // RING * RING
                    for u in range(1, 1 + RING):
                        gate_up(g0 + u, (g0 + u) % RING, None, u)
                    shifted_tiles(pe, g0 + 1 + RING, g1, lambda n, s, t, u, f=gate_up: f(n, s, t, u + (1 + RING)))
                    for d in range(g1, d1):
                        pe.wait_ge(hid_r.sem, hr + (g1 - g0))
                        d_unit(pe, d, d % RING, outs, lambda kk, j=d - g1: (hid[:, 0, 2 * j + kk, w], hid[:, 1, 2 * j + kk, w]),
                               d == g1, d_block if d == d1 - 1 else None)
                ln.pe(pe)

            def scalar(act):
                mx.act(act)
                for g0, g1, d1, ag, hf, hh, hr, rs in parts:
                    def gate(n, slot, turn, u, ag=ag, hf=hf):
                        split_next(act, n, slot, turn)
                        act.wait_ge(tile_used, n + 1)
                        if not isinstance(u, int) or u >= RING:
                            act.wait_ge(hid_f.sem, u + (hf - (RING - 1)))
                        nc.scalar.activation(work[:, slot, w], ps(2 * slot)[:, w], ACT.Silu).then_inc(act_gate.sem, 1)
                    for u in range(RING):
                        gate(g0 + u, (g0 + u) % RING, (g0 + u + ADA_TILES) // RING, u)
                    shifted_tiles(act, g0 + RING, g1, lambda n, s, t, u, f=gate: f(n, s, t, u + RING))
                    plain_splits(act, g1, d1)
                ln.act(act)

            def vector(dve):
                mx.dve(dve)
                dve.wait_ge(xm_a.sem, mx.a + KD)
                for i, (g0, g1, d1, ag, hf, hh, hr, rs) in enumerate(parts):
                    if i == 1:
                        dve.wait_ge(tile_used, parts[0][2])
                    def up(n, slot, turn, u, ag=ag, hf=hf, hh=hh, hr=hr):
                        dve.wait_ge(act_gate.sem, u + (ag + 1))
                        nc.vector.tensor_tensor(work[:, 3 + slot, w], work[:, slot, w], ps(2 * slot + 1)[:, w],
                                                ALU.mult).then_inc(hid_f.sem, 1)
                        dve.wait_ge(hid_f.sem, u + (hf + 1))
                        at = slice(u, u + 1) if isinstance(u, int) else bass.ds(u, 1)
                        nc.vector.tensor_scalar(hid[:, 0, at, w], work[:, 3 + slot:4 + slot, w], 1.0, None, ALU.mult)\
                            .then_inc(hid_h.sem, 1)
                        dve.wait_ge(hid_h.sem, u + (hh + 1))
                        nc.vector.tensor_tensor(hid[:, 1, at, w], work[:, 3 + slot:4 + slot, w],
                                                hid[:, 0, at, w].bitcast(F32), ALU.subtract).then_inc(hid_r.sem, 1)
                    each_tile(dve, g0, g1, up)
                    if i == 1:
                        dve.wait_ge(res.sem, parts[0][-1].r + KD * parts[0][-1].s)
                    rs.dve(dve)
                ln.dve(dve)

            stage(t0, t1, tensor, vector, scalar)

        def shifted_tiles(eng, t0, t1, body):
            if t1 > t0:
                each_tile(eng, t0, t1, body)

        q_of = [hid[:, a, 0:8, :] for a in range(2)]
        k_of = [hid[:, a, 8:10, :] for a in range(2)]
        v_of = [hid[:, a, 10:12, :].rearrange("p a b -> p (a b)").rearrange("p (t c) -> p t c", t=4) for a in range(2)]
        rope = work[:, 10:12, :].rearrange("p a b -> p (a b)")[:, 0:2 * SEQ + 128]
        sq_done, rms_done, head_f, swapped, rope_in = (sig("sq_done"), sig("rms_done"), sig("head_f"), sig("swapped"),
                                                       sig("rope_in"))
        head_std, head_r = sig("head_std"), sig("head_r")

        def attention_in():
            t0, t1 = FIRST["att_in"]
            mx = Modulated(0, 3, TOK)
            b_sq, b_rms, b_f, b_sw, b_r = sq_done.take(5), rms_done.take(5), head_f.take(5), swapped.take(5), head_r.take(6)
            b_std = head_std.take(5)

            late_bank, buffers = ps(7), tmp[:, 2, :]

            def late(unit, u, b, *more):
                if u < 6:
                    unit(t0 + 3 * u + 1 + b, 2 * u + b, late_bank, *more)

            def tensor(pe):
                def swap(j):
                    pe.wait_ge(head_f.sem, b_f + j + 1)
                    pe.wait_ge(rope_in.sem, 16)
                    if j >= 1:
                        pe.wait_ge(head_r.sem, b_r + j)
                    for b in range(2):
                        last = pe.matmul(ps(6)[:, b * 256:b * 256 + 256], rope[:, 2 * SEQ:2 * SEQ + 128], work[:, 4 + b, 0:SEQ],
                                         start=True, stop=True)
                    last.then_inc(swapped.sem, 1)

                for u in range(6):
                    if u < 5:
                        if u >= 2:
                            pe.wait_ge(head_f.sem, b_f + u - 1)
                        c_unit(pe, t0 + 3 * u, t0 % RING, [ps(2 * (u % 2)), ps(2 * (u % 2) + 1)],
                               ready=mx.ready(pe) if u == 0 else None)
                    if u == 5:
                        pe.wait_ge(head_f.sem, b_f + 4)
                        t_unit(pe, t0 + 15, t0 % RING,
                               [ps(2 + t // 2)[:, t % 2 * 256:t % 2 * 256 + 256] for t in range(4)], 4, False)
                    if u >= 1:
                        swap(u - 1)
                    late(lambda *at: late_unit(pe, *at), u, 0)
                    if u < 5:
                        pe.wait_ge(sq_done.sem, b_sq + u + 1)
                        if u >= 1:
                            pe.wait_ge(head_std.sem, b_std + u)
                        for b in range(2):
                            last = pe.matmul(ps(4 + b), ones_one[:, 0:P], work[:, b, :], start=True, stop=True)
                        last.then_inc(rms_done.sem, 1)
                    late(lambda *at: late_unit(pe, *at), u, 1)

            def scalar(act):
                act.dma_start(rope, const_d[:, KEPT_CONST:KEPT_CONST + 2 * SEQ + 128]).then_inc(rope_in.sem, 16)
                mx.act(act)
                for u in range(6):
                    split_next(act, t0 + 3 * u, t0 % RING, (t0 + 3 * u + ADA_TILES) // RING)
                    if u < 5:
                        act.wait_ge(tile_used, t0 + 3 * u + 1)
                        if u >= 1:
                            act.wait_ge(rms_done.sem, b_rms + u)
                        nc.scalar.activation(work[:, 0:2, :], pair(u % 2)[:, :, :], ACT.Square).then_inc(sq_done.sem, 1)
                    late(lambda *at: late_rows(act, *at), u, 0, buffers)
                    if u < 5:
                        act.wait_ge(rms_done.sem, b_rms + u + 1)
                        if u >= 1:
                            act.wait_ge(head_f.sem, b_f + u)
                        nc.scalar.activation(work[:, 2:4, :], pair(2)[:, :, :], ACT.Sqrt, bias=eps[:, 1:2], scale=1.0 / P)\
                            .then_inc(head_std.sem, 1)
                    late(lambda *at: late_rows(act, *at), u, 1, buffers)

            def vector(dve):
                mx.dve(dve)
                run = linked(dve, vlink)
                dve.wait_ge(rope_in.sem, 16)
                for u in range(5):
                    gain = v("q_gain") if u < 4 else v("k_gain")
                    dst = [q_of[a][:, 2 * u:2 * u + 2, :] if u < 4 else k_of[a] for a in range(2)]
                    dve.wait_ge(head_std.sem, b_std + u + 1)
                    run(nc.vector.reciprocal(work[:, 8:10, :], work[:, 2:4, :]))
                    if u >= 1:
                        dve.wait_ge(swapped.sem, b_sw + u)
                    nc.vector.scalar_tensor_tensor(out=work[:, 4:6, :], in0=pair(u % 2)[:, :, :], scalar=gain,
                                                   in1=work[:, 8:10, :], op0=ALU.mult, op1=ALU.mult)\
                        .then_inc(head_f.sem, 1)
                    dve.wait_ge(swapped.sem, b_sw + u + 1)
                    for b in range(2):
                        nc.vector.tensor_tensor(work[:, 6, b * 256:b * 256 + 256], ps(6)[:, b * 256:b * 256 + 256],
                                                rope[:, SEQ:2 * SEQ], ALU.mult)
                        run(nc.vector.tensor_tensor(work[:, 7, b * 256:b * 256 + 256], work[:, 4 + b, 0:SEQ],
                                                    rope[:, 0:SEQ], ALU.mult))
                    for b in range(2):
                        run(nc.vector.tensor_tensor(work[:, 4 + b, 0:SEQ], work[:, 7, b * 256:b * 256 + 256],
                                                    work[:, 6, b * 256:b * 256 + 256], ALU.add))
                    run(nc.vector.tensor_copy(dst[0], work[:, 4:6, :]))
                    nc.vector.tensor_tensor(dst[1], work[:, 4:6, :], dst[0].bitcast(F32), ALU.subtract)\
                        .then_inc(head_r.sem, 1)
                dve.wait_ge(tile_used, t0 + 16)
                vv = pair(1)[:, :, :].rearrange("p a (t c) -> p (a t) c", c=256)
                run(nc.vector.tensor_copy(v_of[0], vv))
                nc.vector.tensor_tensor(v_of[1], vv, v_of[0].bitcast(F32), ALU.subtract).then_inc(head_r.sem, 1)

            stage(t0, t1, tensor, vector, scalar)

        row_max, exp_done, prob_done, prob_t, prob_s, pv_done, o_done = (
            sig("row_max"), sig("exp_done"), sig("prob_done"), sig("prob_t"), sig("prob_s"), sig("pv_done"), sig("o_done"))
        score_done = sig("score_done")

        def attention_core():
            items = [(hd, s) for hd in range(8) for s in range(2)]
            n_items = len(items)
            b_sc, b_mx, b_ex, b_pr, b_pt, b_ps, b_pv, b_o = (
                score_done.take(n_items), row_max.take(n_items), exp_done.take(2 * n_items), prob_done.take(n_items),
                prob_t.take(n_items), prob_s.take(n_items), pv_done.take(n_items), o_done.take(n_items))
            t0, t1 = FIRST["att_core"]
            late_bank, buffers = ps(7), tmp[:, 0, :]

            def late(unit, i, b, *more):
                if i < n_items and not (b == 1 and i % 2):
                    j = i + (i + 1) // 2 + b
                    unit(t0 + j, ADA_GROUP + j, late_bank, *more)

            def keys(s):
                return (0, 4) if s == 0 else (2, 4)

            def scores(pe, i):
                hd, s = items[i]
                k0, k1 = keys(s)
                if i >= 2:
                    pe.wait_ge(exp_done.sem, b_ex + 2 * (i - 1))
                kk = slice(k0 * P, k1 * P)
                for q in range(2):
                    at = slice(s * SEQ + q * P, s * SEQ + q * P + P)
                    last = mm3(pe, ps(2 * (i % 2) + q)[:, kk], q_of[0][:, hd, at], q_of[1][:, hd, at],
                               k_of[0][:, hd // 4, kk], k_of[1][:, hd // 4, kk], True)
                last.then_inc(score_done.sem, 1)

            def tensor(pe):
                scores(pe, 0)
                for i in range(n_items + 1):
                    if i + 1 < n_items:
                        scores(pe, i + 1)
                    late(lambda *at: late_unit(pe, *at), i, 0)
                    if i < n_items:
                        k0, k1 = keys(items[i][1])
                        pe.wait_ge(prob_done.sem, b_pr + i + 1)
                        if i >= 1:
                            pe.wait_ge(prob_s.sem, b_ps + i)
                        for b in range(k0, k1):
                            for q in range(2):
                                at = (b - k0) * 256 + q * P
                                last = pe.transpose(ps(4 + at // 512)[:, at % 512:at % 512 + P],
                                                    work[:, 2 * (i % 2) + q, b * P:b * P + P], ident)
                        last.then_inc(prob_t.sem, 1)
                    late(lambda *at: late_unit(pe, *at), i, 1)
                    if i >= 1:
                        j = i - 1
                        hd, s = items[j]
                        k0, k1 = keys(s)
                        pe.wait_ge(prob_s.sem, b_ps + j + 1)
                        if j >= 1:
                            pe.wait_ge(o_done.sem, b_o + j)
                        c0 = hd // 4 * P
                        for b in range(k0, k1):
                            pt = slice((b - k0) * 256, (b - k0) * 256 + 256)
                            last = mm3(pe, ps(6)[:, 0:256], v_of[0][:, b, c0:c0 + P], v_of[1][:, b, c0:c0 + P],
                                       pt_of(j)[0][:, pt], pt_of(j)[1][:, pt], b == k0)
                        last.then_inc(pv_done.sem, 1)

            def pt_of(j):
                return [xm[:, a, 6:8, :].rearrange("p a b -> p (a b)") for a in range(2)]

            def scalar(act):
                for i, (hd, s) in enumerate(items):
                    kk = slice(keys(s)[0] * P, keys(s)[1] * P)
                    act.wait_ge(row_max.sem, b_mx + i + 1)
                    if i >= 2:
                        act.wait_ge(prob_t.sem, b_pt + i - 1)
                    for q in range(2):
                        nc.scalar.activation(work[:, 2 * (i % 2) + q, kk], ps(2 * (i % 2) + q)[:, kk], ACT.Exp,
                                             bias=small[:, 4 + 2 * (i % 2) + q:5 + 2 * (i % 2) + q], scale=ATT_SCALE,
                                             accum_out=small[:, 8 + 2 * (i % 2) + q:9 + 2 * (i % 2) + q])\
                            .then_inc(exp_done.sem, 1)
                    for b in range(2):
                        late(lambda *at: late_rows(act, *at), i, b, buffers)
                late_back(act, 0, 3, tmp[0:96, 1, 0:384])

            def vector(dve):
                run = linked(dve, vlink)

                def maxima(i):
                    s = items[i][1]
                    kk = slice(keys(s)[0] * P, keys(s)[1] * P)
                    dve.wait_ge(score_done.sem, b_sc + i + 1)
                    a = 2 * (i % 2)
                    run(nc.vector.tensor_reduce(small[:, a:a + 2], pair(i % 2)[:, :, kk], AX_X, ALU.max))
                    nc.vector.tensor_scalar(small[:, 4 + a:6 + a], small[:, a:a + 2], -ATT_SCALE, None, ALU.mult)\
                        .then_inc(row_max.sem, 1)

                maxima(0)
                for i, (hd, s) in enumerate(items):
                    if i + 1 < n_items:
                        maxima(i + 1)
                    k0, k1 = keys(s)
                    kk = slice(k0 * P, k1 * P)
                    a = 2 * (i % 2)
                    dve.wait_ge(exp_done.sem, b_ex + 2 * (i + 1))
                    run(nc.vector.reciprocal(small[:, 12:14], small[:, 8 + a:10 + a]))
                    run(nc.vector.tensor_scalar(work[:, a, kk], work[:, a, kk], small[:, 12:13], None, ALU.mult))
                    nc.vector.tensor_scalar(work[:, a + 1, kk], work[:, a + 1, kk], small[:, 13:14], None, ALU.mult)\
                        .then_inc(prob_done.sem, 1)
                    dve.wait_ge(prob_t.sem, b_pt + i + 1)
                    if i >= 1:
                        dve.wait_ge(pv_done.sem, b_pv + i)
                        output(dve, i - 1, run)
                    n = (k1 - k0) * 256
                    src = pair(2)[:, :, :].rearrange("p a b -> p (a b)")[:, 0:n]
                    run(nc.vector.tensor_copy(pt_of(i)[0][:, 0:n], src))
                    nc.vector.tensor_tensor(pt_of(i)[1][:, 0:n], src, pt_of(i)[0][:, 0:n].bitcast(F32), ALU.subtract)\
                        .then_inc(prob_s.sem, 1)
                output(dve, n_items - 1, run)

            def output(dve, j, run):
                hd, s = items[j]
                dve.wait_ge(pv_done.sem, b_pv + j + 1)
                nc.vector.tensor_copy(work[:, 4 + hd, s * SEQ:s * SEQ + SEQ], ps(6)[:, 0:256])\
                    .then_inc(o_done.sem, 1)

            stage(t0, t1, tensor, vector, scalar)

        def project(name, layer, part, width, index, source, late, late_src):
            t0, t1 = FIRST[name]
            late_parts = [((g + 2) // 3, range((g + 2) % 3 * 3, (g + 2) % 3 * 3 + 3)) for g in range(*late)]
            rs = Residual(t1, layer, part, width)
            ln = LayerNorm(index, width, rs)
            b_r = xm_r.take(KD)
            w = slice(0, width)
            outs = d_outs(width)

            def tensor(pe):
                late_turn(pe, late[1] - late[0], late_src)
                pe.wait_ge(late_added.sem, late_sum.n)
                for d in range(t0, t1):
                    pe.wait_ge(xm_r.sem, b_r + 2 * (d - t0) + 2)
                    d_unit(pe, d, d % RING, outs, lambda kk, j=d - t0: (xm[:, 0, 2 * j + kk, w], xm[:, 1, 2 * j + kk, w]),
                           d == t0, d_block if d == t1 - 1 else None)
                ln.pe(pe)

            def scalar(act):
                plain_splits(act, t0, t1)
                ln.act(act)

            def vector(dve):
                run = linked(dve, vlink)
                late_add(dve, run, *late)
                for k in range(KD):
                    run(nc.vector.tensor_copy(xm[:, 0, k, w], source(k)))
                    nc.vector.tensor_tensor(xm[:, 1, k, w], source(k), xm[:, 0, k, w].bitcast(F32), ALU.subtract)\
                        .then_inc(xm_r.sem, 1)
                for layer, parts in late_parts:
                    adjust(run, layer, parts)
                rs.dve(dve)
                ln.dve(dve)

            stage(t0, t1, tensor, vector, scalar)

        flat_hid = [hid[:, a, :, :].rearrange("p a b -> p (a b)") for a in range(2)]
        mk = [flat_hid[a][:, 0:4 * TOK].rearrange("p (h t) -> p h t", h=4) for a in range(2)]
        mv = [flat_hid[a][:, 4 * TOK:12 * TOK].rearrange("p (t c) -> p t c", t=4) for a in range(2)]
        q_raw = work[:, 0:2, :].rearrange("p a b -> p (a b)").rearrange("p (h t) -> p h t", h=4)
        o_gate = work[:, 2:6, :].rearrange("p a b -> p (a b)").rearrange("p (k t) -> p k t", k=KD)
        mq = [xm[:, a, 0:2, :].rearrange("p a b -> p (a b)").rearrange("p (h t) -> p h t", h=4) for a in range(2)]
        gates_in, ml_evac, conv_act, o_act, abs_done, soft_done, stab_sum = (
            sig("gates_in"), sig("ml_evac"), sig("conv_act"), sig("o_act"), sig("abs_done"),
            sig("soft_done"), sig("stab_sum"))

        def mlstm_in():
            t0, t1 = FIRST["ml_in"]
            mx = Modulated(1, 3, TOK)
            lat = slice(0, SEQ)
            rows = slice(0, GATE_ROWS)

            def tensor(pe):
                for u in range(13):
                    if u == 4:
                        pe.wait_ge(gates_in.sem, 2)
                    if u >= 5:
                        pe.wait_ge(ml_evac.sem, u - 4)
                    a, n = 2 * (u % 4), t0 + u
                    if u < 3:
                        c_unit(pe, n, n % RING, [ps(a), ps(a + 1)], ready=mx.ready(pe) if u == 0 else None)
                    elif 5 <= u < 9:
                        t_unit(pe, n, n % RING, [ps(a + t // 2)[:, t % 2 * 256:t % 2 * 256 + 256] for t in range(4)],
                               4, False)
                    else:
                        c_unit(pe, n, n % RING, [ps(a)[:, lat], ps(a + 1)[:, lat]], lat)

            def scalar(act):
                run = linked(act, slink)
                mx.act(act)
                for u in range(13):
                    n = t0 + u
                    split_next(act, n, n % RING, (n + ADA_TILES) // RING)
                    act.wait_ge(tile_used, n + 1)
                    if u == 0:
                        nc.scalar.activation(work[rows, 10, :], ps(0)[rows, :], ACT.Identity, bias=v("gate_b", 0)[rows, :])\
                            .then_inc(gates_in.sem, 1)
                        nc.scalar.activation(work[rows, 11, :], ps(1)[rows, :], ACT.Identity, bias=v("gate_b", 1)[rows, :])\
                            .then_inc(gates_in.sem, 1)
                        act.wait_ge(abs_done.sem, 1)
                        run(nc.scalar.activation(tmp[rows, 1, :], tmp[rows, 0, :], ACT.Exp, scale=-1.0))
                        nc.scalar.activation(tmp[rows, 0, :], tmp[rows, 1, :], ACT.Ln, bias=eps[rows, 2:3])\
                            .then_inc(soft_done.sem, 1)
                        act.wait_ge(stab_sum.sem, 1)
                        run(nc.scalar.activation(work[rows, 11, SEQ:TOK], tmp[rows, 2, lat], ACT.Exp, scale=-1.0))
                    elif u < 5:
                        j = u - 1
                        act.wait_ge(ml_evac.sem, j + 1)
                        out = work[:, 8:10, :] if j < 2 else q_raw[:, 2 * (j - 2):2 * (j - 2) + 2, :]
                        src = work[:, 6:8, :] if j < 2 else work[:, 6:8, lat]
                        nc.scalar.activation(out, src, ACT.Silu).then_inc(conv_act.sem, 1)
                    elif u >= 9:
                        j = u - 9
                        nc.scalar.activation(o_gate[:, 2 * j:2 * j + 2, :], pair(u % 4)[:, :, lat], ACT.Sigmoid)\
                            .then_inc(o_act.sem, 1)

            def vector(dve):
                run = linked(dve, vlink)
                mx.dve(dve)
                f, b = slice(0, 4), slice(32, 36)
                dve.wait_ge(gates_in.sem, 2)
                nc.vector.scalar_tensor_tensor(out=tmp[rows, 0, :], in0=work[rows, 11, :], scalar=-1.0, in1=work[rows, 11, :], op0=ALU.mult, op1=ALU.max).then_inc(abs_done.sem, 1)
                run(nc.vector.memset(tmp[rows, 3, :], 0.0))
                dve.wait_ge(soft_done.sem, 1)
                run(nc.vector.scalar_tensor_tensor(out=tmp[rows, 2, :], in0=work[rows, 11, :], scalar=0.0,
                                                   in1=tmp[rows, 0, :], op0=ALU.min, op1=ALU.subtract))

                def scans(dst, src, op):
                    run(nc.vector.tensor_tensor_scan(dst[f, SEQ:TOK], ones_one[f, :], src[f, SEQ:TOK], 0.0, ALU.mult, op))
                    run(nc.vector.tensor_tensor_scan(dst[f, 0:SEQ], ones_one[f, :], src[f, 0:SEQ],
                                                     dst[f, TOK - 1:TOK], ALU.mult, op))
                    run(nc.vector.tensor_tensor_scan(dst[b, TOK - 1:SEQ - 1:-1], ones_one[b, :], src[b, TOK - 1:SEQ - 1:-1],
                                                     0.0, ALU.mult, op))
                    run(nc.vector.tensor_tensor_scan(dst[b, SEQ - 1::-1], ones_one[b, :], src[b, SEQ - 1::-1],
                                                     dst[b, SEQ:SEQ + 1], ALU.mult, op))
                scans(tmp[:, 3, :], tmp[:, 2, :], ALU.add)
                run(nc.vector.tensor_tensor(work[rows, 10, :], work[rows, 10, :], tmp[rows, 3, :], ALU.subtract))
                run(nc.vector.memset(tmp[rows, 1, :], 0.0))
                scans(tmp[:, 1, :], work[:, 10, :], ALU.max)
                run(nc.vector.tensor_copy(work[rows, 11, lat], tmp[rows, 1, lat]))
                nc.vector.tensor_tensor(tmp[rows, 2, lat], tmp[rows, 1, lat], tmp[rows, 3, lat], ALU.add)\
                    .then_inc(stab_sum.sem, 1)
                for j in range(4):
                    u = j + 1
                    width = TOK if j < 2 else SEQ
                    dve.wait_ge(tile_used, t0 + u + 1)
                    if j >= 1:
                        dve.wait_ge(conv_act.sem, j)
                    src = pair(u % 4)
                    for blk in range(2):
                        fb = 4 + 2 * j + blk if j < 2 else 2 * (j - 2) + blk
                        y = work[:, 6 + blk, :]
                        run(nc.vector.tensor_scalar(y[:, 0:width], src[:, blk, 0:width], v("ml_conv_w", KD + fb),
                                                    v("ml_conv_b", fb), ALU.mult, ALU.add))
                        for s in range(width // SEQ):
                            lo, hi = s * SEQ, s * SEQ + SEQ
                            run(nc.vector.scalar_tensor_tensor(out=y[:, lo + 1:hi], in0=src[:, blk, lo:hi - 1],
                                                               scalar=v("ml_conv_w", fb), in1=y[:, lo + 1:hi],
                                                               op0=ALU.mult, op1=ALU.add))
                            last = nc.vector.scalar_tensor_tensor(out=y[:, lo:hi - 1], in0=src[:, blk, lo + 1:hi],
                                                                  scalar=v("ml_conv_w", 2 * KD + fb), in1=y[:, lo:hi - 1],
                                                                  op0=ALU.mult, op1=ALU.add)
                            if not (blk == 1 and hi == width):
                                run(last)
                    last.then_inc(ml_evac.sem, 1)
                    if j < 2:
                        dve.wait_ge(conv_act.sem, j + 1)
                        dst = [mk[a][:, 2 * j:2 * j + 2, :] for a in range(2)]
                        run(nc.vector.tensor_copy(dst[0], work[:, 8:10, :]))
                        run(nc.vector.tensor_tensor(dst[1], work[:, 8:10, :], dst[0].bitcast(F32), ALU.subtract))
                for j in range(4):
                    u = 5 + j
                    dve.wait_ge(tile_used, t0 + u + 1)
                    vv = pair(u % 4)[:, :, :].rearrange("p a (t c) -> p (a t) c", c=256)
                    dst = [mv[a][:, :, j * 256:j * 256 + 256] for a in range(2)]
                    run(nc.vector.tensor_copy(dst[0], vv))
                    nc.vector.tensor_tensor(dst[1], vv, dst[0].bitcast(F32), ALU.subtract).then_inc(ml_evac.sem, 1)

            stage(t0, t1, tensor, vector, scalar)

        cols_turned, spread, ml_args, ml_exp, ml_prob, ml_turned, ml_split, ml_num, ml_var, ml_std, ml_hn, ml_hnt, ml_out = (
            sig(n) for n in ("cols_turned", "spread", "ml_args", "ml_exp", "ml_prob", "ml_turned", "ml_split", "ml_num",
                             "ml_var", "ml_std", "ml_hn", "ml_hnt", "ml_out"))
        cols_ready, select_in = sig("cols_ready"), sig("select_in")

        def mlstm_core():
            t0, t1 = FIRST["ml_core"]
            items = [(hd, t) for hd in range(4) for t in range(2)]
            n_items = len(items)
            b_sc = score_done.take(n_items)
            late_bank, buffers = ps(6), work[:, 0, :]

            def late(unit, i, b, *more):
                if i < n_items and not (b == 1 and i % 2):
                    j = i + (i + 1) // 2 + b
                    unit(t0 + j, 3 * ADA_GROUP + j, late_bank, *more)
            rows = slice(0, GATE_ROWS)
            mpt = [xm[:, a, 2, :] for a in range(2)]
            select = tmp[0:GATE_ROWS, 1:3, :].rearrange("p a b -> p (a b)").rearrange("p (r c) -> p r c", r=8)
            gcol = tmp[:, 3, 0:256]

            def row(hd, back):
                return hd + 32 * back

            def tensor(pe):
                for m in range(4):
                    last = pe.transpose(ps(7)[:, m * 64:m * 64 + 64], work[rows, 11, m * P:m * P + P], ident[rows, rows])
                last.then_inc(cols_turned.sem, 1)
                pe.wait_ge(select_in.sem, 16)
                pe.wait_ge(cols_ready.sem, 1)

                def front(i):
                    hd, t = items[i]
                    if t == 0:
                        if i >= 2:
                            pe.wait_ge(ml_args.sem, i)
                        for back in range(2):
                            last = pe.matmul(ps(2 + back), select[:, hd + 4 * back, :], work[rows, 10, :],
                                             start=True, stop=True)
                        last.then_inc(spread.sem, 1)
                    if i >= 2:
                        pe.wait_ge(ml_prob.sem, i - 1)
                    at = slice(t * P, t * P + P)
                    mm3(pe, ps(i % 2), mq[0][:, hd, at], mq[1][:, hd, at], mk[0][:, hd, :], mk[1][:, hd, :], True)\
                        .then_inc(score_done.sem, 1)

                def middle(i):
                    pe.wait_ge(ml_prob.sem, i + 1)
                    if i >= 1:
                        pe.wait_ge(ml_split.sem, i)
                    for b in range(4):
                        last = pe.transpose(ps(4)[:, b * P:b * P + P], work[:, 8, b * P:b * P + P], ident)
                    last.then_inc(ml_turned.sem, 1)
                    late(lambda *at: late_unit(pe, *at), i, 1)
                    if i >= 1:
                        pe.wait_ge(ml_hn.sem, i)
                    pe.wait_ge(ml_split.sem, i + 1)
                    hd = items[i][0]
                    for b in range(4):
                        pt = slice(b * P, b * P + P)
                        vc = slice(hd * 256, hd * 256 + 256)
                        last = mm3(pe, ps(5)[:, 0:256], mpt[0][:, pt], mpt[1][:, pt],
                                   mv[0][:, b, vc], mv[1][:, b, vc], b == 0)
                    last.then_inc(ml_num.sem, 1)

                def back_end(i):
                    pe.wait_ge(ml_hn.sem, i + 1)
                    if i >= 1:
                        pe.wait_ge(ml_out.sem, i)
                    for b in range(2):
                        last = pe.transpose(ps(7)[:, b * P:b * P + P], tmp[:, 0, b * P:b * P + P], ident)
                    last.then_inc(ml_hnt.sem, 1)

                front(0)
                for i in range(n_items):
                    if i + 1 < n_items:
                        front(i + 1)
                    late(lambda *at: late_unit(pe, *at), i, 0)
                    middle(i)
                    if i >= 1:
                        back_end(i - 1)
                back_end(n_items - 1)

            def scalar(act):
                act.dma_start(tmp[0:GATE_ROWS, 1:3, :].rearrange("p a b -> p (a b)"),
                              const_d[0:GATE_ROWS, CONST_AT["select"]:CONST_AT["slots"]]).then_inc(select_in.sem, 16)
                act.wait_ge(cols_ready.sem, 1)
                for i in range(n_items + 1):
                    if i < n_items:
                        hd, t = items[i]
                        act.wait_ge(ml_args.sem, i + 1)
                        for back in range(2):
                            c = t * 64 + row(hd, back)
                            nc.scalar.activation(work[:, 6 + back, :], work[:, 6 + back, :], ACT.Exp, bias=gcol[:, c:c + 1])\
                                .then_inc(ml_exp.sem, 1)
                    if i >= 1:
                        act.wait_ge(ml_var.sem, i)
                        nc.scalar.activation(small[:, 20:21], small[:, 19:20], ACT.Sqrt, bias=eps[:, 0:1])\
                            .then_inc(ml_std.sem, 1)
                    for b in range(2):
                        late(lambda *at: late_rows(act, *at), i, b, buffers)
                late_back(act, 3, 4, work[0:96, 1, 0:P])

            def vector(dve):
                run = linked(dve, vlink)
                run(nc.vector.tensor_copy(mq[0], q_raw))
                run(nc.vector.tensor_tensor(mq[1], q_raw, mq[0].bitcast(F32), ALU.subtract))
                dve.wait_ge(cols_turned.sem, 1)
                run(nc.vector.tensor_scalar(gcol[:, 0:128], ps(7)[:, 0:128], -1.0, None, ALU.mult))
                nc.vector.tensor_copy(gcol[:, 128:256], ps(7)[:, 128:256]).then_inc(cols_ready.sem, 1)
                dve.wait_ge(cols_ready.sem, 1)

                def args(i):
                    hd, t = items[i]
                    dve.wait_ge(spread.sem, hd + 1)
                    for back in range(2):
                        run(nc.vector.tensor_copy(work[:, 6 + back, :], ps(2 + back)))
                    own = slice(t * P, t * P + P)
                    run(nc.vector.tensor_tensor(work[:, 6, own], work[:, 6, own], cst("tri_f", 128), ALU.add))
                    run(nc.vector.memset(work[:, 6 + t, (1 - t) * P:(1 - t) * P + P], MASKED))
                    nc.vector.tensor_tensor(work[:, 7, own], work[:, 7, own], cst("tri_b", 128), ALU.add)\
                        .then_inc(ml_args.sem, 1)

                def probs(i):
                    hd, t = items[i]
                    dve.wait_ge(score_done.sem, b_sc + i + 1)
                    dve.wait_ge(ml_exp.sem, 2 * i + 2)
                    if i >= 1:
                        dve.wait_ge(ml_turned.sem, i)
                    for back in range(2):
                        run(nc.vector.tensor_tensor_reduce(work[:, 8 + back, :], work[:, 6 + back, :], ps(i % 2), ML_SCALE, 0.0,
                                                           ALU.mult, ALU.add, small[:, back:back + 1]))
                    run(nc.vector.scalar_tensor_tensor(out=small[:, 2:4], in0=small[:, 0:2], scalar=-1.0, in1=small[:, 0:2], op0=ALU.mult, op1=ALU.max))
                    for back in range(2):
                        c = 128 + t * 64 + row(hd, back)
                        run(nc.vector.tensor_tensor(small[:, 2 + back:3 + back], small[:, 2 + back:3 + back],
                                                    gcol[:, c:c + 1], ALU.max))
                    run(nc.vector.reciprocal(small[:, 4:6], small[:, 2:4]))
                    run(nc.vector.tensor_scalar(work[:, 9, :], work[:, 9, :], small[:, 5:6], None, ALU.mult))
                    nc.vector.scalar_tensor_tensor(out=work[:, 8, :], in0=work[:, 8, :], scalar=small[:, 4:5],
                                                   in1=work[:, 9, :], op0=ALU.mult, op1=ALU.add).then_inc(ml_prob.sem, 1)

                def split(i):
                    dve.wait_ge(ml_turned.sem, i + 1)
                    if i >= 1:
                        dve.wait_ge(ml_num.sem, i)
                    run(nc.vector.tensor_copy(mpt[0], ps(4)))
                    nc.vector.tensor_tensor(mpt[1], ps(4), mpt[0].bitcast(F32), ALU.subtract).then_inc(ml_split.sem, 1)

                num = ps(5)[:, 0:256]

                def moments(i):
                    dve.wait_ge(ml_num.sem, i + 1)
                    run(nc.vector.bn_stats(small[:, 8:14], num))
                    nc.vector.bn_aggr(small[:, 18:20], small[:, 8:14]).then_inc(ml_var.sem, 1)

                def norm(i):
                    dve.wait_ge(ml_std.sem, i + 1)
                    run(nc.vector.reciprocal(small[:, 21:22], small[:, 20:21]))
                    if i >= 1:
                        dve.wait_ge(ml_hnt.sem, i)
                    nc.vector.tensor_scalar(tmp[:, 0, 0:256], num, small[:, 18:19], small[:, 21:22], ALU.subtract, ALU.mult)\
                        .then_inc(ml_hn.sem, 1)

                def gated(i):
                    hd, t = items[i]
                    dve.wait_ge(ml_hnt.sem, i + 1)
                    for b in range(2):
                        fb = hd * 2 + b
                        g = o_gate[:, fb, t * P:t * P + P]
                        last = nc.vector.scalar_tensor_tensor(out=g, in0=ps(7)[:, b * P:b * P + P], scalar=v("ml_norm_g", fb),
                                                              in1=g, op0=ALU.mult, op1=ALU.mult)
                        if b == 0:
                            run(last)
                    last.then_inc(ml_out.sem, 1)

                args(0)
                for i in range(n_items):
                    probs(i)
                    if i >= 1:
                        moments(i - 1)
                    if i + 1 < n_items:
                        args(i + 1)
                    if i >= 1:
                        norm(i - 1)
                    split(i)
                    if i >= 2:
                        gated(i - 2)
                moments(n_items - 1)
                gated(n_items - 2)
                norm(n_items - 1)
                gated(n_items - 1)

            stage(t0, t1, tensor, vector, scalar)

        lat = slice(0, SEQ)
        spare = slice(SEQ, TOK)
        g8 = work[:, 0:4, :].rearrange("p a b -> p (a b)").rearrange("p (k t) -> p k t", k=KD)
        r8 = work[:, 4:8, :].rearrange("p a b -> p (a b)").rearrange("p (k t) -> p k t", k=KD)
        i8 = work[:, 8:12, :].rearrange("p a b -> p (a b)").rearrange("p (k t) -> p k t", k=KD)
        t8 = tmp[:, :, :].rearrange("p a b -> p (a b)").rearrange("p (k t) -> p k t", k=KD)
        dq = [flat_hid[a][:, 0:KD * SEQ].rearrange("p (h t) -> p h t", h=KD) for a in range(2)]
        dk = [flat_hid[a][:, KD * SEQ:2 * KD * SEQ].rearrange("p (h t) -> p h t", h=KD) for a in range(2)]
        dv = [flat_hid[a][:, 2 * KD * SEQ:3 * KD * SEQ].rearrange("p (t c) -> p t c", t=2) for a in range(2)]
        neg_sp, neg_lam, sub_gain = small[:, 48:56], small[:, 40:41], small[:, 41:42]
        lru_conv, gelu_sq, gelu_in, gelu_act, gelu_out, gates_done, xc_split = (
            sig(n) for n in ("lru_conv", "gelu_sq", "gelu_in", "gelu_act", "gelu_out", "gates_done", "xc_split"))
        scal_a, scal_b, lam_sum = sig("scal_a"), sig("scal_b"), sig("lam_sum")

        def lru_in():
            t0, t1 = FIRST["lru_in"]
            rms = RmsNorm("g_mix")

            def tensor(pe):
                rms.pe(pe)
                pe.wait_ge(scal_a.sem, 1)
                pe.matmul(ps(0)[:, 0:2], ones_one[:, 0:P], small[:, 42:44], start=True, stop=True).then_inc(lam_sum.sem, 1)
                pe.wait_ge(scal_b.sem, 1)
                for u in range(8):
                    n = t0 + u
                    c_unit(pe, n, n % RING, [ps(u)[:, b * 256:b * 256 + 256] for b in range(2)], lat,
                           rms.ready(pe) if u == 0 else None)
                n = t0 + 8
                pe.wait_ge(lo_done, n + 1)
                for kb in range(KD):
                    pe.wait_ge(xc_split.sem, kb + 1)
                    if kb >= 4:
                        pe.wait_ge(gelu_out.sem, kb - 3)
                    for g in range(2):
                        at = slice((2 * kb + g) * P, (2 * kb + g) * P + P)
                        last = mm3(pe, ps(kb)[:, g * 256:g * 256 + 256], whi[:, n % RING, at], wlo[:, n % RING, at],
                                   xm[:, 0, kb, spare], xm[:, 1, kb, spare], True)
                last.then_inc(tile_used, 1)

            def scalar(act):
                run = linked(act, slink)
                rms.act(act)
                act.wait_ge(lam_sum.sem, 1)
                nc.scalar.activation(small[:, 44:46], ps(0)[:, 0:2], ACT.Exp).then_inc(scal_b.sem, 1)
                run(nc.scalar.activation(small[:, 24:32], small[:, 32:40], ACT.Exp, scale=-1.0))
                nc.scalar.activation(small[:, 24:32], small[:, 24:32], ACT.Ln, bias=eps[:, 2:3]).then_inc(scal_b.sem, 1)
                for u in range(8):
                    n = t0 + u
                    split_next(act, n, n % RING, (n + ADA_TILES) // RING)
                    if u >= 4:
                        j = u - 4
                        act.wait_ge(tile_used, n + 1)
                        if j >= 1:
                            act.wait_ge(gelu_out.sem, j)
                        nc.scalar.activation(work[:, 8, :], ps(u), ACT.Square).then_inc(gelu_sq.sem, 1)
                        act.wait_ge(gelu_in.sem, j + 1)
                        nc.scalar.activation(work[:, 9, :], work[:, 8, :], ACT.Tanh, scale=GELU_C).then_inc(gelu_act.sem, 1)
                n = t0 + 8
                split_next(act, n, n % RING, (n + ADA_TILES) // RING)
                act.wait_ge(tile_used, n + 1)
                act.wait_ge(gelu_out.sem, 4)
                for kb in range(KD):
                    nc.scalar.activation(r8[:, kb, :], ps(kb)[:, 0:256], ACT.Sigmoid, bias=v("b_rg", kb))
                    last = nc.scalar.activation(i8[:, kb, :], ps(kb)[:, 256:512], ACT.Sigmoid, bias=v("b_ig", kb))
                last.then_inc(gates_done.sem, 1)

            def vector(dve):
                run = linked(dve, vlink)
                lam = v("lam", 0, 4)
                run(nc.vector.tensor_tensor(small[:, 42:43], lam[:, 0:1], lam[:, 1:2], ALU.mult))
                run(nc.vector.tensor_tensor(small[:, 43:44], lam[:, 2:3], lam[:, 3:4], ALU.mult))
                lru_l = v("lru_lambda", 0, 8)
                nc.vector.scalar_tensor_tensor(out=small[:, 32:40], in0=lru_l, scalar=-1.0, in1=lru_l, op0=ALU.mult, op1=ALU.max).then_inc(scal_a.sem, 1)
                rms.dve(dve)
                dve.wait_ge(scal_b.sem, 2)
                run(nc.vector.tensor_tensor(small[:, 46:47], small[:, 45:46], small[:, 44:45], ALU.subtract))
                run(nc.vector.tensor_scalar(neg_lam, small[:, 46:47], -LAM_INIT, None, ALU.add))
                run(nc.vector.tensor_scalar(neg_sp, lru_l, -1.0, 0.0, ALU.mult, ALU.max))
                run(nc.vector.tensor_tensor(neg_sp, neg_sp, small[:, 24:32], ALU.add))
                run(nc.vector.tensor_scalar(neg_sp, neg_sp, -LRU_C, None, ALU.mult))
                run(nc.vector.tensor_scalar(sub_gain, v("g_subln"), 1.0 - LAM_INIT, None, ALU.mult))
                for u in range(4):
                    dve.wait_ge(tile_used, t0 + u + 1)
                    for blk in range(2):
                        fb = 2 * u + blk
                        y = h[:, fb, spare]
                        src = ps(u)[:, blk * 256:blk * 256 + 256]
                        run(nc.vector.tensor_scalar(y, src, v("w_conv", 3 * KD + fb), v("b_conv", fb), ALU.mult, ALU.add))
                        for d in range(1, 4):
                            run(nc.vector.scalar_tensor_tensor(out=y[:, d:], in0=src[:, 0:SEQ - d],
                                                               scalar=v("w_conv", (3 - d) * KD + fb), in1=y[:, d:],
                                                               op0=ALU.mult, op1=ALU.add))
                        run(nc.vector.tensor_copy(xm[:, 0, fb, spare], y))
                        nc.vector.tensor_tensor(xm[:, 1, fb, spare], y, xm[:, 0, fb, spare].bitcast(F32), ALU.subtract)\
                            .then_inc(xc_split.sem, 1)
                for j in range(4):
                    dve.wait_ge(gelu_sq.sem, j + 1)
                    run(nc.vector.tensor_scalar(work[:, 8, :], work[:, 8, :], 0.044715, 1.0, ALU.mult, ALU.add))
                    nc.vector.tensor_tensor(work[:, 8, :], work[:, 8, :], ps(4 + j), ALU.mult).then_inc(gelu_in.sem, 1)
                    dve.wait_ge(gelu_act.sem, j + 1)
                    nc.vector.scalar_tensor_tensor(out=work[:, j, :], in0=work[:, 9, :], scalar=1.0, in1=ps(4 + j),
                                                   op0=ALU.add, op1=ALU.mult).then_inc(gelu_out.sem, 1)
                dve.wait_ge(gates_done.sem, 1)

            stage(t0, t1, tensor, vector, scalar)

        qkv_evac, lru_tanh, lru_ratio, lru_sqrt, lru_prod = (sig(n) for n in ("qkv_evac", "lru_tanh", "lru_ratio", "lru_sqrt",
                                                                            "lru_prod"))

        def qkv():
            t0, t1 = FIRST["qkv"]

            def tensor(pe):
                for u in range(12):
                    n = t0 + u
                    if u >= 8:
                        pe.wait_ge(qkv_evac.sem, u - 7)
                    outs = [ps(u % 8)[:, b * 256:b * 256 + 256] for b in range(2)]
                    if u < 8:
                        c_unit(pe, n, n % RING, outs, lat)
                    else:
                        t_unit(pe, n, n % RING, outs, 2, False)

            def scalar(act):
                for kb in range(KD):
                    nc.scalar.activation(t8[:, kb, :], r8[:, kb, :], ACT.Tanh, scale=neg_sp[:, kb:kb + 1])\
                        .then_inc(lru_tanh.sem, 1)
                act.wait_ge(lru_tanh.sem, KD)
                for kb in range(KD):
                    nc.scalar.activation(r8[:, kb, :], r8[:, kb, :], ACT.Exp, scale=neg_sp[:, kb:kb + 1])\
                        .then_inc(lru_tanh.sem, 1)
                n = t0
                split_next(act, n, n % RING, (n + ADA_TILES) // RING)
                for kb in range(KD):
                    act.wait_ge(lru_ratio.sem, kb + 1)
                    nc.scalar.activation(t8[:, kb, :], t8[:, kb, :], ACT.Sqrt).then_inc(lru_sqrt.sem, 1)
                for n in range(t0 + 1, t1):
                    split_next(act, n, n % RING, (n + ADA_TILES) // RING)

            def vector(dve):
                run = linked(dve, vlink)

                def evacuate(u):
                    dve.wait_ge(tile_used, t0 + u + 1)
                    if u < 8:
                        dst = [(dq if u < 4 else dk)[a][:, 2 * (u % 4):2 * (u % 4) + 2, :] for a in range(2)]
                    else:
                        dst = [dv[a][:, :, (u - 8) * 256:(u - 8) * 256 + 256] for a in range(2)]
                    src = ps(u % 8).rearrange("p (a b) -> p a b", a=2)
                    run(nc.vector.tensor_copy(dst[0], src))
                    nc.vector.tensor_tensor(dst[1], src, dst[0].bitcast(F32), ALU.subtract).then_inc(qkv_evac.sem, 1)

                for kb in range(KD):
                    dve.wait_ge(lru_tanh.sem, KD + kb + 1)
                    run(nc.vector.tensor_scalar(ratio[:, :], t8[:, kb, :], -1.0, 1.0, ALU.mult, ALU.add))
                    run(nc.vector.reciprocal(ratio[:, :], ratio[:, :]))
                    nc.vector.scalar_tensor_tensor(out=t8[:, kb, :], in0=t8[:, kb, :], scalar=-2.0, in1=ratio[:, :],
                                                   op0=ALU.mult, op1=ALU.mult).then_inc(lru_ratio.sem, 1)
                    run(nc.vector.tensor_tensor(i8[:, kb, :], i8[:, kb, :], h[:, kb, spare], ALU.mult))
                for kb in range(KD):
                    dve.wait_ge(lru_sqrt.sem, kb + 1)
                    run(nc.vector.tensor_tensor(i8[:, kb, :], i8[:, kb, :], t8[:, kb, :], ALU.mult))
                    run(nc.vector.tensor_tensor_scan(t8[:, kb, :], r8[:, kb, :], i8[:, kb, :], 0.0, ALU.mult, ALU.add))
                    run(nc.vector.scalar_tensor_tensor(out=g8[:, kb, :], in0=t8[:, kb, :], scalar=0.5, in1=g8[:, kb, :],
                                                       op0=ALU.mult, op1=ALU.mult))
                    evacuate(kb)
                for u in range(KD, 12):
                    evacuate(u)

            stage(t0, t1, tensor, vector, scalar)

        df = {n: sig(n) for n in ("df_scores", "df_max", "df_exp", "df_prob", "df_turned", "df_split", "df_pv", "df_sq",
                                  "df_ms", "df_std", "df_out", "ab_done")}

        def diff_attention():
            t0, t1 = FIRST["gates_ab"]
            s = {n: x.sem for n, x in df.items()}
            pt = [xm[:, a, 0:2, spare] for a in range(2)]

            def tensor(pe):
                def scores(i):
                    if i >= 2:
                        pe.wait_ge(s["df_max"], i - 1)
                    for q in range(2):
                        at = slice(q * P, q * P + P)
                        for c in range(2):
                            r = slice(c * 64, c * 64 + 64)
                            last = mm3(pe, ps(2 * (i % 2) + c)[:, q * 256:q * 256 + 256], dq[0][r, i, at], dq[1][r, i, at],
                                       dk[0][r, i, :], dk[1][r, i, :], True)
                    last.then_inc(s["df_scores"], 1)

                scores(0)
                for i in range(8):
                    if i < 7:
                        scores(i + 1)
                    pe.wait_ge(s["df_prob"], i + 1)
                    if i >= 1:
                        pe.wait_ge(s["df_split"], i)
                    for b in range(2):
                        for q in range(2):
                            last = pe.transpose(ps(4)[:, b * 256 + q * P:b * 256 + q * P + P],
                                                dsm(i)[:, q, 0, b * P:b * P + P], ident)
                    last.then_inc(s["df_turned"], 1)
                    n = t0 + i
                    if i >= 1:
                        pe.wait_ge(s["ab_done"], i)
                    c_unit(pe, n, n % RING, [ps(7)[:, b * 256:b * 256 + 256] for b in range(2)], lat)
                    if i >= 1:
                        pe.wait_ge(s["df_out"], i)
                    pe.wait_ge(s["df_split"], i + 1)
                    for b in range(2):
                        last = mm3(pe, ps(5)[:, 0:256], dv[0][:, b, i * P:i * P + P], dv[1][:, b, i * P:i * P + P],
                                   pt[0][:, b, :], pt[1][:, b, :], b == 0)
                    last.then_inc(s["df_pv"], 1)
                for c in range(4):
                    pe.wait_ge(s["df_sq"], c + 1)
                    pe.matmul(ps(c), ones_one[:, 0:P], tmp[:, c, :], start=True, stop=True).then_inc(s["df_ms"], 1)

            def dsm(i):
                return tmp[:, 2 * (i % 2):2 * (i % 2) + 2, :].rearrange("p c (q k) -> p q c k", q=2)

            def scalar(act):
                def exps(i):
                    act.wait_ge(s["df_max"], i + 1)
                    for q in range(2):
                        for c in range(2):
                            j = 2 * q + c
                            nc.scalar.activation(dsm(i)[:, q, c, :], dsm(i)[:, q, c, :], ACT.Exp,
                                                 bias=small[:, 8 + j:9 + j], scale=DIFF_SCALE,
                                                 accum_out=small[:, 12 + j:13 + j]).then_inc(s["df_exp"], 1)

                exps(0)
                for i in range(8):
                    if i < 7:
                        exps(i + 1)
                    n = t0 + i
                    split_next(act, n, n % RING, (n + ADA_TILES) // RING)
                    act.wait_ge(tile_used, n + 1)
                    dst = (r8 if i < 4 else i8)[:, 2 * (i % 4):2 * (i % 4) + 2, :]
                    nc.scalar.copy(dst, ps(7).rearrange("p (a b) -> p a b", a=2)).then_inc(s["ab_done"], 1)
                act.wait_ge(s["ab_done"], 8)
                for gates in (r8, i8):
                    nc.scalar.activation(gates, gates, ACT.Sigmoid)
                act.wait_ge(s["df_turned"], 8)
                for c in range(4):
                    act.wait_ge(s["df_out"], 2 * c + 2)
                    nc.scalar.activation(pairs(c), h[:, 2 * c:2 * c + 2, spare], ACT.Square).then_inc(s["df_sq"], 1)
                for c in range(4):
                    act.wait_ge(s["df_ms"], c + 1)
                    nc.scalar.activation(tmp[:, c, :], ps(c), ACT.Sqrt, bias=eps[:, 0:1], scale=1.0 / P).then_inc(s["df_std"], 1)

            def pairs(c):
                return tmp[:, c, :].rearrange("p (a b) -> p a b", a=2)

            def vector(dve):
                run = linked(dve, vlink)

                def front(i):
                    m = dsm(i)
                    dve.wait_ge(s["df_scores"], i + 1)
                    run(nc.vector.tensor_copy(tmp[:, 2 * (i % 2):2 * (i % 2) + 2, :], pair(i % 2)[:, :, :]))
                    for q in range(2):
                        for c in range(2):
                            own = m[:, q, c, q * P:q * P + P]
                            run(nc.vector.tensor_tensor(own, own, cst("tri_f", 128), ALU.add))
                    run(nc.vector.memset(m[:, 0, :, P:2 * P], MASKED))
                    run(nc.vector.tensor_reduce(small[:, 4:8].rearrange("p (q c) -> p q c", q=2), m, AX_X, ALU.max))
                    nc.vector.tensor_scalar(small[:, 8:12], small[:, 4:8], -DIFF_SCALE, None, ALU.mult)\
                        .then_inc(s["df_max"], 1)

                def output(i):
                    dve.wait_ge(s["df_pv"], i + 1)
                    nc.vector.tensor_copy(h[:, i, spare], ps(5)[:, 0:256]).then_inc(s["df_out"], 1)

                front(0)
                for i in range(8):
                    m = dsm(i)
                    dve.wait_ge(s["df_exp"], 4 * i + 4)
                    run(nc.vector.reciprocal(small[:, 16:20], small[:, 12:16]))
                    for q in range(2):
                        j = 16 + 2 * q
                        run(nc.vector.tensor_tensor(small[:, j + 1:j + 2], small[:, j + 1:j + 2], neg_lam, ALU.mult))
                        run(nc.vector.tensor_scalar(m[:, q, 1, :], m[:, q, 1, :], small[:, j + 1:j + 2], None, ALU.mult))
                        last = nc.vector.scalar_tensor_tensor(out=m[:, q, 0, :], in0=m[:, q, 0, :], scalar=small[:, j:j + 1],
                                                              in1=m[:, q, 1, :], op0=ALU.mult, op1=ALU.add)
                        if q == 0:
                            run(last)
                    last.then_inc(s["df_prob"], 1)
                    if i < 7:
                        front(i + 1)
                    dve.wait_ge(s["df_turned"], i + 1)
                    if i >= 1:
                        output(i - 1)
                    src = ps(4).rearrange("p (a b) -> p a b", a=2)
                    run(nc.vector.tensor_copy(pt[0], src))
                    nc.vector.tensor_tensor(pt[1], src, pt[0].bitcast(F32), ALU.subtract).then_inc(s["df_split"], 1)
                output(7)

            stage(t0, t1, tensor, vector, scalar)

        dx_out, mix_in = (sig(n) for n in ("dx_out", "mix_in"))

        def mix():
            t0 = FIRST["lru_br"][0]
            t1 = FIRST["w_out"][1]
            rs = Residual(t1, None, 0, SEQ)
            low = [ps(ko // 2)[:, ko % 2 * SEQ:ko % 2 * SEQ + SEQ] for ko in range(KD)]
            high = d_outs(SEQ)

            def tensor(pe):
                for d in range(4):
                    n = t0 + d
                    pe.wait_ge(dx_out.sem, 2 * d + 2)
                    d_unit(pe, n, n % RING, high, lambda kk, j=d: (xm[:, 0, 2 * j + kk, lat], xm[:, 1, 2 * j + kk, lat]), d == 0)
                for d in range(4):
                    n = t0 + 4 + d
                    pe.wait_ge(dx_out.sem, KD + 2 * d + 2)
                    d_unit(pe, n, n % RING, low, lambda kk, j=d: (xm[:, 0, 2 * j + kk, spare], xm[:, 1, 2 * j + kk, spare]), d == 0)
                for d in range(4):
                    n = t0 + 8 + d
                    pe.wait_ge(mix_in.sem, 2 * d + 2)
                    d_unit(pe, n, n % RING, high, lambda kk, j=d: (xm[:, 0, 2 * j + kk, lat], xm[:, 1, 2 * j + kk, lat]), d == 0,
                           d_block if d == 3 else None)

            def scalar(act):
                plain_splits(act, t0, t1)

            def vector(dve):
                run = linked(dve, vlink)
                for cols, src in ((lat, lambda k: g8[:, k, :]), (spare, lambda k: h[:, k, spare])):
                    for k in range(KD):
                        if cols == spare and k % 2 == 0:
                            root, y = tmp[:, k // 2, :], h[:, k:k + 2, spare]
                            run(nc.vector.reciprocal(root, root))
                            run(nc.vector.scalar_tensor_tensor(out=y, in0=y, scalar=sub_gain,
                                                               in1=root.rearrange("p (a b) -> p a b", a=2),
                                                               op0=ALU.mult, op1=ALU.mult))
                        run(nc.vector.tensor_copy(xm[:, 0, k, cols], src(k)))
                        nc.vector.tensor_tensor(xm[:, 1, k, cols], src(k), xm[:, 0, k, cols].bitcast(F32), ALU.subtract)\
                            .then_inc(dx_out.sem, 1)
                dve.wait_ge(tile_used, t0 + 4)
                for k in range(KD):
                    run(nc.vector.tensor_tensor(i8[:, k, :], i8[:, k, :], high[k], ALU.mult))
                dve.wait_ge(tile_used, t0 + 8)
                for k in range(KD):
                    run(nc.vector.tensor_tensor(r8[:, k, :], r8[:, k, :], low[k], ALU.mult))
                    run(nc.vector.tensor_tensor(r8[:, k, :], r8[:, k, :], i8[:, k, :], ALU.add))
                    run(nc.vector.tensor_copy(xm[:, 0, k, lat], r8[:, k, :]))
                    nc.vector.tensor_tensor(xm[:, 1, k, lat], r8[:, k, :], xm[:, 0, k, lat].bitcast(F32), ALU.subtract)\
                        .then_inc(mix_in.sem, 1)
                rs.dve(dve)

            stage(t0, t1, tensor, vector, scalar)

        route = work[:, 8, 0:128].rearrange("p (t c) -> p t c", t=2)
        comb = work[:, 8, 128:192].rearrange("p (t c) -> p t c", t=2)
        comb_t, comb_e = work[0:EXPERTS, 9, 0:256], work[0:EXPERTS, 9, 256:512]
        rt_max, rt_exp, rt_comb, rt_turned = sig("rt_max"), sig("rt_exp"), sig("rt_comb"), sig("rt_turned")

        rows_of = [flat_hid[a][:, 0:2 * D].rearrange("p (t d) -> p t d", t=2) for a in range(2)]
        gx = [flat_hid[a][:, 2 * D:2 * D + KD * 4 * P].rearrange("p (k s) -> p k s", k=KD) for a in range(2)]
        slot_rows = xm[:, 1, 4:8, spare]
        slot_cols = xm[:, 0, 4:8, spare]
        slot_weight = work[:, 8, 192:320]
        before = work[:, 11, 0:P]
        slot_base = work[:, 10, 0:4 * P:P]
        largest = idx8[0:1, 0, 0, 0:1]

        def chosen(t):
            return route[:, t, 48:52]

        def slot_of(t, g):
            return xm[:, 1, 4 + 2 * t + g // 2, SEQ + g % 2 * P:SEQ + g % 2 * P + P]

        tok_turned, tok_split, slot_mask, slot_count, slot_made, slot_turned, gather_step, gathered, slots_in = (
            sig(n) for n in ("tok_turned", "tok_split", "slot_mask", "slot_count", "slot_made", "slot_turned",
                             "gather_step", "gathered", "slots_in"))

        def router():
            t0, t1 = FIRST["router"]
            rms = RmsNorm("g_moe")

            def tensor(pe):
                rms.pe(pe)
                pe.wait_ge(xm_r.sem, rms.x + KD)
                t_unit(pe, t0, t0 % RING, [ps(2)[:, 0:256], ps(2)[:, 256:512]], 2, False)
                for t in range(2):
                    for k in range(KD):
                        last = pe.transpose(ps(4 + 2 * t + k // 4)[:, k % 4 * P:k % 4 * P + P], g8[:, k, t * P:t * P + P], ident)
                last.then_inc(tok_turned.sem, 1)
                pe.wait_ge(rt_comb.sem, 1)
                for t in range(2):
                    last = pe.transpose(ps(3)[0:EXPERTS, t * P:t * P + P], comb[:, t, :], ident)
                last.then_inc(rt_turned.sem, 1)
                pe.wait_ge(slot_mask.sem, 1)
                for t in range(2):
                    for u in range(t + 1):
                        pe.matmul(ps(1)[:, t * 4:t * 4 + 4], before[:, :] if u == t else ones_one[:, 0:P], chosen(u),
                                  start=(u == 0), stop=(u == t))
                for u in range(2):
                    last = pe.matmul(ps(1)[:, 8:12], ones_one[:, 0:P], chosen(u), start=(u == 0), stop=(u == 1))
                last.then_inc(slot_count.sem, 1)
                pe.wait_ge(slot_made.sem, 1)
                for g in range(GROUPS):
                    for t in range(2):
                        pe.matmul(ps(0)[:, 32 * g:32 * g + 32], slot_of(t, g).bitcast(F32), comb[:, t, :],
                                  start=(t == 0), stop=(t == 1))
                for g in range(GROUPS):
                    for t in range(2):
                        last = pe.transpose(ps(2 + g // 2)[:, g % 2 * 256 + t * P:g % 2 * 256 + t * P + P],
                                            slot_of(t, g).bitcast(F32), ident)
                last.then_inc(slot_turned.sem, 1)
                pe.wait_ge(tok_split.sem, 2)
                for k in range(KD):
                    if k >= 4:
                        pe.wait_ge(gathered.sem, k - 3)
                    for t in range(2):
                        for a in range(2):
                            last = pe.matmul(ps(4 + k % 4), rows_of[a][:, t, k * P:k * P + P],
                                             slot_rows[:, 2 * t:2 * t + 2, :], start=(t == 0 and a == 0),
                                             stop=(t == 1 and a == 1))
                    last.then_inc(gather_step.sem, 1)

            def scalar(act):
                act.dma_start(work[:, 10, :], const_d[:, CONST_AT["slots"]:CONST_AT["slots"] + 4 * P]).then_inc(slots_in.sem, 16)
                rms.act(act)
                split_next(act, t0, t0 % RING, (t0 + ADA_TILES) // RING)
                for t in range(2):
                    a = small[:, 20 * t:20 * t + 20]
                    act.wait_ge(rt_max.sem, 2 * t + 1)
                    nc.scalar.activation(a[:, 12:16], route[:, t, 0:4], ACT.Exp, bias=a[:, 8:9], accum_out=a[:, 9:10])\
                        .then_inc(rt_exp.sem, 1)
                    act.wait_ge(rt_max.sem, 2 * t + 2)
                    nc.scalar.activation(a[:, 10:11], a[:, 1:2], ACT.Exp, bias=a[:, 8:9]).then_inc(rt_exp.sem, 1)

            def vector(dve):
                run = linked(dve, vlink)
                rms.dve(dve, keep=True)
                dve.wait_ge(tile_used, t1)
                for t in range(2):
                    a, r, iota = small[:, 20 * t:20 * t + 20], route[:, t, :], cst("iota", 8)
                    idx_f = a[:, 16:18]
                    idx = r[:, 56:64].bitcast(U32)
                    run(nc.vector.tensor_tensor(r[:, 0:36], ps(2)[:, t * 256:t * 256 + 36], v("b_rt", 0, 36), ALU.add))
                    run(nc.vector.memset(r[:, 40:48], MASKED))
                    run(nc.vector.tensor_copy(r[:, 40:44], r[:, 0:4]))
                    run(nc.vector.max(a[:, 0:8], r[:, 40:48]))
                    run(nc.vector.max_index(idx, a[:, 0:8], r[:, 40:48]))
                    run(nc.vector.tensor_copy(idx_f[:, 0:1], idx[:, 0:1]))
                    run(nc.vector.tensor_scalar(r[:, 48:56], iota, idx_f[:, 0:1], None, ALU.is_equal))
                    nc.vector.tensor_scalar(a[:, 8:9], a[:, 0:1], -1.0, None, ALU.mult).then_inc(rt_max.sem, 1)
                    dve.wait_ge(rt_exp.sem, 2 * t + 1)
                    run(nc.vector.tensor_scalar(r[:, 40:48], r[:, 4:12], r[:, 48:49], None, ALU.mult))
                    for g in range(1, GROUPS):
                        run(nc.vector.scalar_tensor_tensor(out=r[:, 40:48], in0=r[:, 4 + 8 * g:12 + 8 * g],
                                                           scalar=r[:, 48 + g:49 + g], in1=r[:, 40:48],
                                                           op0=ALU.mult, op1=ALU.add))
                    run(nc.vector.max(a[:, 0:8], r[:, 40:48]))
                    run(nc.vector.max_index(idx, a[:, 0:8], r[:, 40:48]))
                    run(nc.vector.tensor_copy(idx_f, idx[:, 0:2]))
                    nc.vector.tensor_scalar(a[:, 8:9], a[:, 0:1], -1.0, None, ALU.mult).then_inc(rt_max.sem, 1)
                    dve.wait_ge(rt_exp.sem, 2 * t + 2)
                    run(nc.vector.tensor_scalar(a[:, 11:12], a[:, 10:11], 1.0, None, ALU.add))
                    run(nc.vector.tensor_tensor(a[:, 11:12], a[:, 11:12], a[:, 9:10], ALU.mult))
                    run(nc.vector.reciprocal(a[:, 12:13], a[:, 11:12]))
                    run(nc.vector.tensor_tensor(a[:, 13:14], a[:, 12:13], a[:, 10:11], ALU.mult))
                    run(nc.vector.tensor_scalar(r[:, 40:48], iota, idx_f[:, 0:1], a[:, 12:13], ALU.is_equal, ALU.mult))
                    run(nc.vector.tensor_scalar(r[:, 4:12], iota, idx_f[:, 1:2], a[:, 13:14], ALU.is_equal, ALU.mult))
                    run(nc.vector.tensor_tensor(r[:, 40:48], r[:, 40:48], r[:, 4:12], ALU.add))
                    for g in range(GROUPS):
                        last = nc.vector.tensor_scalar(comb[:, t, 8 * g:8 * g + 8], r[:, 40:48], r[:, 48 + g:49 + g], None,
                                                       ALU.mult)
                        if not (t == 1 and g == GROUPS - 1):
                            run(last)
                last.then_inc(rt_comb.sem, 1)
                dve.wait_ge(rt_turned.sem, 1)
                run(nc.vector.tensor_copy(comb_t, ps(3)[0:EXPERTS, 0:256]))
                nc.vector.tensor_scalar(before[:, :], cst("tri_f", 128), -1.0, None, ALU.is_lt).then_inc(slot_mask.sem, 1)
                dve.wait_ge(slot_count.sem, 1)
                dve.wait_ge(slots_in.sem, 16)
                for t in range(2):
                    a = small[:, 20 * t:20 * t + 20]
                    run(nc.vector.tensor_tensor(a[:, 0:4], ps(1)[:, t * 4:t * 4 + 4], slot_base, ALU.add))
                    run(nc.vector.tensor_tensor(a[:, 4:8], a[:, 0:4], chosen(t), ALU.mult))
                    run(nc.vector.tensor_reduce(a[:, 8:9], a[:, 4:8], AX_X, ALU.add))
                    run(nc.vector.tensor_scalar(slot_rows[:, 2 * t:2 * t + 2, :],
                                                work[:, 10, :].rearrange("p (a b) -> p a b", a=2), a[:, 8:9], None,
                                                ALU.is_equal))
                run(nc.vector.tensor_reduce(small[:, 62:63], ps(1)[:, 8:12], AX_X, ALU.max))
                run(nc.vector.tensor_copy(largest, small[0:1, 62:63]))
                nc.vector.tensor_copy(small[:, 63:64], small[:, 62:63]).then_inc(slot_made.sem, 1)
                dve.wait_ge(tok_turned.sem, 1)
                for t in range(2):
                    src = pair(2 + t)[:, :, :].rearrange("p a b -> p (a b)")
                    run(nc.vector.tensor_copy(rows_of[0][:, t, :], src))
                    nc.vector.tensor_tensor(rows_of[1][:, t, :], src, rows_of[0][:, t, :].bitcast(F32), ALU.subtract)\
                        .then_inc(tok_split.sem, 1)
                dve.wait_ge(slot_turned.sem, 1)
                run(nc.vector.tensor_copy(slot_weight, ps(0)[:, 0:128]))
                run(nc.vector.tensor_copy(slot_cols, pair(1)[:, :, :].rearrange("p a (g t) -> p (a g) t", g=2)))
                for k in range(KD):
                    dve.wait_ge(gather_step.sem, k + 1)
                    run(nc.vector.tensor_copy(gx[0][:, k, :], ps(4 + k % 4)))
                    nc.vector.tensor_tensor(gx[1][:, k, :], ps(4 + k % 4), gx[0][:, k, :].bitcast(F32), ALU.subtract)\
                        .then_inc(gathered.sem, 1)

            stage(t0, t1, tensor, vector, scalar)

        ex_weight, ex_spread, ex_gate, ex_f, ex_h, ex_r, acc_clear = (
            sig(n) for n in ("ex_weight", "ex_spread", "ex_gate", "ex_f", "ex_h", "ex_r", "acc_clear"))
        ex_scaled = sig("ex_scaled")

        sp_gate, sp_f, sp_t, sp_h, sp_r, y_split, scattered, sp_link = (
            sig(n) for n in ("sp_gate", "sp_f", "sp_t", "sp_h", "sp_r", "y_split", "scattered", "sp_link"))

        def experts():
            t0, t1 = FIRST["experts"]
            rs = Residual(t1, None, 0, SEQ)
            outs = d_outs(SEQ)
            eh = [flat_hid[a][:, 0:8 * SEQ].rearrange("p (b k t) -> p b k t", b=2, k=4) for a in range(2)]

            def up_tile(e, j):
                return t0 + j if isinstance(e, int) and e == 0 else e * 6 + (t0 - 2 + j)

            def down_tile(e, j):
                return e * 6 + (t0 + 8 + j) if not (isinstance(e, int) and e == EXPERTS - 1) else t1 - 2 + j

            def up_slot(first, j):
                return (t0 + j) % RING if first else (t0 - 2 + j) % RING

            def down_slot(last, j):
                return (t1 - 2 + j) % RING if last else (t0 + 8 + j) % RING

            def turn(n_expr_base, e):
                return e * 2 + (n_expr_base + ADA_TILES) // RING

            def over_experts(eng, up, down):
                up(0, 0)
                with eng.Fori(0, (EXPERTS - 2) // 2) as i:
                    for b in (1, 0):
                        e = i * 2 + (1 if b else 2)
                        up(e, b)
                        down(i * 2 + (0 if b else 1), 1 - b)
                up(EXPERTS - 1, 1)
                down(EXPERTS - 2, 0)
                down(EXPERTS - 1, 1)

            def half_after(dve, n, slot):
                if not (isinstance(n, int) and n + RING >= t1):
                    split_half(dve, n + RING, slot)

            def dense_pe(pe):
                def up(e, b):
                    first = isinstance(e, int) and e == 0
                    pe.wait_ge(ex_weight.sem, e + 1)
                    if not first:
                        pe.wait_ge(ex_r.sem, e * 4)
                    pe.matmul(ps(3)[:, lat], ones_one[0:EXPERTS, 0:P], comb_e, start=True, stop=True)\
                        .then_inc(ex_spread.sem, 1)
                    for j in range(4):
                        slot = up_slot(first, j)
                        if not (first and j < RING):
                            pe.wait_ge(ex_f.sem, e * 4 + (j - RING + 1))
                        c_unit(pe, up_tile(e, j), slot, [ps(bank_of(j, b))[:, c * 256:c * 256 + 256] for c in range(2)], lat,
                               shared=not (first and j < RING))

                def down(e, b):
                    last = isinstance(e, int) and e == EXPERTS - 1
                    pe.wait_ge(ex_r.sem, e * 4 + 4)
                    for j in range(2):
                        d_unit(pe, down_tile(e, j), down_slot(last, j), outs,
                               lambda kk: (eh[0][:, b, 2 * j + kk, :], eh[1][:, b, 2 * j + kk, :]), False,
                               d_block if last and j == 1 else None, shared=True)
                pe.wait_ge(acc_clear.sem, 1)
                over_experts(pe, up, down)

            def bank_of(j, b):
                return j % RING

            def dense_act(act):
                def up(e, b):
                    first = isinstance(e, int) and e == 0
                    for j in range(4):
                        n = up_tile(e, j)
                        base = t0 + j if first else t0 - 2 + j
                        split_next(act, n, base % RING, turn(base, e))
                        act.wait_ge(tile_used, n + 1)
                        if not (first and j < 2):
                            act.wait_ge(ex_scaled.sem, e * 4 + (j - 1))
                        nc.scalar.activation(work[:, j % 2, lat], ps(bank_of(j, b))[:, lat], ACT.Silu)\
                            .then_inc(ex_gate.sem, 1)

                def down(e, b):
                    last = isinstance(e, int) and e == EXPERTS - 1
                    for j in range(2):
                        n = down_tile(e, j)
                        if last:
                            split_next(act, n, n % RING, (n + ADA_TILES) // RING)
                        else:
                            base = t0 + 8 + j
                            split_next(act, n, base % RING, turn(base, e))
                over_experts(act, up, down)

            def dense_dve(dve):
                for b in range(4):
                    last = nc.vector.memset(ps(4 + b), 0.0)
                last.then_inc(acc_clear.sem, 1)

                def weigh(e):
                    nc.vector.tensor_scalar(comb_e, comb_t, ident[0:EXPERTS, e:e + 1] if isinstance(e, int)
                                            else const[0:EXPERTS, bass.ds(e, 1)], None, ALU.mult).then_inc(ex_weight.sem, 1)

                def up(e, b):
                    for j in range(4):
                        bk = ps(bank_of(j, b))
                        if j == 0:
                            dve.wait_ge(ex_spread.sem, e + 1)
                        dve.wait_ge(ex_gate.sem, e * 4 + (j + 1))
                        nc.vector.tensor_tensor(work[:, 2 + j % 2, lat], work[:, j % 2, lat], ps(3)[:, lat], ALU.mult)\
                            .then_inc(ex_scaled.sem, 1)
                        dve.wait_ge(ex_scaled.sem, e * 4 + (j + 1))
                        nc.vector.tensor_tensor(work[:, 4 + j % 2, lat], work[:, 2 + j % 2, lat], bk[:, 256:512], ALU.mult)\
                            .then_inc(ex_f.sem, 1)
                        dve.wait_ge(ex_f.sem, e * 4 + (j + 1))
                        nc.vector.tensor_copy(eh[0][:, b, j, :], work[:, 4 + j % 2, lat]).then_inc(ex_h.sem, 1)
                        dve.wait_ge(ex_h.sem, e * 4 + (j + 1))
                        nc.vector.tensor_tensor(eh[1][:, b, j, :], work[:, 4 + j % 2, lat], eh[0][:, b, j, :].bitcast(F32),
                                                ALU.subtract).then_inc(ex_r.sem, 1)
                        if j == 0 and not (isinstance(e, int) and e == EXPERTS - 1):
                            weigh(e + 1)
                        half_after(dve, up_tile(e, j), up_slot(isinstance(e, int) and e == 0, j))

                def down(e, b):
                    for j in range(2):
                        half_after(dve, down_tile(e, j), down_slot(isinstance(e, int) and e == EXPERTS - 1, j))
                weigh(0)
                over_experts(dve, up, down)
                rs.dve(dve)

            xh = [xm[:, a, 0:4, spare] for a in range(2)]

            def acc(g, half):
                return ps(4 + 2 * (g % 2) + half)

            def over_slots(eng, up_down, down_last):
                up_down(0, 0, 0)
                for g in range(GROUPS):
                    with eng.Fori(0, 3) as i:
                        for b in (1, 0):
                            up_down(i * 2 + (PER_GROUP * g + (1 if b else 2)), b, g)
                    up_down(PER_GROUP * g + 7, 1, g)
                    if g + 1 < GROUPS:
                        up_down(PER_GROUP * (g + 1), 0, g + 1)
                down_last(EXPERTS - 1)

            def starts_group(e):
                return isinstance(e, int) and e % PER_GROUP == 0

            def sparse_pe(pe):
                def up(e, b, g, j):
                    first = isinstance(e, int) and e == 0
                    n, slot = up_tile(e, j), up_slot(first, j)
                    tile_ready(pe, n, not (first and j < RING))
                    if not (first and j < 2):
                        pe.wait_ge(sp_f.sem, e * 4 + (j - 1))
                    for k in range(KD):
                        at, w = slice(g * P, g * P + P), slice(k * 256, k * 256 + 256)
                        last = mm3(pe, ps(j % 2)[:, 0:256], gx[0][:, k, at], gx[1][:, k, at],
                                   whi[:, slot, w], wlo[:, slot, w], k == 0)
                    last.then_inc(tile_used, 1)

                def turn_hidden(e, b, j):
                    pe.wait_ge(sp_f.sem, e * 4 + (j + 1))
                    if not (isinstance(e, int) and e == 0 and j == 0):
                        pe.wait_ge(sp_r.sem, e * 4 + j)
                    pe.transpose(ps(2)[:, 0:P], work[:, 11, (j % 2) * P:(j % 2) * P + P], ident).then_inc(sp_t.sem, 1)

                def down(e, b, g, j):
                    last_e = isinstance(e, int) and e == EXPERTS - 1
                    n, slot = down_tile(e, j), down_slot(last_e, j)
                    if j == 0:
                        pe.wait_ge(sp_r.sem, e * 4 + 4)
                        if g >= 2:
                            pe.wait_ge(acc_clear.sem, g)
                    tile_ready(pe, n, True)
                    for kk in range(2):
                        for half in range(2):
                            w = slice(kk * D + half * 512, kk * D + half * 512 + 512)
                            x = slice(b * P, b * P + P)
                            last = mm3(pe, acc(g, half), xh[0][:, 2 * j + kk, x], xh[1][:, 2 * j + kk, x],
                                       whi[:, slot, w], wlo[:, slot, w], False)
                    last.then_inc(tile_used, 1)

                def up_down(e, b, g):
                    gd = g - 1 if starts_group(e) else g
                    up(e, b, g, 0)
                    up(e, b, g, 1)
                    turn_hidden(e, b, 0)
                    up(e, b, g, 2)
                    turn_hidden(e, b, 1)
                    up(e, b, g, 3)
                    turn_hidden(e, b, 2)
                    if gd >= 0:
                        down(e - 1, 1 - b, gd, 0)
                    turn_hidden(e, b, 3)
                    if gd >= 0:
                        down(e - 1, 1 - b, gd, 1)

                def down_last(e):
                    down(e, 1, GROUPS - 1, 0)
                    down(e, 1, GROUPS - 1, 1)
                pe.wait_ge(acc_clear.sem, 1)
                over_slots(pe, up_down, down_last)
                for g in range(GROUPS):
                    pe.wait_ge(y_split.sem, g + 1)
                    for ko in range(KD):
                        out = ps(ko // 2)[:, ko % 2 * SEQ:ko % 2 * SEQ + SEQ]
                        for a in range(2):
                            last = pe.matmul(out, gx[a][:, 2 * g + ko // 4, ko % 4 * P:ko % 4 * P + P], slot_cols[:, g, :],
                                             start=(g == 0 and a == 0 and ko % 2 == 0), stop=(g == GROUPS - 1 and a == 1),
                                             skip_group_check=True)
                last.then_inc(scattered.sem, 1)

            def sparse_act(act):
                def after(n, base, e):
                    split_next(act, n, base % RING, turn(base, e) if not isinstance(e, int) else (n + ADA_TILES) // RING)

                def up_down(e, b, g):
                    first = isinstance(e, int) and e == 0
                    for j in range(4):
                        n = up_tile(e, j)
                        act.wait_ge(tile_used, n + 1)
                        if not (first and j < 2):
                            act.wait_ge(sp_f.sem, e * 4 + (j - 1))
                        nc.scalar.activation(work[:, 10, (j % 2) * P:(j % 2) * P + P], ps(j % 2)[:, 0:P], ACT.Silu)\
                            .then_inc(sp_gate.sem, 1)
                        after(n, t0 + j if first else t0 - 2 + j, e)
                    if not first:
                        for j in range(2):
                            after(down_tile(e - 1, j), t0 + 8 + j, e - 1)

                def down_last(e):
                    for j in range(2):
                        after(down_tile(e, j), t1 - 2 + j, e)
                over_slots(act, up_down, down_last)

            def sparse_dve(dve):
                run = linked(dve, sp_link)
                for b in range(4):
                    last = nc.vector.memset(ps(4 + b), 0.0)
                last.then_inc(acc_clear.sem, 1)

                def weighted(e, g, j):
                    dve.wait_ge(sp_gate.sem, e * 4 + (j + 1))
                    if not (isinstance(e, int) and e == 0 and j < 2):
                        dve.wait_ge(sp_t.sem, e * 4 + (j - 1))
                    c = weight_col(e, g)
                    nc.vector.scalar_tensor_tensor(out=work[:, 11, (j % 2) * P:(j % 2) * P + P],
                                                   in0=work[:, 10, (j % 2) * P:(j % 2) * P + P], scalar=c,
                                                   in1=ps(j % 2)[:, P:2 * P], op0=ALU.mult, op1=ALU.mult).then_inc(sp_f.sem, 1)

                def weight_col(e, g):
                    at = e + 32 * g
                    return slot_weight[:, at:at + 1] if isinstance(e, int) else slot_weight[:, bass.ds(at, 1)]

                def evacuate(e, b, j):
                    dve.wait_ge(sp_t.sem, e * 4 + (j + 1))
                    x = slice(b * P, b * P + P)
                    nc.vector.tensor_copy(xh[0][:, j, x], ps(2)[:, 0:P]).then_inc(sp_h.sem, 1)
                    dve.wait_ge(sp_h.sem, e * 4 + (j + 1))
                    nc.vector.tensor_tensor(xh[1][:, j, x], ps(2)[:, 0:P], xh[0][:, j, x].bitcast(F32), ALU.subtract)\
                        .then_inc(sp_r.sem, 1)

                def up_down(e, b, g):
                    first = isinstance(e, int) and e == 0
                    for j in range(4):
                        weighted(e, g, j)
                        if j >= 1:
                            evacuate(e, b, j - 1)
                        half_after(dve, up_tile(e, j), up_slot(first, j))
                    if first:
                        evacuate(e, b, 3)
                        return
                    half_after(dve, down_tile(e - 1, 0), down_slot(False, 0))
                    evacuate(e, b, 3)
                    half_after(dve, down_tile(e - 1, 1), down_slot(False, 1))
                    if starts_group(e):
                        finish_group(g - 1, down_tile(e - 1, 1) + 1)

                def finish_group(g, used):
                    dve.wait_ge(tile_used, used)
                    for half in range(2):
                        run(nc.vector.tensor_copy(work[:, 2 * g + half, :], acc(g, half)))
                        if g < 2:
                            last = nc.vector.memset(acc(g, half), 0.0)
                            if half == 0:
                                run(last)
                    if g < 2:
                        last.then_inc(acc_clear.sem, 1)

                def down_last(e):
                    finish_group(GROUPS - 1, t1)
                over_slots(dve, up_down, down_last)
                for g in range(GROUPS):
                    y = work[:, 2 * g:2 * g + 2, :]
                    run(nc.vector.tensor_copy(gx[0][:, 2 * g:2 * g + 2, :], y))
                    nc.vector.tensor_tensor(gx[1][:, 2 * g:2 * g + 2, :], y, gx[0][:, 2 * g:2 * g + 2, :].bitcast(F32),
                                            ALU.subtract).then_inc(y_split.sem, 1)
                dve.wait_ge(scattered.sem, 1)
                for ko in range(KD):
                    run(nc.vector.tensor_tensor(h[:, ko, lat], h[:, ko, lat],
                                                ps(ko // 2)[:, ko % 2 * SEQ:ko % 2 * SEQ + SEQ], ALU.add))

            def either(eng, sparse, dense):
                size = eng.value_load(largest, min_val=0, max_val=SEQ)
                with eng.If(size < FEW + 1):
                    sparse(eng)
                with eng.Else():
                    dense(eng)
                eng.nop()

            stage(t0, t1, lambda pe: either(pe, sparse_pe, dense_pe), lambda dve: either(dve, sparse_dve, dense_dve),
                  lambda act: either(act, sparse_act, dense_act))

        p_in, p_split, ple_gate = sig("p_in"), sig("p_split"), sig("ple_gate")
        out_ready, out_sent = sig("out_ready"), sig("out_sent")

        def ple():
            t0, t1 = FIRST["ple"]
            rms = RmsNorm("g_ple")
            b_res = res.take(KD)
            outs = d_outs(SEQ)
            p_raw = work[:, 10, :].rearrange("p (k t) -> p k t", k=2)

            def tensor(pe):
                pe.wait_ge(p_split.sem, 1)
                d_unit(pe, t0, t0 % RING, outs, lambda kk: (xm[:, 0, kk, spare], xm[:, 1, kk, spare]), True)
                rms.pe(pe)
                for u in range(4):
                    n = t0 + 1 + u
                    c_unit(pe, n, n % RING, [ps(u)[:, b * 256:b * 256 + 256] for b in range(2)], lat,
                           rms.ready(pe) if u == 0 else None)

            def scalar(act):
                act.dma_start(p_raw, p_d).then_inc(p_in.sem, 16)
                split_next(act, t0, t0 % RING, (t0 + ADA_TILES) // RING)
                rms.act(act)
                for u in range(4):
                    n = t0 + 1 + u
                    split_next(act, n, n % RING, (n + ADA_TILES) // RING)
                    act.wait_ge(tile_used, n + 1)
                    nc.scalar.activation(g8[:, 2 * u:2 * u + 2, :],
                                         ps(u).rearrange("p (a b) -> p a b", a=2), ACT.Sigmoid).then_inc(ple_gate.sem, 1)

            def vector(dve):
                run = linked(dve, vlink)
                dve.wait_ge(p_in.sem, 16)
                run(nc.vector.tensor_copy(xm[:, 0, 0:2, spare], p_raw))
                nc.vector.tensor_tensor(xm[:, 1, 0:2, spare], p_raw, xm[:, 0, 0:2, spare].bitcast(F32), ALU.subtract)\
                    .then_inc(p_split.sem, 1)
                rms.dve(dve)
                for k in range(KD):
                    if k % 2 == 0:
                        dve.wait_ge(ple_gate.sem, k // 2 + 1)
                    run(nc.vector.tensor_tensor(g8[:, k, :], g8[:, k, :], outs[k], ALU.mult))
                    nc.vector.tensor_tensor(h[:, k, lat], h[:, k, lat], g8[:, k, :], ALU.add).then_inc(res.sem, 1)

            stage(t0, t1, tensor, vector, scalar)

        def last_norm():
            rms = RmsNorm("g_final")

            def scalar(act):
                rms.act(act)
                act.wait_ge(out_ready.sem, 1)
                act.dma_start(out_d, work[:, 0:KD, lat]).then_inc(out_sent.sem, 16)
                act.wait_ge(out_sent.sem, 16)

            def vector(dve):
                rms.dve(dve, split=False)
                nc.vector.tensor_copy(small[:, 0:1], small[:, 1:2]).then_inc(out_ready.sem, 1)

            stage(TILES, TILES, rms.pe, vector, scalar)

        ffn("ffn00", 0, 0, TOK)
        attention_in()
        attention_core()
        project("att_out", 0, 5, TOK, 1, lambda k: work[:, 4 + k, :], (0, 3), tmp[0:96, 1, 0:384])
        ffn("ffn01", 0, 1, TOK)
        ffn("ffn10", 1, 0, TOK)
        mlstm_in()
        mlstm_core()
        project("ml_out", 1, 5, SEQ, 4, lambda k: o_gate[:, k, :], (3, 4), work[0:96, 1, 0:P])
        ffn("ffn11", 1, 1, SEQ)
        lru_in()
        qkv()
        diff_attention()
        mix()
        router()
        experts()
        ple()
        last_norm()


def column_tile(w, cols):
    return w[:, cols].reshape(KD, P, 256).transpose(1, 0, 2).reshape(P, TILE)


def row_tile(w, r):
    return w[r * 256:r * 256 + 256].reshape(2, P, D).transpose(1, 0, 2).reshape(P, TILE)


def pack_stream(a):
    out = np.zeros((ADA_TILES + TILES, P, TILE), np.float32)
    n = 0

    def add(tile):
        nonlocal n
        out[n] = tile
        n += 1

    def columns(w, first=0, count=None):
        for c in range(first, first + (count or w.shape[1] // 256)):
            add(column_tile(w, slice(c * 256, c * 256 + 256)))

    def rows(w):
        for r in range(w.shape[0] // 256):
            add(row_tile(w, r))

    def gate_up(w_gate, w_up, j):
        at = slice(j * P, j * P + P)
        add(column_tile(np.concatenate([w_gate[:, at], w_up[:, at]], axis=1), slice(0, 256)))

    def ffn(w_in, w_out):
        for first, count in ((0, HALF_A), (HALF_A, HALF_B)):
            for j in range(first, first + count):
                gate_up(w_in[:, :FF], w_in[:, FF:], j)
            for r in range(first // 2, (first + count) // 2):
                add(row_tile(w_out, r))

    columns(a["ada_w"][0], 0, ADA_TILES)
    ffn(a["ffn_w_in"][0, 0], a["ffn_w_out"][0, 0])
    for u in range(6):
        columns(a["att_w_in"][0], u, 1)
        columns(a["ada_w"][0], ADA_TILES + 2 * u, 2)
    columns(a["ada_w"][1], 0, 2 * ADA_GROUP)
    rows(a["att_w_out"][0])
    ffn(a["ffn_w_in"][0, 1], a["ffn_w_out"][0, 1])
    ffn(a["ffn_w_in"][1, 0], a["ffn_w_out"][1, 0])
    w = a["ml_w_in"][0]
    gates = np.zeros((D, 256), np.float32)
    gates[:, 0:4], gates[:, 32:36] = w[:, 3072:3076], w[:, 3080:3084]
    gates[:, 128:132], gates[:, 160:164] = w[:, 3076:3080], w[:, 3084:3088]
    columns(gates)
    columns(w, 2, 2)
    columns(w, 0, 2)
    columns(w, 4, 4)
    columns(w, 8, 4)
    columns(a["ada_w"][1], 2 * ADA_GROUP, ADA_GROUP)
    rows(a["ml_w_out"][0])
    ffn(a["ffn_w_in"][1, 1], a["ffn_w_out"][1, 1])
    w = a["w_in_2"][0]
    columns(w, 12, 4)
    columns(w, 16, 4)
    block = np.zeros((P, KD, 2, P), np.float32)
    for g, name in enumerate(("w_rg_2", "w_ig_2")):
        for b in range(16):
            at = slice(b % 2 * 64, b % 2 * 64 + 64)
            block[at, b // 2, g, at] = a[name][0, b]
    add(block.reshape(P, TILE))
    columns(w, 0, 4)
    columns(w, 4, 4)
    columns(w, 8, 4)
    columns(w, 20, 8)
    rows(a["w_lru_br_2"][0])
    rows(a["w_attn_br_2"][0])
    rows(a["w_out_2"][0])
    router = np.zeros((D, 256), np.float32)
    router[:, 0:GROUPS] = a["w_rt_group_2"][0]
    router[:, GROUPS:GROUPS + EXPERTS] = a["w_rt_expert_2"][0].transpose(1, 0, 2).reshape(D, EXPERTS)
    columns(router)
    wg, wu, wd = a["w_e_gate_2"][0], a["w_e_up_2"][0], a["w_e_down_2"][0]
    for e in range(EXPERTS + 1):
        if e < EXPERTS:
            for j in range(4):
                gate_up(wg[e], wu[e], j)
        if e >= 1:
            rows(wd[e - 1])
    rows(a["w_ple_proj_2"][0])
    columns(a["w_ple_gate_2"][0])
    assert n == ADA_TILES + TILES
    return out


def pack_vectors(a):
    def blocks(x):
        return np.asarray(x).reshape(-1, P).T

    def gates(x):
        out = np.zeros((P, 2), np.float32)
        out[0:4, 0], out[32:36, 0] = x[0:4], x[8:12]
        out[0:4, 1], out[32:36, 1] = x[4:8], x[12:16]
        return out

    lam = np.zeros((P, 4), np.float32)
    for i, name in enumerate(("lam_q1_2", "lam_k1_2", "lam_q2_2", "lam_k2_2")):
        lam[0:64, i] = a[name][0]
    parts = {
        "c": np.stack([a["c"][0], a["c_ctx"]], 1).reshape(KD, P, 2).transpose(1, 0, 2).reshape(P, 16),
        "ada_b": blocks(a["ada_b"]), "ln_g": blocks(a["ln_g"]), "ln_b": blocks(a["ln_b"]),
        "q_gain": blocks(a["att_q_gain"]), "k_gain": blocks(a["att_k_gain"]),
        "ml_conv_w": blocks(a["ml_conv_w"]), "ml_conv_b": blocks(a["ml_conv_b"]), "ml_norm_g": blocks(a["ml_norm_g"]),
        "gate_b": gates(a["ml_gate_b"][0]),
        "g_mix": blocks(a["g_mix_2"]), "g_moe": blocks(a["g_moe_2"]), "g_ple": blocks(a["g_ple_2"]),
        "g_final": blocks(a["g_final_2"]), "g_subln": blocks(a["g_subln_2"]),
        "w_conv": blocks(a["w_conv_2"]), "b_conv": blocks(a["b_conv_2"]), "b_rg": blocks(a["b_rg_2"]),
        "b_ig": blocks(a["b_ig_2"]), "lru_lambda": blocks(a["lru_lambda_2"]), "lam": lam,
        "b_rt": np.tile(np.concatenate([a["b_rt_group_2"].reshape(-1), a["b_rt_expert_2"].reshape(-1)]), (P, 1)),
    }
    return np.ascontiguousarray(np.concatenate([parts[name] for name, _ in VECTORS], axis=1))


def pack_constants():
    i = np.arange(P)
    inv = (np.float32(10000.0) ** (-np.arange(32, dtype=np.float32) / np.float32(32))).astype(np.float32)
    t = np.arange(SEQ)
    ang = np.where((i < 64)[:, None], (t // 64)[None, :], (t % 64)[None, :]).astype(np.float32) * inv[i % 32][:, None]
    sign = np.where(i % 64 < 32, -1.0, 1.0)[:, None]
    select = np.zeros((P, 8, P), np.float32)
    for hd in range(4):
        select[hd, hd], select[32 + hd, 4 + hd] = 1.0, 1.0
    parts = {
        "ident": np.eye(P), "tri_f": np.where(i[None, :] <= i[:, None], 0.0, MASKED),
        "tri_b": np.where(i[None, :] >= i[:, None], 0.0, MASKED), "iota": np.tile(np.arange(8.0), (P, 1)),
        "cos": np.cos(ang), "sin": sign * np.sin(ang), "swap": np.eye(P)[i ^ 32], "select": select.reshape(P, -1),
        "slots": np.tile(np.arange(4.0 * P), (P, 1)),
    }
    return np.ascontiguousarray(np.concatenate([parts[name] for name, _ in CONSTS], axis=1).astype(np.float32))


def kernel(**inputs):
    import concourse.bacc as bacc
    from concourse.bass_utils import run_bass_kernel_spmd

    a = {name: np.asarray(x) for name, x in inputs.items()}
    arrays = {
        "stream": pack_stream(a),
        "vectors": pack_vectors(a),
        "constants": pack_constants(),
        "x_t": np.ascontiguousarray(np.concatenate([a["x"][0], a["ctx"][0]]).T.reshape(KD, P, TOK).transpose(1, 0, 2)),
        "p_t": np.ascontiguousarray(a["p_2"][0, 0].T.reshape(2, P, SEQ).transpose(1, 0, 2)),
    }
    nc = bacc.Bacc("TRN2", target_bir_lowering=False, num_devices=1)
    args = [nc.dram_tensor(name, x.shape, F32, kind="ExternalInput").ap() for name, x in arrays.items()]
    ada_rows = nc.dram_tensor("ada_rows", (2, ADA_TILES * 256), F32, kind="Internal").ap()
    late_rows = nc.dram_tensor("late_rows", (LATE_GROUPS, 4, ADA_GROUP * 256), F32, kind="Internal").ap()
    out = nc.dram_tensor("out", (P, KD, SEQ), F32, kind="ExternalOutput").ap()
    program(nc, *args, ada_rows, late_rows, out)
    r = run_bass_kernel_spmd(nc, [arrays], core_ids=[0])
    y = r.results[0]["out"]
    return np.ascontiguousarray(y.transpose(1, 0, 2).reshape(D, SEQ).T).reshape(1, SEQ, D)
```
